# Optimizing a Trainium2 kernel written in Bass

```python
import math
import numpy as np
import jax, jax.numpy as jnp
from jax import lax

D_MODEL = 1024
BATCH = 1
SEQ = 512
DEPTH = 1

N_HEADS = 8
HEAD_DIM = 64
N_KV_GROUPS = 2
HEADS_PER_GROUP = N_HEADS // N_KV_GROUPS
ATTN_WIDTH = N_HEADS * HEAD_DIM
KV_WIDTH = N_KV_GROUPS * HEAD_DIM
CMP_BLOCK = 32
CMP_STRIDE = 16
CMP_HIDDEN = 128
SEL_BLOCK = 64
SEL_TOP = 16
WINDOW = 512
Q_CHUNK = 64
FORCE_BONUS = 1.0e4
NEG_INF = -1.0e30
CONV_CH = 512
CONV_WIDTH = 31
FFN_DIM = 2816
FFN_CONV_WIDTH = 3
NORM_EPS = 1e-6

IN_SIZES = (ATTN_WIDTH, KV_WIDTH, KV_WIDTH, KV_WIDTH, KV_WIDTH, KV_WIDTH, KV_WIDTH,
            3 * N_HEADS, 2 * CONV_CH, 2 * D_MODEL)
N_IN = sum(IN_SIZES)


def rms_norm(x, g):
    xf = x.astype(jnp.float32)
    y = xf * lax.rsqrt(jnp.mean(xf * xf, axis=-1, keepdims=True) + NORM_EPS)
    return (y * g.astype(jnp.float32)).astype(x.dtype)

def layer_norm(x, g, b):
    xf = x.astype(jnp.float32)
    mu = jnp.mean(xf, axis=-1, keepdims=True)
    var = jnp.mean(jnp.square(xf - mu), axis=-1, keepdims=True)
    y = (xf - mu) * lax.rsqrt(var + NORM_EPS)
    return (y * g.astype(jnp.float32) + b.astype(jnp.float32)).astype(x.dtype)

def causal_dwconv(x, w):
    k, c = w.shape
    return lax.conv_general_dilated(x, w[:, None, :], window_strides=(1,), padding=[(k - 1, 0)],
                                    dimension_numbers=('NWC', 'WIO', 'NWC'), feature_group_count=c)

def alibi_slopes():
    return jnp.power(2.0, -8.0 * jnp.arange(1, N_HEADS + 1, dtype=jnp.float32) / N_HEADS)

def compress(kv, pe, w1, w2):
    b, s, g, dh = kv.shape
    ncmp = (s - CMP_BLOCK) // CMP_STRIDE + 1
    idx = np.arange(ncmp)[:, None] * CMP_STRIDE + np.arange(CMP_BLOCK)[None, :]
    blk = kv[:, idx] + pe[None, None, :, None, :]
    blk = jnp.transpose(blk, (0, 1, 3, 2, 4)).reshape(b, ncmp, g, CMP_BLOCK * dh)
    return jax.nn.gelu(blk @ w1) @ w2

def cmp_to_sel_map(s):
    ncmp = (s - CMP_BLOCK) // CMP_STRIDE + 1
    nsel = s // SEL_BLOCK
    cs = np.arange(ncmp) * CMP_STRIDE
    ce = cs + CMP_BLOCK - 1
    ss = np.arange(nsel) * SEL_BLOCK
    se = ss + SEL_BLOCK - 1
    ov = np.minimum(ce[:, None], se[None, :]) - np.maximum(cs[:, None], ss[None, :]) + 1
    return jnp.asarray(np.clip(ov, 0, None).astype(np.float32) / CMP_BLOCK)

def nsa_attention(q, k_cmp, v_cmp, k_sel, v_sel, k_win, v_win, gate_logits, pe_k, pe_v, ck1, ck2, cv1, cv2):
    b, s, _ = q.shape
    G, J, Dh = N_KV_GROUPS, HEADS_PER_GROUP, HEAD_DIM
    f32 = jnp.float32
    q = q.reshape(b, s, G, J, Dh)
    kv = lambda t: t.reshape(b, s, G, Dh)
    k_cmp, v_cmp, k_sel, v_sel, k_win, v_win = map(kv, (k_cmp, v_cmp, k_sel, v_sel, k_win, v_win))
    slopes = alibi_slopes().reshape(G, J)
    pos = jnp.arange(s)
    scale = HEAD_DIM ** -0.5

    kc = compress(k_cmp, pe_k, ck1, ck2)
    vc = compress(v_cmp, pe_v, cv1, cv2)
    ncmp = kc.shape[1]
    c_end = jnp.arange(ncmp) * CMP_STRIDE + CMP_BLOCK - 1
    dist_c = pos[:, None] - c_end[None, :]
    valid_c = dist_c >= 0
    s_c = jnp.einsum('btgjd,bngd->bgjtn', q, kc).astype(f32) * scale - slopes[:, :, None, None] * dist_c
    s_c = jnp.where(valid_c, s_c, NEG_INF)
    p_c = jax.nn.softmax(s_c, axis=-1) * valid_c
    o_c = jnp.einsum('bgjtn,bngd->btgjd', p_c.astype(vc.dtype), vc)

    nsel = s // SEL_BLOCK
    n_top = min(SEL_TOP, nsel)
    imp = jnp.einsum('bgjtn,nk->bgtk', p_c, cmp_to_sel_map(s))
    blk_id = jnp.arange(nsel)[None, :]
    cur = (pos // SEL_BLOCK)[:, None]
    forced = (blk_id == 0) | (blk_id == cur) | (blk_id == cur - 1)
    imp = jnp.where(blk_id <= cur, imp + FORCE_BONUS * forced, NEG_INF)
    _, sel_idx = lax.top_k(imp, n_top)

    ks_blocks = k_sel.reshape(b, nsel, SEL_BLOCK, G, Dh).transpose(0, 3, 1, 2, 4)
    vs_blocks = v_sel.reshape(b, nsel, SEL_BLOCK, G, Dh).transpose(0, 3, 1, 2, 4)
    gather = jax.vmap(jax.vmap(lambda blocks, ids: blocks[ids]))
    kw_pad = jnp.pad(k_win, ((0, 0), (WINDOW, 0), (0, 0), (0, 0)))
    vw_pad = jnp.pad(v_win, ((0, 0), (WINDOW, 0), (0, 0), (0, 0)))
    m_sel = n_top * SEL_BLOCK

    def chunk(c):
        t0 = c * Q_CHUNK
        qc = lax.dynamic_slice_in_dim(q, t0, Q_CHUNK, axis=1)
        tq = t0 + jnp.arange(Q_CHUNK)
        ids = lax.dynamic_slice_in_dim(sel_idx, t0, Q_CHUNK, axis=2)
        ksg = gather(ks_blocks, ids).reshape(b, G, Q_CHUNK, m_sel, Dh)
        vsg = gather(vs_blocks, ids).reshape(b, G, Q_CHUNK, m_sel, Dh)
        kpos = (ids[..., None] * SEL_BLOCK + jnp.arange(SEL_BLOCK)).reshape(b, G, Q_CHUNK, m_sel)
        dist_s = (tq[None, None, :, None] - kpos)[:, :, None]
        s_s = jnp.einsum('btgjd,bgtmd->bgjtm', qc, ksg).astype(f32) * scale \
            - slopes[None, :, :, None, None] * dist_s
        p_s = jax.nn.softmax(jnp.where(dist_s >= 0, s_s, NEG_INF), axis=-1)
        o_s = jnp.einsum('bgjtm,bgtmd->btgjd', p_s.astype(vsg.dtype), vsg)
        kw = lax.dynamic_slice_in_dim(kw_pad, t0, Q_CHUNK + WINDOW, axis=1)
        vw = lax.dynamic_slice_in_dim(vw_pad, t0, Q_CHUNK + WINDOW, axis=1)
        kpos_w = t0 - WINDOW + jnp.arange(Q_CHUNK + WINDOW)
        dist_w = tq[:, None] - kpos_w[None, :]
        valid_w = (dist_w >= 0) & (dist_w < WINDOW) & (kpos_w[None, :] >= 0)
        s_w = jnp.einsum('btgjd,bsgd->bgjts', qc, kw).astype(f32) * scale - slopes[:, :, None, None] * dist_w
        p_w = jax.nn.softmax(jnp.where(valid_w, s_w, NEG_INF), axis=-1)
        o_w = jnp.einsum('bgjts,bsgd->btgjd', p_w.astype(vw.dtype), vw)
        return o_s, o_w

    o_s, o_w = lax.map(chunk, jnp.arange(s // Q_CHUNK))
    o_s = jnp.moveaxis(o_s, 0, 1).reshape(b, s, G, J, Dh)
    o_w = jnp.moveaxis(o_w, 0, 1).reshape(b, s, G, J, Dh)

    g = jax.nn.sigmoid(gate_logits).reshape(b, s, G, J, 3)
    o = g[..., 0:1] * o_c + g[..., 1:2] * o_s + g[..., 2:3] * o_w
    return o.reshape(b, s, ATTN_WIDTH)

def conformer_conv(u, dw_w, dw_b, ln_g, ln_b, w_proj):
    a, gate = jnp.split(u, 2, axis=-1)
    z = a * jax.nn.sigmoid(gate)
    z = causal_dwconv(z, dw_w) + dw_b
    z = jax.nn.silu(layer_norm(z, ln_g, ln_b))
    return z @ w_proj

def conv_ffn(h, w_up, dw_w, dw_b, w_down):
    u = causal_dwconv(h @ w_up, dw_w) + dw_b
    a, v = jnp.split(u, 2, axis=-1)
    return (jax.nn.silu(a) * v) @ w_down

def first_inputs(seed: int = 0) -> dict:
    key = jax.random.key(seed)
    keys = jax.random.split(key, 32)
    counter = [0]
    f32 = jnp.float32

    def nxt():
        k = keys[counter[0]]
        counter[0] += 1
        return k

    def dense(shape, fan_in):
        return jax.random.normal(nxt(), shape, f32) * fan_in ** -0.5

    def gain(shape):
        return 1.0 + 0.05 * jax.random.normal(nxt(), shape, f32)

    def small(shape, scale=0.02):
        return scale * jax.random.normal(nxt(), shape, f32)

    L = DEPTH
    return {
        "x": jax.random.normal(nxt(), (BATCH, SEQ, D_MODEL), f32),
        "norm1_g": gain((L, D_MODEL)),
        "w_in": dense((L, D_MODEL, N_IN), D_MODEL),
        "cmp_pe_k": small((L, CMP_BLOCK, HEAD_DIM), 0.1),
        "cmp_pe_v": small((L, CMP_BLOCK, HEAD_DIM), 0.1),
        "cmp_k_w1": dense((L, CMP_BLOCK * HEAD_DIM, CMP_HIDDEN), CMP_BLOCK * HEAD_DIM),
        "cmp_k_w2": dense((L, CMP_HIDDEN, HEAD_DIM), CMP_HIDDEN),
        "cmp_v_w1": dense((L, CMP_BLOCK * HEAD_DIM, CMP_HIDDEN), CMP_BLOCK * HEAD_DIM),
        "cmp_v_w2": dense((L, CMP_HIDDEN, HEAD_DIM), CMP_HIDDEN),
        "w_attn_br": dense((L, ATTN_WIDTH, D_MODEL), ATTN_WIDTH),
        "conv_dw_w": dense((L, CONV_WIDTH, CONV_CH), CONV_WIDTH),
        "conv_dw_b": small((L, CONV_CH)),
        "conv_ln_g": gain((L, CONV_CH)),
        "conv_ln_b": small((L, CONV_CH)),
        "w_conv_br": dense((L, CONV_CH, D_MODEL), CONV_CH),
        "w_out": dense((L, D_MODEL, D_MODEL), D_MODEL),
        "norm2_g": gain((L, D_MODEL)),
        "ffn_w_up": dense((L, D_MODEL, 2 * FFN_DIM), D_MODEL),
        "ffn_dw_w": dense((L, FFN_CONV_WIDTH, 2 * FFN_DIM), FFN_CONV_WIDTH),
        "ffn_dw_b": small((L, 2 * FFN_DIM)),
        "ffn_w_down": dense((L, FFN_DIM, D_MODEL), FFN_DIM),
        "final_g": gain((D_MODEL,)),
    }

def first_block(x, norm1_g, w_in, cmp_pe_k, cmp_pe_v, cmp_k_w1, cmp_k_w2, cmp_v_w1, cmp_v_w2,
              w_attn_br, conv_dw_w, conv_dw_b, conv_ln_g, conv_ln_b, w_conv_br, w_out,
              norm2_g, ffn_w_up, ffn_dw_w, ffn_dw_b, ffn_w_down, final_g):
    split_points = list(np.cumsum(IN_SIZES)[:-1])
    for l in range(DEPTH):
        h = rms_norm(x, norm1_g[l])
        proj = h @ w_in[l]
        (q, k_c, v_c, k_s, v_s, k_w, v_w, g_nsa, u_conv, g_merge) = jnp.split(proj, split_points, axis=-1)
        y_attn = nsa_attention(q, k_c, v_c, k_s, v_s, k_w, v_w, g_nsa, cmp_pe_k[l], cmp_pe_v[l],
                               cmp_k_w1[l], cmp_k_w2[l], cmp_v_w1[l], cmp_v_w2[l]) @ w_attn_br[l]
        y_conv = conformer_conv(u_conv, conv_dw_w[l], conv_dw_b[l], conv_ln_g[l], conv_ln_b[l], w_conv_br[l])
        g_a, g_b = jnp.split(jax.nn.sigmoid(g_merge), 2, axis=-1)
        x = x + (g_a * y_attn + g_b * y_conv) @ w_out[l]
        x = x + conv_ffn(rms_norm(x, norm2_g[l]), ffn_w_up[l], ffn_dw_w[l], ffn_dw_b[l], ffn_w_down[l])
    return rms_norm(x, final_g)


DEPTH_2 = 2

GRID_W = 64
Q_BLOCK = 128
EPS = 1e-6
ROPE_THETA = 10000.0

A_HEADS = 8
A_KV_HEADS = 2
A_GROUPS = A_HEADS // A_KV_HEADS
A_Q = A_HEADS * HEAD_DIM
A_KV = A_KV_HEADS * HEAD_DIM
A_OUT = A_Q

B_HEADS = 8
B_NOPE = 64
B_ROPE = 32
B_V = 64
B_Q_LORA = 256
B_KV_LORA = 128
B_OUT = B_HEADS * B_V

C_HEADS = 16
C_KV_HEADS = 4
C_GROUPS = C_HEADS // C_KV_HEADS
C_Q = C_HEADS * HEAD_DIM
C_KV = C_KV_HEADS * HEAD_DIM
WINDOW_2 = 128

EVEN_IN = A_Q + 2 * A_KV + A_OUT + B_Q_LORA + B_KV_LORA + B_ROPE + B_OUT
EVEN_MIX = A_OUT + B_OUT
ODD_IN = C_Q + 2 * C_KV + C_Q
ODD_MIX = C_Q
N_EVEN = (DEPTH_2 + 1) // 2
N_ODD = DEPTH_2 // 2


def rms_norm_2(x, g):
    xf = x.astype(jnp.float32)
    y = xf * lax.rsqrt(jnp.mean(xf * xf, axis=-1, keepdims=True) + EPS)
    return (y * g.astype(jnp.float32)).astype(x.dtype)

def rope_cos_sin(pos, dim):
    inv = ROPE_THETA ** (-jnp.arange(0, dim, 2, dtype=jnp.float32) / dim)
    ang = pos.astype(jnp.float32)[:, None] * inv[None, :]
    return jnp.cos(ang), jnp.sin(ang)

def apply_rope(x, cos, sin):
    half = x.shape[-1] // 2
    x1, x2 = x[..., :half], x[..., half:]
    cos = cos.astype(x.dtype)
    sin = sin.astype(x.dtype)
    return jnp.concatenate([x1 * cos - x2 * sin, x1 * sin + x2 * cos], axis=-1)

def axial_rope(x, cos_r, sin_r, cos_c, sin_c):
    half = HEAD_DIM // 2
    xr = apply_rope(x[..., :half], cos_r[:, None, :], sin_r[:, None, :])
    xc = apply_rope(x[..., half:], cos_c[:, None, :], sin_c[:, None, :])
    return jnp.concatenate([xr, xc], axis=-1)

def to_blocks(t):
    b, s = t.shape[:2]
    return jnp.moveaxis(t.reshape((b, s // Q_BLOCK, Q_BLOCK) + t.shape[2:]), 1, 0)

def from_blocks(t):
    nb, b = t.shape[:2]
    return jnp.moveaxis(t, 0, 1).reshape((b, nb * Q_BLOCK) + t.shape[3:])

def dense_gqa_attention(q, k, v):
    b, s = q.shape[:2]
    scale = HEAD_DIM ** -0.5

    def block(qi):
        sc = jnp.einsum('bqkgd,bskd->bkgqs', qi, k).astype(jnp.float32) * scale
        p = jax.nn.softmax(sc, axis=-1).astype(v.dtype)
        return jnp.einsum('bkgqs,bskd->bqkgd', p, v)

    o = from_blocks(lax.map(block, to_blocks(q)))
    return o.reshape(b, s, A_HEADS * HEAD_DIM)

def mla_attention(q_lat, q_rope, c_kv, k_rope, w_uv):
    b, s = q_lat.shape[:2]
    scale = (B_NOPE + B_ROPE) ** -0.5

    def block(args):
        ql, qr = args
        sc = (jnp.einsum('bqhc,bsc->bhqs', ql, c_kv)
              + jnp.einsum('bqhr,bsr->bhqs', qr, k_rope)).astype(jnp.float32) * scale
        p = jax.nn.softmax(sc, axis=-1).astype(c_kv.dtype)
        return jnp.einsum('bhqs,bsc->bqhc', p, c_kv)

    o_lat = from_blocks(lax.map(block, (to_blocks(q_lat), to_blocks(q_rope))))
    o = jnp.einsum('bshc,chd->bshd', o_lat, w_uv)
    return o.reshape(b, s, B_HEADS * B_V)

def windowed_sink_attention(q, k, v, sink, slopes):
    b, s = q.shape[:2]
    nb = s // Q_BLOCK
    scale = HEAD_DIM ** -0.5
    qb = q.reshape(b, nb, Q_BLOCK, C_KV_HEADS, C_GROUPS, HEAD_DIM)

    def neighbours(t):
        tb = t.reshape(b, nb, Q_BLOCK, C_KV_HEADS, HEAD_DIM)
        tp = jnp.pad(tb, ((0, 0), (1, 1), (0, 0), (0, 0), (0, 0)))
        return jnp.concatenate([tp[:, :-2], tp[:, 1:-1], tp[:, 2:]], axis=2)

    kb, vb = neighbours(k), neighbours(v)
    rel = jnp.arange(3 * Q_BLOCK)[None, :] - Q_BLOCK - jnp.arange(Q_BLOCK)[:, None]
    key_pos = (jnp.arange(nb)[:, None] - 1) * Q_BLOCK + jnp.arange(3 * Q_BLOCK)[None, :]
    valid = (jnp.abs(rel) <= WINDOW_2)[None] & ((key_pos >= 0) & (key_pos < s))[:, None, :]
    bias = -slopes.reshape(C_KV_HEADS, C_GROUPS)[:, :, None, None] * jnp.abs(rel).astype(jnp.float32)
    sc = jnp.einsum('bnqkgd,bnskd->bnkgqs', qb, kb).astype(jnp.float32) * scale + bias
    sc = jnp.where(valid[None, :, None, None], sc, -jnp.inf)
    sink_l = sink.astype(jnp.float32).reshape(C_KV_HEADS, C_GROUPS)[None, None, :, :, None, None]
    m = jnp.maximum(jnp.max(sc, axis=-1, keepdims=True), sink_l)
    p = jnp.exp(sc - m)
    denom = jnp.sum(p, axis=-1, keepdims=True) + jnp.exp(sink_l - m)
    o = jnp.einsum('bnkgqs,bnskd->bnqkgd', (p / denom).astype(v.dtype), vb)
    return o.reshape(b, s, C_HEADS * HEAD_DIM)

def even_mixer(h, w_in, q_norm_a, k_norm_a, q_lora_norm, kv_lora_norm, w_uq, w_uk, w_uv, w_out,
               cos_r, sin_r, cos_c, sin_c, cos_t, sin_t):
    b, s, _ = h.shape
    proj = h @ w_in
    splits = list(np.cumsum([A_Q, A_KV, A_KV, A_OUT, B_Q_LORA, B_KV_LORA, B_ROPE]))
    qa, ka, va, ga, cq, ckv, kr, gb = jnp.split(proj, splits, axis=-1)
    qa = axial_rope(rms_norm_2(qa.reshape(b, s, A_HEADS, HEAD_DIM), q_norm_a), cos_r, sin_r, cos_c, sin_c)
    ka = axial_rope(rms_norm_2(ka.reshape(b, s, A_KV_HEADS, HEAD_DIM), k_norm_a), cos_r, sin_r, cos_c, sin_c)
    oa = dense_gqa_attention(qa.reshape(b, s, A_KV_HEADS, A_GROUPS, HEAD_DIM), ka,
                             va.reshape(b, s, A_KV_HEADS, HEAD_DIM))
    oa = oa * jax.nn.silu(ga)
    cq = rms_norm_2(cq, q_lora_norm)
    ckv = rms_norm_2(ckv, kv_lora_norm)
    qb = (cq @ w_uq).reshape(b, s, B_HEADS, B_NOPE + B_ROPE)
    q_nope, q_rope = qb[..., :B_NOPE], qb[..., B_NOPE:]
    q_rope = apply_rope(q_rope, cos_t[:, None, :], sin_t[:, None, :])
    k_rope = apply_rope(kr, cos_t, sin_t)
    q_lat = jnp.einsum('bshd,chd->bshc', q_nope, w_uk)
    ob = mla_attention(q_lat, q_rope, ckv, k_rope, w_uv) * jax.nn.silu(gb)
    return jnp.concatenate([oa, ob], axis=-1) @ w_out

def odd_mixer(h, w_in, sink, w_out, slopes):
    b, s, _ = h.shape
    proj = h @ w_in
    qc, kc, vc, gc = jnp.split(proj, [C_Q, C_Q + C_KV, C_Q + 2 * C_KV], axis=-1)
    oc = windowed_sink_attention(qc.reshape(b, s, C_KV_HEADS, C_GROUPS, HEAD_DIM),
                                 kc.reshape(b, s, C_KV_HEADS, HEAD_DIM),
                                 vc.reshape(b, s, C_KV_HEADS, HEAD_DIM), sink, slopes)
    return (oc * jax.nn.silu(gc)) @ w_out

def second_inputs(seed: int = 0) -> dict:
    key = jax.random.key(seed)
    ks = jax.random.split(key, 20)
    f32 = jnp.float32
    nrm = lambda k, shape, s: jax.random.normal(k, shape, f32) * s
    gain = lambda k, shape: 1.0 + 0.02 * jax.random.normal(k, shape, f32)
    return {
        "x": nrm(ks[0], (BATCH, SEQ, D_MODEL), 1.0),
        "c": nrm(ks[1], (BATCH, D_MODEL), 1.0),
        "norm_w": gain(ks[2], (DEPTH_2, D_MODEL)),
        "ada_w": nrm(ks[3], (DEPTH_2, D_MODEL, 3 * D_MODEL), 0.02),
        "ada_b": nrm(ks[4], (DEPTH_2, 3 * D_MODEL), 0.02),
        "even_w_in": nrm(ks[5], (N_EVEN, D_MODEL, EVEN_IN), D_MODEL ** -0.5),
        "a_q_norm": gain(ks[6], (N_EVEN, HEAD_DIM)),
        "a_k_norm": gain(ks[7], (N_EVEN, HEAD_DIM)),
        "b_q_lora_norm": gain(ks[8], (N_EVEN, B_Q_LORA)),
        "b_kv_lora_norm": gain(ks[9], (N_EVEN, B_KV_LORA)),
        "b_w_uq": nrm(ks[10], (N_EVEN, B_Q_LORA, B_HEADS * (B_NOPE + B_ROPE)), B_Q_LORA ** -0.5),
        "b_w_uk": nrm(ks[11], (N_EVEN, B_KV_LORA, B_HEADS, B_NOPE), B_KV_LORA ** -0.5),
        "b_w_uv": nrm(ks[12], (N_EVEN, B_KV_LORA, B_HEADS, B_V), B_KV_LORA ** -0.5),
        "even_w_out": nrm(ks[13], (N_EVEN, EVEN_MIX, D_MODEL), EVEN_MIX ** -0.5),
        "odd_w_in": nrm(ks[14], (N_ODD, D_MODEL, ODD_IN), D_MODEL ** -0.5),
        "c_sink": nrm(ks[15], (N_ODD, C_HEADS), 0.5),
        "odd_w_out": nrm(ks[16], (N_ODD, ODD_MIX, D_MODEL), ODD_MIX ** -0.5),
        "final_norm": gain(ks[17], (D_MODEL,)),
    }

def second_block(x, c, norm_w, ada_w, ada_b, even_w_in, a_q_norm, a_k_norm, b_q_lora_norm,
              b_kv_lora_norm, b_w_uq, b_w_uk, b_w_uv, even_w_out, odd_w_in, c_sink, odd_w_out,
              final_norm):
    s = x.shape[1]
    rows = s // GRID_W
    row = jnp.repeat(jnp.arange(rows), GRID_W)
    col = jnp.tile(jnp.arange(GRID_W), rows)
    tok = jnp.arange(s)
    cos_r, sin_r = rope_cos_sin(row, HEAD_DIM // 2)
    cos_c, sin_c = rope_cos_sin(col, HEAD_DIM // 2)
    cos_t, sin_t = rope_cos_sin(tok, B_ROPE)
    slopes = 2.0 ** (-8.0 * jnp.arange(1, C_HEADS + 1, dtype=jnp.float32) / C_HEADS)
    c_act = jax.nn.silu(c)
    for layer in range(DEPTH_2):
        mod = c_act @ ada_w[layer] + ada_b[layer]
        shift, scale, gate = jnp.split(mod, 3, axis=-1)
        h = rms_norm_2(x, norm_w[layer]) * (1.0 + scale[:, None, :]) + shift[:, None, :]
        if layer % 2 == 0:
            i = layer // 2
            y = even_mixer(h, even_w_in[i], a_q_norm[i], a_k_norm[i], b_q_lora_norm[i],
                           b_kv_lora_norm[i], b_w_uq[i], b_w_uk[i], b_w_uv[i], even_w_out[i],
                           cos_r, sin_r, cos_c, sin_c, cos_t, sin_t)
        else:
            i = layer // 2
            y = odd_mixer(h, odd_w_in[i], c_sink[i], odd_w_out[i], slopes)
        x = x + gate[:, None, :] * y
    return rms_norm_2(x, final_norm)


def setup_inputs(seed=0):
    out = dict(first_inputs(seed))
    for name, value in second_inputs(seed + 1).items():
        if name != "x":
            out[name + "_2"] = value
    return out


def reference(
    x, norm1_g, w_in, cmp_pe_k, cmp_pe_v, cmp_k_w1, cmp_k_w2, cmp_v_w1, cmp_v_w2, w_attn_br,
    conv_dw_w, conv_dw_b, conv_ln_g, conv_ln_b, w_conv_br, w_out, norm2_g, ffn_w_up, ffn_dw_w,
    ffn_dw_b, ffn_w_down, final_g, c_2, norm_w_2, ada_w_2, ada_b_2, even_w_in_2, a_q_norm_2,
    a_k_norm_2, b_q_lora_norm_2, b_kv_lora_norm_2, b_w_uq_2, b_w_uk_2, b_w_uv_2, even_w_out_2,
    odd_w_in_2, c_sink_2, odd_w_out_2, final_norm_2,
):
    x = first_block(
        x, norm1_g, w_in, cmp_pe_k, cmp_pe_v, cmp_k_w1, cmp_k_w2, cmp_v_w1, cmp_v_w2, w_attn_br,
        conv_dw_w, conv_dw_b, conv_ln_g, conv_ln_b, w_conv_br, w_out, norm2_g, ffn_w_up,
        ffn_dw_w, ffn_dw_b, ffn_w_down, final_g,
    )
    return second_block(
        x, c_2, norm_w_2, ada_w_2, ada_b_2, even_w_in_2, a_q_norm_2, a_k_norm_2,
        b_q_lora_norm_2, b_kv_lora_norm_2, b_w_uq_2, b_w_uk_2, b_w_uv_2, even_w_out_2,
        odd_w_in_2, c_sink_2, odd_w_out_2, final_norm_2,
    )


_drawn_inputs = setup_inputs


def setup_inputs(seed=0):
    import zlib

    import numpy as np

    out = dict(_drawn_inputs(seed))
    spreads = {}
    factors = {'cmp_pe_k': 8.0,
     'cmp_pe_v': 2.926,
     'conv_dw_b': 3.756,
     'conv_ln_g': 2.813,
     'conv_ln_b': 7.92,
     'ffn_dw_b': 4.115,
     'norm_w_2': 8.0,
     'ada_b_2': 4.52,
     'a_q_norm_2': 8.0,
     'a_k_norm_2': 8.0,
     'b_q_lora_norm_2': 8.0,
     'b_kv_lora_norm_2': 8.0,
     'b_w_uq_2': 3.18,
     'b_w_uk_2': 3.374,
     'c_sink_2': 8.0,
     'final_norm_2': 2.842}
    for name, (base, spread) in spreads.items():
        noise = np.random.default_rng([zlib.crc32(name.encode()), seed]).standard_normal(out[name].shape)
        drawn = base * np.exp(spread * noise) if base else spread * noise
        out[name] = __import__('jax').numpy.asarray(drawn.astype(out[name].dtype))
    for name, factor in factors.items():
        out[name] = (out[name] * factor).astype(out[name].dtype)
    return out
```

```python
from contextlib import ExitStack

import numpy as np

import concourse.bass as bass
from concourse import mybir

F32 = mybir.dt.float32
F32R = mybir.dt.float32r
I32 = mybir.dt.int32
ACT = mybir.ActivationFunctionType
ALU = mybir.AluOpType
AX_X = mybir.AxisListType.X

P = 128
T = 512
TT = T // P
D = 1024
DC = D // P
EPS = 1e-6
NEG = -1.0e30
HEADS = 8
HD = 64
CMP_BLOCK, CMP_STRIDE = 32, 16
NCMP = (T - CMP_BLOCK) // CMP_STRIDE + 1
NCP = 32
TAPS = 31
CONV_CH = 512
CC = CONV_CH // P
FFN = 2816
FC = FFN // P
WIN = 128
C_HEADS = 16
ROPE_THETA = 10000.0

UNITS = (
    [("conv", i) for i in range(2 * CC)]
    + [("tok", i) for i in range(3)]
    + [("q", i) for i in range(4)]
    + [("k", i) for i in range(4)]
    + [("ga", i) for i in range(DC)]
    + [u for i in range(DC) for u in (("gb", i), ("y", i))]
    + [("wout", i) for i in range(DC)]
    + [("up", i) for i in range(2 * FC)]
    + [("down", i) for i in range(FC)]
    + [("ecq", 0), ("ecq", 1), ("eckv", 0), ("ekr", 0)]
    + [("eq", i) for i in range(4)] + [("ek", 0), ("ev", 0)]
    + [("ega", i) for i in range(4)] + [("egb", i) for i in range(4)]
    + [("eout", i) for i in range(DC)]
    + [("oq", i) for i in range(DC)] + [("ok", i) for i in range(2)] + [("ov", i) for i in range(2)]
    + [("og", i) for i in range(DC)]
    + [("oout", i) for i in range(DC)]
)
UNIT = {u: n for n, u in enumerate(UNITS)}
NU = len(UNITS)
RAW = 2
WS = 4

COLS = {}
_n = 0
for _name, _w in (
    ("n1g", DC), ("n2g", DC), ("fg", DC), ("dwb", CC), ("lng", CC), ("lnb", CC),
    ("dww", CC * TAPS), ("ffw", 2 * FC * 3), ("ffb", 2 * FC), ("pek", CMP_BLOCK), ("pev", CMP_BLOCK),
    ("rowvalid", 1), ("nw", 2 * DC), ("adab", 2 * 3 * DC), ("c", DC), ("qn", 1), ("kn", 1),
    ("cqg", 2), ("ckvg", 1), ("fn", DC), ("sink", C_HEADS),
):
    COLS[_name] = (_n, _w)
    _n += _w
NCOLS = _n


def order_up(i):
    return i // 2 + (i % 2) * FC


class Signal:

    def __init__(self, sem, name, known, found):
        self.sem, self.name, self.known, self.found, self.n = sem, name, known, found, 0

    def up(self, key, by=1):
        self.n += by
        self.found[(self.name, key)] = self.n
        return self.sem, by

    def at(self, key):
        return self.sem, self.known.get((self.name, key), 1)


class Banks:

    def __init__(self, tiles, signals, known, found):
        self.tiles, self.signals, self.known, self.found = tiles, signals, known, found
        self.last, self.turn = {}, {}

    def take(self, pe, pool, key):
        n = self.turn.get(pool, 0)
        self.turn[pool] = n + 1
        b = pool[n % len(pool)]
        if b in self.last:
            name, step = self.known.get(("freed", self.last[b]), ("sq_ready", "x"))
            pe.wait_ge(*self.signals[name].at(step))
        self.last[b] = key
        self.found[("bank", key)] = b
        return self.tiles[b]

    def of(self, key):
        return self.tiles[self.known.get(("bank", key), 0)]

    def freed(self, key, signal, step):
        self.found[("freed", key)] = (signal.name, step)


LIN, SC, TR, OB = (0, 1), (2, 3), (4, 5), (6, 7)


def program(nc, d, out, known):
    found = {}
    ctx = ExitStack()
    with ctx:
        def sb(name, cols, dt=F32):
            return ctx.enter_context(nc.sbuf_tensor(name, [P] + list(cols), dt))

        signals = {}

        def signal(name):
            signals[name] = Signal(ctx.enter_context(nc.semaphore(name)), name, known, found)
            return signals[name]

        bank = Banks([ctx.enter_context(nc.psum_tensor(f"bank{b}", [P, 512], F32)) for b in range(8)],
                     signals, known, found)

        with nc.sbuf_tensor("h_first", [P, 16 * T], F32) as h_use:
            pass
        hhi, hlo = sb("hhi", [DC, T], F32R), sb("hlo", [DC, T], F32R)
        ZW = TAPS - 1 + T
        with nc.sbuf_tensor("first", [P, 16 * T], F32) as first_use:
            pass
        ysplit = sb("ysplit", [16, T], F32R)
        z = first_use[:, 8 * T:8 * T + CC * ZW].rearrange("p (c t) -> p c t", c=CC)
        ctap = first_use[:, 8 * T + CC * ZW:8 * T + CC * ZW + CC * TAPS].rearrange("p (c n) -> p c n", c=CC)

        def yhi(k):
            return ysplit[:, k // 4 * 8 + k % 4, :]

        def ylo(k):
            return ysplit[:, k // 4 * 8 + 4 + k % 4, :]

        whi, wlo = sb("whi", [WS, D], F32R), sb("wlo", [WS, D], F32R)
        raw = sb("raw", [RAW, D])
        ident, ones = sb("ident", [P]), sb("ones", [2])
        cols = sb("cols", [NCOLS])
        stat = sb("stat", [24, 16])
        nmax, rsum, rinv = sb("nmax", [192]), sb("rsum", [192]), sb("rinv", [192])
        XB, AB = DC * T, 17920
        xbuf = sb("xbuf", [XB])
        arena = sb("arena", [AB])
        xT = xbuf[:].rearrange("p (c t) -> p c t", c=DC)

        place = [0]

        def area(n, at=None):
            if at is not None:
                place[0] = at
            a = place[0]
            place[0] += n
            assert place[0] <= AB, place[0]
            return arena[:, a:a + n]

        def col(name, i=0, n=1):
            return cols[:, COLS[name][0] + i:COLS[name][0] + i + n]

        def chunks(ap, c):
            return ap.rearrange("p (c t) -> p c t", c=c)

        qT = chunks(area(4 * T, 0), 4)
        kv = chunks(area(4 * T), 4)
        vtok = area(TT * 256).rearrange("p (t n) -> p t n", t=TT)
        gate3 = area(TT * 24).rearrange("p (t n) -> p t n", t=TT)
        cacc = chunks(area(CC * T), CC)
        dist = area(T)
        distc = area(TT * NCP)
        biasc = area(TT * HEADS * NCP).rearrange("p (t h n) -> p t h n", t=TT, h=HEADS)
        kcmp = area(2 * NCP)[:, 0:NCP]
        vblk = area(2 * 256).rearrange("p (g n) -> p g n", g=2)
        w2k, w2v = area(HD), area(HD)
        w1_at = place[0]
        bias = chunks(area(HEADS * T), HEADS)
        ptile = chunks(area(2 * T), 2)
        pttile = chunks(area(2 * T), 2)
        otile = area(T)
        tmp = chunks(area(2 * T), 2)
        hs = sb("hs", [2, T])
        w1v = xbuf[:].rearrange("p (j m) -> p j m", j=CMP_BLOCK)
        w1k = arena[:, w1_at:w1_at + CMP_BLOCK * P].rearrange("p (j m) -> p j m", j=CMP_BLOCK)
        blk_at = w1_at + CMP_BLOCK * P
        blk = arena[:, blk_at:blk_at + 2 * CMP_BLOCK * NCMP].rearrange(
            "p (v j n) -> p v j n", v=2, j=CMP_BLOCK)
        assert blk_at + 2 * CMP_BLOCK * NCMP <= w1_at + HEADS * T + 5 * T
        gel = hs[:, 0:1, :]
        hidk = tmp[:, 0, 0:64].rearrange("p (g n) -> p g n", g=2)
        hidv = tmp[:, 0, 128:384].rearrange("p (g r n) -> p g r n", g=2, r=4)
        merged = xT
        fa = chunks(area(FC * T, 0), FC)
        ua = chunks(area(4 * T), 4)
        ft = chunks(area(2 * T), 2)
        ada = area(2 * D).rearrange("p (s n) -> p s n", s=2)
        sqt = sb("sqt", [2, T])
        modc = sb("modc", [2, 3 * DC])

        statf = stat[:].rearrange("p a b -> p (a b)")
        EY, EV, ET = 256, 296, 336
        def st40(at):
            return statf[:, at:at + 40]
        eq = chunks(area(4 * T, 0), 4)
        btok = eq
        ek = area(T)
        ev = area(TT * P).rearrange("p (t n) -> p t n", t=TT)
        ecq = chunks(area(2 * T), 2)
        eckv, ekr = area(T), area(T)
        esg = chunks(area(8 * T), 8)
        cosT, sinT = area(T), area(T)
        eotile = area(T)
        etmp = chunks(area(3 * T), 3)
        p2 = chunks(area(2 * T), 2)
        pt2 = chunks(area(2 * T), 2)
        late = first_use[:, 8 * T:16 * T]
        cosA, sinA = late[:, 0:T], late[:, T:2 * T]
        uq = late[:, 2 * T:2 * T + 1536].rearrange("p (k h m) -> p k h m", k=2, h=8)
        uk, uv = late[:, 2 * T + 1536:3 * T + 1536], late[:, 3 * T + 1536:4 * T + 1536]
        vB = chunks(h_use[:, 0:4 * T], 4)
        QF = chunks(h_use[:, 4 * T:6 * T], 2)
        KF = chunks(h_use[:, 6 * T:8 * T], 2)
        oq = chunks(area(8 * T, 0), 8)
        ok = chunks(area(2 * T), 2)
        ov = area(TT * 256).rearrange("p (t n) -> p t n", t=TT)
        osg = chunks(area(8 * T), 8)
        ootile = area(T)
        otmp = chunks(area(2 * T), 2)
        p3 = chunks(area(2 * T), 2)
        pt3 = chunks(area(2 * T), 2)
        distC = area(3 * P)
        nsink = area(C_HEADS)
        esink = area(C_HEADS * TT)
        obias = h_use[:, 0:C_HEADS * 3 * P].rearrange("p (h n) -> p h n", h=C_HEADS)
        sel2 = sb("sel2", [2])
        cact, gn = sb("cact", [DC]), sb("gn", [2, DC])

        loaded = signal("loaded")
        landed = [signal(f"landed{r}") for r in range(RAW)]
        w_hi = signal("w_hi")
        w_split = signal("w_split")
        unit_done = signal("unit_done")
        pe_did = signal("pe_did")
        s_done = signal("s_done")
        pt_done = signal("pt_done")
        pv_done = signal("pv_done")
        sq_ready = signal("sq_ready")
        act_did = signal("act_did")
        p_ready = signal("p_ready")
        ptc = signal("ptc")
        dve_did = signal("dve_did")
        sm_ready = signal("sm_ready")
        pool_did = signal("pool_did")
        stored = signal("stored")
        xload = signal("xload")
        x2load = [signal(f"x2load{c}") for c in range(DC)]
        c1load = signal("c1load")
        w1load = signal("w1load")
        w1v_load = signal("w1v_load")
        block = ctx.enter_context(nc.Block())

        adaload = [signal(f"adaload{i}") for i in range(2)]
        tabload = signal("tabload")

        def tiles_of(phase):
            groups, per = {"A": (TT, HEADS), "B": (HEADS, TT), "C": (2 * TT, HEADS)}[phase]
            return [(phase, g, u) for g in range(groups) for u in range(per)]

        def geometry(tile):
            phase, g, u = tile
            if phase == "A":
                half = 64 * (u // 4)
                return eq[half:half + 64, u % 4, g * P:(g + 1) * P], ek[half:half + 64, :], 0, TT, g * 8 + u
            if phase == "B":
                return QF[0:96, g % 2, u * P:(u + 1) * P], KF[0:96, g % 2, :], 0, TT, 32 + g * 4 + u
            qt, h = g // 2, g % 2 * 8 + u
            half = 64 * (h // 4 % 2)
            k0, k1 = max(qt - 1, 0), min(qt + 1, TT - 1)
            return (oq[half:half + 64, h // 8 * 4 + h % 4, qt * P:(qt + 1) * P],
                    ok[half:half + 64, h // 8, k0 * P:(k1 + 1) * P], k0, k1 - k0 + 1, 64 + g * 8 + u)

        def values(tile, k):
            phase, g, u = tile
            if phase == "A":
                return ev[:, k, u // 4 * HD:(u // 4 + 1) * HD]
            if phase == "B":
                return vB[:, k, g * HD:(g + 1) * HD]
            h = g % 2 * 8 + u
            return ov[:, k, h // 4 * HD:(h // 4 + 1) * HD]

        def p_of(phase):
            return (p3, pt3) if phase == "C" else (p2, pt2)

        nsa = []
        for qt in range(TT):
            nsa.append(("cmp", qt, 0))
            for br in range(2):
                nsa += [("nsa", qt, br * HEADS + h) for h in range(HEADS)]

        @block.tensor
        def _(pe):
            mm = nc.tensor.matmul

            def h_parts(k):
                return hhi[:, k, :], hlo[:, k, :]

            def y_parts(k):
                return yhi(k), ylo(k)

            def unit(name, i, src=h_parts, first=None, inline=True):
                u = UNIT[(name, i)]
                s = u % WS
                state = {}

                def piece(k):
                    if k == 0:
                        pe.wait_ge(w_split.sem, u + 1)
                        state["b"] = bank.take(pe, LIN, (name, i))
                    if first:
                        pe.wait_ge(*first(k))
                    b = state["b"]
                    hi, lo = src(k)
                    for part, (w, x) in enumerate(((whi, hi), (whi, lo), (wlo, hi))):
                        m = mm(b[:, :], w[:, s, k * P:(k + 1) * P], x,
                               start=(k == 0 and part == 0), stop=(k == DC - 1 and part == 2))
                    if k == DC - 1:
                        m.then_inc(*unit_done.up(u))
                if inline:
                    for k in range(DC):
                        piece(k)
                return piece

            def tok_unit(name, i, n=P):
                u = UNIT[(name, i)]
                s = u % WS
                pe.wait_ge(w_split.sem, u + 1)
                b = bank.take(pe, LIN, (name, i))
                for tt in range(TT):
                    for k in range(DC):
                        for part, (w, x) in enumerate(((whi, hhi), (whi, hlo), (wlo, hhi))):
                            m = mm(b[:, tt * P:tt * P + n], x[:, k, tt * P:(tt + 1) * P],
                                   w[:, s, k * P:k * P + n],
                                   start=(k == 0 and part == 0), stop=(k == DC - 1 and part == 2))
                m.then_inc(*unit_done.up(u))

            def stats(name, n, src=None, ready=None):
                b = bank.take(pe, TR, (name, "sum"))
                for c in range(n):
                    pe.wait_ge(*(ready(c) if ready else sq_ready.at((name, c))))
                    x = src[:, c, :] if src is not None else sqt[:, known.get(("sqslot", (name, c)), 0), :]
                    for tt in range(TT):
                        m = mm(b[:, tt:tt + 1], x[:, tt * P:(tt + 1) * P], ones[:, 0:1],
                               start=(c == 0 and tt == 0), stop=(c == n - 1), skip_group_check=True)
                    m.then_inc(*pe_did.up((name, "sum", c)))

            def spread(name, c0):
                pe.wait_ge(*dve_did.at((name, "stat")))
                b = bank.take(pe, TR, (name, "spread"))
                for tt in range(TT):
                    m = mm(b[:, tt * P:(tt + 1) * P], stat[:, c0, tt:tt + 1].to_broadcast([P, P]),
                           ident[:, :], start=True, stop=True)
                m.then_inc(*pe_did.up((name, "spread")))

            def norm(name, c0=0):
                stats(name, DC)
                spread(name, c0)

            def att_scores(a):
                kind, qt, j = a
                b = bank.take(pe, SC, ("S", a))
                if kind == "cmp":
                    for h in range(HEADS):
                        g = h // 4
                        if h == 4:
                            b = bank.take(pe, SC, ("S2", a))
                        m = mm(b[:, h % 4 * NCP:(h % 4 + 1) * NCP], qT[64 * g:64 * g + 64, h % 4, qt * P:(qt + 1) * P],
                               kcmp[64 * g:64 * g + 64, :], start=True, stop=True)
                else:
                    br, h = j // HEADS, j % HEADS
                    g = h // 4
                    L = (qt + 1) * P
                    m = mm(b[:, 0:L], qT[64 * g:64 * g + 64, h % 4, qt * P:(qt + 1) * P],
                           kv[64 * g:64 * g + 64, br, 0:L], start=True, stop=True)
                m.then_inc(*s_done.up(a))

            def att_turn(a, n):
                kind, qt, j = a
                pe.wait_ge(*p_ready.at(a))
                b = bank.take(pe, TR, ("T", a))
                for k in range(n):
                    m = nc.tensor.transpose(b[:, k * P:(k + 1) * P], ptile[:, known.get(("pslot", a), 0), k * P:(k + 1) * P], ident[:, :])
                m.then_inc(*pt_done.up(a))

            def att_pv(a, n, key, h, first, rhs, width=HD):
                pe.wait_ge(*ptc.at(a))
                if first:
                    bank.take(pe, OB, key)
                b = bank.tiles[found[("bank", key)]]
                s = known.get(("pslot", a), 0)
                for k in range(n):
                    m = mm(b[:, h * width:(h + 1) * width], pttile[:, s, k * P:(k + 1) * P], rhs(k),
                           start=(first and k == 0), stop=(k == n - 1), skip_group_check=True)
                m.then_inc(*pv_done.up(a))

            def nsa_turn(a):
                att_turn(a, 2 if a[0] == "cmp" else a[1] + 1)

            def nsa_pv(a):
                kind, qt, j = a
                if kind == "cmp":
                    pe.wait_ge(*ptc.at(a))
                    b = bank.take(pe, OB, ("O", qt, 0))
                    s = known.get(("pslot", a), 0)
                    for g in range(2):
                        m = mm(b[:, g * 256:(g + 1) * 256], pttile[:, s, g * P:(g + 1) * P], vblk[:, g, :],
                               start=True, stop=True)
                    m.then_inc(*pv_done.up(a))
                else:
                    br, h = j // HEADS, j % HEADS
                    att_pv(a, qt + 1, ("O", qt, 1 + br), h, h == 0,
                           lambda k: vtok[:, k, br * P + (h // 4) * HD:br * P + (h // 4) * HD + HD])

            def turn_o(phase, qt, n=4):
                for half in range(n // 4):
                    pe.wait_ge(*dve_did.at((phase, "o", qt)))
                    b = bank.take(pe, TR, (phase, "oT", qt, half))
                    for c in range(4):
                        m = nc.tensor.transpose(b[:, c * P:(c + 1) * P],
                                                otile[:, (half * 4 + c) * P:(half * 4 + c + 1) * P],
                                                ident[:, :])
                    m.then_inc(*pe_did.up((phase, "oT", qt, half)))

            pe.wait_ge(*pool_did.at("const"))
            norm("n1")
            for i in range(2 * CC):
                unit("conv", i, first=(lambda k: dve_did.at(("n1", "h", k))) if i == 0 else None)
            for i in range(3):
                tok_unit("tok", i, P if i < 2 else 24)
            for i in range(4):
                unit("q", i)
            for i in range(4):
                unit("k", i)
            hb = [bank.take(pe, TR, ("hid", g)) for g in range(2)]
            for v in range(2):
                pe.wait_ge(*(w1load, w1v_load)[v].at(("w1", v)))
                pe.wait_ge(*dve_did.at(("blk", v)))
                w1 = w1k if v == 0 else w1v
                for g in range(2):
                    for j in range(CMP_BLOCK):
                        m = mm(hb[g][:, v * NCP:v * NCP + NCMP],
                               w1[64 * g:64 * g + 64, j, :], blk[64 * g:64 * g + 64, v, j, :],
                               start=(j == 0), stop=(j == CMP_BLOCK - 1))
            m.then_inc(*pe_did.up("hid"))
            pe.wait_ge(*dve_did.at("hid"))
            pe.wait_ge(*c1load.at("dist"))
            b = bank.take(pe, TR, "cmp2")
            for g in range(2):
                mm(b[64 * g:64 * g + 64, 0:NCMP], w2k[:, :], hidk[:, g, 0:NCMP], start=True, stop=True)
            for g in range(2):
                m = mm(b[:, 64 + g * HD:64 + (g + 1) * HD],
                       tmp[:, 0, 128 + g * P:128 + (g + 1) * P], w2v[:, :], start=True, stop=True)
            m.then_inc(*pe_did.up("cmp2"))
            pe.wait_ge(*dve_did.at("cmp2"))
            pieces = []
            for i in range(DC):
                part = unit("ga", i, inline=False)
                pieces += [(part, k) for k in range(DC)]
            n = len(nsa)
            for i in range(n + 2):
                if i < n:
                    att_scores(nsa[i])
                if 0 <= i - 1 < n:
                    nsa_turn(nsa[i - 1])
                if i >= 2:
                    nsa_pv(nsa[i - 2])
                if pieces:
                    f, k = pieces.pop(0)
                    f(k)
                if i >= 20 and (i - 20) % 17 == 0:
                    turn_o("nsa", (i - 20) // 17)
                if i == 26:
                    stats("mu", CC, src=cacc, ready=lambda c: dve_did.at(("conv", c)))
                if i == 30:
                    spread("mu", 2)
                if i == 35:
                    stats("var", CC)
                if i == 40:
                    spread("var", 4)
            for f, k in pieces:
                f(k)
            turn_o("nsa", TT - 1)
            for i in range(DC):
                unit("gb", i)
                u = UNIT[("y", i)]
                pe.wait_ge(w_split.sem, u + 1)
                for half, pool in ((0, SC), (1, OB)):
                    if i == 0:
                        for c in range(4):
                            pe.wait_ge(*dve_did.at(("y", 4 * half + c)))
                    b = bank.take(pe, pool, ("y", i, half))
                    for k in range(4):
                        kk = 4 * half + k
                        for part, (w, x) in enumerate(((whi, yhi(kk)), (whi, ylo(kk)), (wlo, yhi(kk)))):
                            m = mm(b[:, :], w[:, u % WS, kk * P:(kk + 1) * P], x,
                                   start=(k == 0 and part == 0), stop=(k == 3 and part == 2))
                m.then_inc(*unit_done.up(u))
            for i in range(DC):
                unit("wout", i, first=(lambda k: dve_did.at(("m", k))) if i == 0 else None)
            norm("n2")
            pe.wait_ge(*dve_did.at("cact"))
            modb = bank.take(pe, SC, "mod")

            def ada_unit(j):
                pe.wait_ge(*adaload[j % 2].at(j))
                for k in range(DC):
                    m = mm(modb[:, j:j + 1], ada[:, j % 2, k * P:(k + 1) * P], cact[:, k:k + 1],
                           start=(k == 0), stop=(k == DC - 1))
                m.then_inc(*pe_did.up(("ada", j)))

            for i in range(2 * FC):
                unit("up", i, first=(lambda k: dve_did.at(("n2", "h", k))) if i == 0 else None)
                ada_unit(i)
            for i in range(2 * FC, 6 * DC):
                ada_unit(i)
            order = (0, 1, 2, 3, 6, 7, 4, 5)
            for i in range(FC):
                u = UNIT[("down", i)]
                pe.wait_ge(w_split.sem, u + 1)
                pe.wait_ge(*dve_did.at(("fa", i)))
                for n in range(DC):
                    if i == 0:
                        bank.take(pe, (order[n],), ("down", n))
                    b = bank.tiles[order[n]]
                    hi, lo = y_parts(i % DC)
                    for part, (w, x) in enumerate(((whi, hi), (whi, lo), (wlo, hi))):
                        m = mm(b[:, :], w[:, u % WS, n * P:(n + 1) * P], x,
                               start=(i == 0 and part == 0), stop=(i == FC - 1 and part == 2))
                    if i == FC - 1 and n < DC - 1:
                        m.then_inc(*pe_did.up(("down", n)))
                m.then_inc(*unit_done.up(u))

            norm("f")
            norm("e")

            def attention(phase, filler=None, events=None):
                tiles = tiles_of(phase)
                n = len(tiles)
                P_, PT_ = p_of(phase)
                copied = dve_did if phase == "C" else ptc
                for i in range(n + 3):
                    if i < n:
                        q, k, k0, nk, x = geometry(tiles[i])
                        if phase == "B" and tiles[i][2] == 0:
                            pe.wait_ge(*dve_did.at(("QF", tiles[i][1])))
                        b = bank.take(pe, SC, ("S", tiles[i]))
                        mm(b[:, 0:nk * P], q, k, start=True, stop=True).then_inc(*s_done.up(tiles[i]))
                    if 1 <= i <= n:
                        a = tiles[i - 1]
                        nk = geometry(a)[3]
                        pe.wait_ge(*p_ready.at(a))
                        b = bank.take(pe, TR, ("T", a))
                        for k in range(nk):
                            m = nc.tensor.transpose(b[:, k * P:(k + 1) * P], P_[:, (i - 1) % 2, k * P:(k + 1) * P],
                                                    ident[:, :])
                        m.then_inc(*pt_done.up(a))
                    if 2 <= i <= n + 1:
                        a = tiles[i - 2]
                        k0, nk = geometry(a)[2:4]
                        pe.wait_ge(*copied.at(("PT", a)))
                        if a[2] == 0:
                            ob = bank.take(pe, OB, ("O", phase, a[1]))
                        for k in range(nk):
                            m = mm(ob[:, a[2] * HD:(a[2] + 1) * HD], PT_[:, (i - 2) % 2, k * P:(k + 1) * P],
                                   values(a, k0 + k), start=(a[2] == 0 and k == 0), stop=(k == nk - 1),
                                   skip_group_check=True)
                        m.then_inc(*pv_done.up(a))
                    if filler:
                        f, k = filler.pop(0)
                        f(k)
                    if phase != "B" and i >= 10 and (i - 10) % 8 == 0:
                        turn2(phase, (i - 10) // 8, (ootile if phase == "C" else eotile)[:, :])
                    if events and i in events:
                        events[i]()
                while filler:
                    f, k = filler.pop(0)
                    f(k)

            def turn2(phase, g, src):
                pe.wait_ge(*dve_did.at((phase, "o", g)))
                b = bank.take(pe, TR, (phase, "oT", g))
                for c in range(4):
                    m = nc.tensor.transpose(b[:, c * P:(c + 1) * P], src[:, c * P:(c + 1) * P], ident[:, :])
                m.then_inc(*pe_did.up((phase, "oT", g)))

            unit("ecq", 0, first=lambda k: dve_did.at(("e", "h", k)))
            unit("ecq", 1)
            unit("eckv", 0)
            unit("ekr", 0)
            for i in range(4):
                unit("eq", i)
            unit("ek", 0)
            tok_unit("ev", 0)
            b = bank.take(pe, TR, ("qk", "sum"))
            for c in range(5):
                pe.wait_ge(*sq_ready.at(("qk", c)))
                for tt in range(TT):
                    m = mm(b[:, tt * 10 + 2 * c:tt * 10 + 2 * c + 2],
                           sqt[:, known.get(("sqslot", ("qk", c)), 0), tt * P:(tt + 1) * P], sel2[:, :],
                           start=(c == 0 and tt == 0), stop=(c == 4), skip_group_check=True)
                m.then_inc(*pe_did.up(("qk", "sum", c)))
            stats("cq", 2)
            stats("ckv", 1)
            spread("ckv", 11)
            pe.wait_ge(*dve_did.at(("qk", "stat")))
            b = bank.take(pe, TR, ("qk", "spread"))
            for tt in range(TT):
                for g in range(2):
                    at = EY + tt * 10 + 8 + g
                    m = mm(b[g * HD:(g + 1) * HD, tt * P:(tt + 1) * P], statf[:, at:at + 1].to_broadcast([P, HD]),
                           ident[:, :], start=True, stop=True)
            m.then_inc(*pe_did.up(("qk", "spread")))
            for i in range(4):
                unit("ega", i)
            pe.wait_ge(*dve_did.at("ek"))
            pieces = []
            for i in range(4):
                part = unit("egb", i, inline=False)
                pieces += [(part, k) for k in range(DC)]
            attention("A", pieces)
            for tt in range(TT):
                pe.wait_ge(*dve_did.at("ckv"))
                b = bank.take(pe, LIN, ("vB", tt))
                mm(b[:, :], eckv[:, tt * P:(tt + 1) * P], uv, start=True, stop=True)\
                    .then_inc(*pe_did.up(("vB", tt)))

            def head_prep(h):
                b = bank.take(pe, LIN, ("KF", h))
                mm(b[0:64, :], uk[:, h * HD:(h + 1) * HD], eckv[:, :], start=True, stop=True)\
                    .then_inc(*pe_did.up(("KF", h)))
                b = bank.take(pe, LIN, ("QF", h))
                for k in range(2):
                    m = mm(b[0:96, :], uq[:, k, h, :], ecq[:, k, :], start=(k == 0), stop=(k == 1))
                m.then_inc(*pe_did.up(("QF", h)))

            head_prep(0)
            attention("B", events={4 * h - 3: (lambda h=h: head_prep(h)) for h in range(1, HEADS)})
            for qt in range(TT):
                turn2("B", qt, btok[:, qt, :])
            for i in range(DC):
                unit("eout", i, src=y_parts, first=(lambda k: dve_did.at(("ey", k))) if i == 0 else None)
            norm("o")
            for i in range(DC):
                unit("oq", i, first=(lambda k: dve_did.at(("o", "h", k))) if i == 0 else None)
            for i in range(2):
                unit("ok", i)
            for i in range(2):
                tok_unit("ov", i)
            for i in range(DC):
                unit("og", i)
            pe.wait_ge(*act_did.at(("ok", 1)))
            pe.wait_ge(*act_did.at(("ov", 1)))
            attention("C")
            for i in range(DC):
                unit("oout", i, src=y_parts, first=(lambda k: dve_did.at(("oy", k))) if i == 0 else None)
            stats("z", DC)
            spread("z", 0)

        @block.gpsimd
        def _(pool):
            g = nc.gpsimd
            g.memset(ident[:, :], 0.0).then_inc(*pool_did.up("ident0"))
            g.memset(ones[:, :], 1.0).then_inc(*pool_did.up("ones"))
            g.memset(sel2[:, :], 0.0).then_inc(*pool_did.up("sel0"))
            pool.wait_ge(*pool_did.at("sel0"))
            g.memset(sel2[0:64, 0:1], 1.0).then_inc(*pool_did.up("sel1"))
            g.memset(sel2[64:128, 1:2], 1.0).then_inc(*pool_did.up("sel2"))
            pool.wait_ge(*pool_did.at("sel2"))
            g.affine_select(out=ident[:, :], in_=ident[:, :], compare_op=ALU.not_equal, fill=1.0, base=0,
                            pattern=[[-1, P]], channel_multiplier=1).then_inc(*pool_did.up("const"))

            def split(u0, s, wait_used):
                pool.wait_ge(landed[s % RAW].sem, 16 * ((u0 + s) // RAW + 1) if isinstance(u0, int)
                             else u0 * (16 // RAW) + 16 * (s // RAW + 1))
                if wait_used:
                    pool.wait_ge(unit_done.sem, u0 + (s + 1 - WS))
                g.tensor_tensor(whi[:, s, 0:2], raw[:, s % RAW, 0:2], ones[:, :], ALU.mult)
                g.tensor_scalar(whi[:, s, 2:D], raw[:, s % RAW, 2:D], 1.0, 1.0, ALU.mult, ALU.mult)\
                    .then_inc(w_hi.sem, 1)
                pool.wait_ge(w_hi.sem, u0 + (s + 1))
                g.tensor_tensor(wlo[:, s, :], raw[:, s % RAW, :], whi[:, s, :].bitcast(F32), ALU.subtract)\
                    .then_inc(w_split.sem, 1)

            for s in range(WS):
                split(0, s, False)
            whole = NU // WS * WS
            with pool.Fori(WS, whole, WS) as u0:
                for s in range(WS):
                    split(u0, s, True)
            for s in range(NU - whole):
                split(whole, s, True)

        @block.sync
        def _(sp):
            for c in range(DC):
                sp.dma_start(xT[:, c, :], d["xT"][c]).then_inc(*x2load[c].up(0, 16))
            sp.dma_start(cols[:, :], d["cols"]).then_inc(*loaded.up("cols", 16))

            def load(u, s, wait):
                if wait:
                    sp.wait_ge(w_split.sem, u + (s + 1 - RAW))
                src = d["w"][bass.ds(u + s, 1)] if not isinstance(u, int) else d["w"][u + s:u + s + 1]
                sp.dma_start(raw[:, s, :], src.rearrange("a p n -> (a p) n")).then_inc(landed[s].sem, 16)

            for s in range(RAW):
                load(0, s, False)
            whole = NU // RAW * RAW
            with sp.Fori(RAW, whole, RAW) as u:
                for s in range(RAW):
                    load(u, s, True)
            for s in range(NU - whole):
                load(whole, s, True)
            for i in range(DC):
                sp.wait_ge(*dve_did.at(("res", i)))
                sp.dma_start(out[i], xT[:, i, :]).then_inc(*stored.up(i, 16))
            sp.wait_ge(*stored.at(DC - 1))

        @block.scalar
        def _(act):
            A = nc.scalar.activation
            sqn = [0]

            def row_scale(a):
                if a[0] == "A":
                    at = EV + a[1] * 10 + a[2] % 4 * 2 + a[2] // 4
                    return statf[:, at:at + 1]
                return stat[:, 9, a[2]:a[2] + 1]

            def square(name, c, src, ready):
                s = sqn[0] % 2
                if sqn[0] >= 2:
                    act.wait_ge(*pe_did.at(sqkeys[sqn[0] - 2]))
                found[("sqslot", (name, c))] = s
                sqkeys.append((name, "sum", c))
                sqn[0] += 1
                if ready is not None:
                    act.wait_ge(*ready)
                A(sqt[:, s, :], src, ACT.Square).then_inc(*sq_ready.up((name, c)))

            sqkeys = []

            def h_high(name, n=DC, shift=None):
                for c in range(n):
                    act.wait_ge(*dve_did.at((name, "hs", c)))
                    if shift is None:
                        A(hhi[:, c, :], hs[:, c % 2, :], ACT.Copy).then_inc(*act_did.up((name, "hhi", c)))
                    else:
                        A(hhi[:, c, :], hs[:, c % 2, :], ACT.Identity, bias=shift(c))\
                            .then_inc(*act_did.up((name, "hhi", c)))

            act.dma_start(w1k, d["w1"][0].rearrange("p (j m) -> p j m", m=P)).then_inc(*w1load.up(("w1", 0), 16))
            act.dma_start(w2k, d["w2"][0]).then_inc(*c1load.up("w2k", 16))
            act.dma_start(w2v, d["w2"][1]).then_inc(*c1load.up("w2v", 16))
            act.dma_start(dist, d["dist"]).then_inc(*c1load.up("d", 16))
            act.dma_start(distc, d["distc"]).then_inc(*c1load.up("dist", 16))
            for c in range(DC):
                square("n1", c, xT[:, c, :], x2load[c].at(0))
            h_high("n1")
            act.wait_ge(*dve_did.at(("n1", "hs", DC - 1)))
            act.dma_start(w1v, d["w1"][1].rearrange("p (j m) -> p j m", m=P)).then_inc(*w1v_load.up(("w1", 1), 16))
            for c in range(CC):
                act.wait_ge(*unit_done.at(UNIT[("conv", 2 * c + 1)]))
                if c >= 2:
                    act.wait_ge(*dve_did.at(("z", c - 2)))
                A(hs[:, c % 2, :], bank.of(("conv", 2 * c + 1))[:, :], ACT.Tanh, scale=0.5)\
                    .then_inc(*act_did.up(("convgate", c)))
                bank.freed(("conv", 2 * c + 1), act_did, ("convgate", c))
            for i in range(2):
                act.wait_ge(*unit_done.at(UNIT[("tok", i)]))
                A(vtok[:, :, i * P:(i + 1) * P], bank.of(("tok", i))[:, :].rearrange("p (t n) -> p t n", t=TT),
                  ACT.Copy).then_inc(*act_did.up(("tok", i)))
                bank.freed(("tok", i), act_did, ("tok", i))
            act.wait_ge(*unit_done.at(UNIT[("tok", 2)]))
            A(gate3, bank.of(("tok", 2))[:, :].rearrange("p (t n) -> p t n", t=TT)[:, :, 0:24], ACT.Tanh,
              scale=0.5).then_inc(*act_did.up(("tok", 2)))
            bank.freed(("tok", 2), act_did, ("tok", 2))
            for i in range(4):
                act.wait_ge(*unit_done.at(UNIT[("q", i)]))
                A(qT[:, i, :], bank.of(("q", i))[:, :], ACT.Copy, scale=HD ** -0.5)\
                    .then_inc(*act_did.up(("q", i)))
                bank.freed(("q", i), act_did, ("q", i))
            for i in range(4):
                act.wait_ge(*unit_done.at(UNIT[("k", i)]))
                A(kv[:, i, :], bank.of(("k", i))[:, :], ACT.Copy).then_inc(*act_did.up(("k", i)))
                bank.freed(("k", i), act_did, ("k", i))
            act.wait_ge(*dve_did.at("cubic"))
            A(gel[:, 0, 256:256 + 4 * NCP], gel[:, 0, 128:128 + 4 * NCP], ACT.Tanh, scale=0.7978845608028654)\
                .then_inc(*act_did.up("gelu"))
            act.wait_ge(*pe_did.at("cmp2"))
            act.wait_ge(*c1load.at("dist"))
            for h in range(HEADS):
                A(bias[:, h, :], dist[:, :], ACT.Copy, scale=2.0 ** -(h + 1)).then_inc(*act_did.up(("bias", h)))
                A(biasc[:, :, h, :], distc.rearrange("p (t n) -> p t n", t=TT), ACT.Copy,
                  scale=2.0 ** -(h + 1)).then_inc(*act_did.up(("biasc", h)))

            n = len(nsa)

            def exp_tile(i):
                a = nsa[i]
                kind, qt, j = a
                found[("pslot", a)] = i % 2
                act.wait_ge(*sm_ready.at(a))
                if kind == "cmp":
                    A(ptile[:, i % 2, 0:256], ptile[:, i % 2, 0:256], ACT.Exp).then_inc(*p_ready.up(a))
                else:
                    L = (qt + 1) * P
                    x = qt * 16 + j
                    A(ptile[:, i % 2, 0:L], ptile[:, i % 2, 0:L], ACT.Exp, bias=nmax[:, x:x + 1], scale=-1.0,
                      accum_out=rsum[:, x:x + 1]).then_inc(*p_ready.up(a))

            def copy_tile(i):
                a = nsa[i]
                w = 256 if a[0] == "cmp" else (a[1] + 1) * P
                act.wait_ge(*pt_done.at(a))
                if i >= 2:
                    act.wait_ge(*pv_done.at(nsa[i - 2]))
                A(pttile[:, i % 2, 0:w], bank.of(("T", a))[:, 0:w], ACT.Copy).then_inc(*ptc.up(a))
                bank.freed(("T", a), ptc, a)

            def ga_evac(i):
                if i == 0:
                    act.wait_ge(*pe_did.at("cmp2"))
                act.wait_ge(*unit_done.at(UNIT[("ga", i)]))
                A(merged[:, i, :], bank.of(("ga", i))[:, :], ACT.Tanh, scale=0.5)\
                    .then_inc(*act_did.up(("ga", i)))
                bank.freed(("ga", i), act_did, ("ga", i))

            def o_high(qt):
                act.wait_ge(*pe_did.at(("nsa", "oT", qt, 0)))
                A(ysplit[:, 0:4, qt * P:(qt + 1) * P],
                  bank.of(("nsa", "oT", qt, 0))[:, :].rearrange("p (c t) -> p c t", c=4), ACT.Copy)\
                    .then_inc(*act_did.up(("ohi", qt)))

            for i in range(n + 1):
                if i < n:
                    exp_tile(i)
                if i >= 1:
                    copy_tile(i - 1)
                if i >= 10 and (i - 10) % 8 == 0 and (i - 10) // 8 < DC:
                    ga_evac((i - 10) // 8)
                if i >= 21 and (i - 21) % 17 == 0:
                    o_high((i - 21) // 17)
                if i == 34:
                    for c in range(CC):
                        square("var", c, cacc[:, c, :], dve_did.at(("zc", c)))
                if i == 46:
                    for c in range(CC):
                        act.wait_ge(*dve_did.at(("zn", c)))
                        A(cacc[:, c, :], cacc[:, c, :], ACT.Identity, scale=col("lng", c), bias=col("lnb", c))\
                            .then_inc(*act_did.up(("zu", c)))
                        if c >= 2:
                            act.wait_ge(*dve_did.at(("zs", c - 2)))
                        act.wait_ge(*act_did.at(("zu", c)))
                        A(hs[:, c % 2, :], cacc[:, c, :], ACT.Tanh, scale=0.5).then_inc(*act_did.up(("zt", c)))
                if i == 56:
                    for c in range(CC):
                        act.wait_ge(*dve_did.at(("zs", c)))
                        A(yhi(4 + c), cacc[:, c, :], ACT.Copy, scale=0.5).then_inc(*act_did.up(("zhi", c)))
            for i in range(DC):
                if 10 + 8 * i > n:
                    ga_evac(i)
            o_high(TT - 1)
            for i in range(DC):
                act.wait_ge(*unit_done.at(UNIT[("gb", i)]))
                if i >= 2:
                    act.wait_ge(*dve_did.at(("mg", i - 2)))
                A(hs[:, i % 2, :], bank.of(("gb", i))[:, :], ACT.Tanh, scale=0.5)\
                    .then_inc(*act_did.up(("gb", i)))
                bank.freed(("gb", i), act_did, ("gb", i))
            for i in range(DC):
                if i == 0:
                    act.wait_ge(*unit_done.at(UNIT[("gb", DC - 1)]))
                act.wait_ge(*dve_did.at(("mg", i)))
                A(hhi[:, i, :], merged[:, i, :], ACT.Copy, scale=0.5).then_inc(*act_did.up(("mhi", i)))
            for i in range(DC):
                act.wait_ge(*dve_did.at(("m", i)))
                act.dma_start(xT[:, i, :], d["xT"][i]).then_inc(*x2load[i].up(1, 16))
            for i in range(DC):
                square("n2", i, xT[:, i, :], dve_did.at(("x1", i)))
            h_high("n2")
            A(cact[:, :], col("c", 0, DC), ACT.Tanh, scale=0.5).then_inc(*act_did.up("cact"))
            def ffn_conv(i):
                u = UNIT[("up", i)]
                act.wait_ge(*unit_done.at(u))
                if i >= 4:
                    act.wait_ge(*dve_did.at(("fs", (i - 4) // 2)))
                A(ua[:, i % 4, :], bank.of(("up", i))[:, :], ACT.Identity,
                  scale=col("ffw", order_up(i) * 3 + 2), bias=col("ffb", order_up(i)))\
                    .then_inc(*act_did.up(("uc", i)))

            def ffn_tanh(j):
                act.wait_ge(*dve_did.at(("ut", 2 * j)))
                if j >= 2:
                    act.wait_ge(*dve_did.at(("fs", j - 2)))
                A(ft[:, j % 2, :], ua[:, (2 * j) % 4, :], ACT.Tanh, scale=0.5).then_inc(*act_did.up(("ft", j)))

            def fa_high(i):
                if i >= DC:
                    act.wait_ge(*unit_done.at(UNIT[("down", i - DC)]))
                act.wait_ge(*dve_did.at(("fs", i)))
                A(yhi(i % DC), fa[:, i, :], ACT.Copy, scale=0.5).then_inc(*act_did.up(("fhi", i)))

            def ada_load(j):
                if j >= 2:
                    act.wait_ge(*pe_did.at(("ada", j - 2)))
                act.dma_start(ada[:, j % 2, :], d["ada"][j]).then_inc(*adaload[j % 2].up(j, 16))

            ada_load(0)
            ada_load(1)
            for i in range(2 * FC):
                ffn_conv(i)
                if 1 <= i:
                    ada_load(i + 1)
                if i >= 2 and i % 2 == 0:
                    ffn_tanh(i // 2 - 1)
            ffn_tanh(FC - 1)
            for j in range(2 * FC + 1, 6 * DC):
                ada_load(j)
            for i in range(FC):
                fa_high(i)
            for i in range(DC):
                square("f", i, xT[:, i, :], dve_did.at(("x2", i)))
            act.wait_ge(*unit_done.at(UNIT[("down", FC - 1)]))
            for dst, name in ((cosA, "cosA"), (sinA, "sinA"), (cosT, "cosT"), (sinT, "sinT"), (uk, "uk"), (uv, "uv")):
                act.dma_start(dst, d[name]).then_inc(*tabload.up(name, 16))
            act.dma_start(late[:, 2 * T:2 * T + 1536], d["uq"]).then_inc(*tabload.up("all", 16))
            for i in range(DC):
                square("e", i, xT[:, i, :], dve_did.at(("xn", i)))
            h_high("e", shift=lambda c: modc[:, 0, c:c + 1])

            def evac(name, i, dst, func=ACT.Copy, scale=1.0, key=None):
                act.wait_ge(*unit_done.at(UNIT[(name, i)]))
                A(dst, bank.of((name, i))[:, :], func, scale=scale).then_inc(*act_did.up(key or (name, i)))

            def square_unit(name, i, key, c):
                act.wait_ge(*unit_done.at(UNIT[(name, i)]))
                square(key, c, bank.of((name, i))[:, :], None)

            def tok_evac(name, i, dst):
                act.wait_ge(*unit_done.at(UNIT[(name, i)]))
                A(dst, bank.of((name, i))[:, :].rearrange("p (t n) -> p t n", t=TT), ACT.Copy)\
                    .then_inc(*act_did.up((name, i)))
                bank.freed((name, i), act_did, (name, i))

            for i in range(2):
                act.wait_ge(*dve_did.at(("cqraw", i)))
                evac("ecq", i, ecq[:, i, :], scale=col("cqg", i))
                bank.freed(("ecq", i), act_did, ("ecq", i))
            act.wait_ge(*dve_did.at("ckvraw"))
            evac("eckv", 0, eckv[:, :], scale=col("ckvg"))
            bank.freed(("eckv", 0), act_did, ("eckv", 0))
            evac("ekr", 0, ekr[:, :])
            bank.freed(("ekr", 0), act_did, ("ekr", 0))
            for i in range(4):
                evac("eq", i, eq[:, i, :])
                bank.freed(("eq", i), act_did, ("eq", i))
            evac("ek", 0, ek[:, :])
            bank.freed(("ek", 0), act_did, ("ek", 0))
            tok_evac("ev", 0, ev)
            for c in range(5):
                square("qk", c, eq[:, c, :] if c < 4 else ek[:, :], act_did.at(("eq", c) if c < 4 else ("ek", 0)))
            for c in range(2):
                square("cq", c, etmp[:, c, :], dve_did.at(("cqraw", c)))
            square("ckv", 0, etmp[:, 2, :], dve_did.at("ckvraw"))
            for i in range(4):
                act.wait_ge(*unit_done.at(UNIT[("ega", i)]))
                A(esg[:, i, :], bank.of(("ega", i))[:, :], ACT.Tanh, scale=0.5).then_inc(*act_did.up(("ega", i)))

            def attention(phase, events=None):
                tiles = tiles_of(phase)
                n = len(tiles)
                P_, PT_ = p_of(phase)
                for i in range(n + 5):
                    if i < n:
                        a = tiles[i]
                        nk, x = geometry(a)[3:5]
                        act.wait_ge(*sm_ready.at(a))
                        if phase == "C":
                            A(P_[:, i % 2, 0:nk * P], P_[:, i % 2, 0:nk * P], ACT.Exp, bias=nmax[:, x:x + 1],
                              scale=-1.0, accum_out=rsum[:, x:x + 1]).then_inc(*p_ready.up(a))
                        else:
                            if i >= 2:
                                act.wait_ge(*pt_done.at(tiles[i - 2]))
                            A(P_[:, i % 2, :], bank.of(("S", a))[:, :], ACT.Exp, bias=nmax[:, x:x + 1],
                              scale=row_scale(a), accum_out=rsum[:, x:x + 1]).then_inc(*p_ready.up(a))
                            bank.freed(("S", a), p_ready, a)
                    if 1 <= i <= n and phase != "C":
                        a = tiles[i - 1]
                        act.wait_ge(*pt_done.at(a))
                        if i >= 3:
                            act.wait_ge(*pv_done.at(tiles[i - 3]))
                        A(PT_[:, (i - 1) % 2, :], bank.of(("T", a))[:, :], ACT.Copy)\
                            .then_inc(*ptc.up(("PT", a)))
                        bank.freed(("T", a), ptc, ("PT", a))
                    if phase != "B" and i >= 12 and (i - 12) % 8 == 0:
                        y_high(phase, (i - 12) // 8)
                    if phase == "C" and i >= 9 and (i - 9) % 8 == 0:
                        g = (i - 9) // 8
                        act.wait_ge(*dve_did.at(("sink", g)))
                        A(esink[:, g * 8:g * 8 + 8], esink[:, g * 8:g * 8 + 8], ACT.Exp)\
                            .then_inc(*act_did.up(("esink", g)))
                    if events and i in events:
                        events[i]()

            def y_high(phase, g):
                act.wait_ge(*dve_did.at((phase, "gated", g)))
                if phase == "C":
                    s, qt, tmp_ = g % 2 * 8, g // 2, otmp[:, 0, :]
                else:
                    s, qt, tmp_ = {"A": 0, "B": 8}[phase], g, etmp[:, g % 2, :]
                A(ysplit[:, s:s + 4, qt * P:(qt + 1) * P], tmp_.rearrange("p (c t) -> p c t", c=4), ACT.Copy,
                  scale=0.5).then_inc(*act_did.up((phase, "yhi", g)))

            def gb_evac(i):
                act.wait_ge(*unit_done.at(UNIT[("egb", i)]))
                A(esg[:, 4 + i, :], bank.of(("egb", i))[:, :], ACT.Tanh, scale=0.5).then_inc(*act_did.up(("egb", i)))

            attention("A", {10: lambda: gb_evac(0), 18: lambda: gb_evac(1), 26: lambda: gb_evac(2),
                            34: lambda: gb_evac(3)})
            for tt in range(TT):
                act.wait_ge(*pe_did.at(("vB", tt)))
                A(vB[:, tt, :], bank.of(("vB", tt))[:, :], ACT.Copy).then_inc(*act_did.up(("vB", tt)))
                bank.freed(("vB", tt), act_did, ("vB", tt))

            def head_copy(h):
                act.wait_ge(*pe_did.at(("KF", h)))
                A(KF[0:64, h % 2, :], bank.of(("KF", h))[0:64, :], ACT.Copy).then_inc(*act_did.up(("KF", h)))
                bank.freed(("KF", h), act_did, ("KF", h))
                act.wait_ge(*pe_did.at(("QF", h)))
                A(QF[0:96, h % 2, :], bank.of(("QF", h))[0:96, :], ACT.Copy).then_inc(*act_did.up(("QF", h)))
                bank.freed(("QF", h), act_did, ("QF", h))

            head_copy(0)
            attention("B", {4 * h - 2: (lambda h=h: head_copy(h)) for h in range(1, HEADS)})
            for g in range(TT):
                y_high("B", g)
            for i in range(DC):
                square("o", i, xT[:, i, :], dve_did.at(("x3", i)))
            h_high("o", shift=lambda c: modc[:, 1, c:c + 1])
            act.dma_start(distC, d["distC"]).then_inc(*tabload.up("distC", 16))
            for i in range(DC):
                evac("oq", i, oq[:, i, :], scale=HD ** -0.5)
                bank.freed(("oq", i), act_did, ("oq", i))
            for i in range(2):
                evac("ok", i, ok[:, i, :])
                bank.freed(("ok", i), act_did, ("ok", i))
            for i in range(2):
                tok_evac("ov", i, ov[:, :, i * P:(i + 1) * P])
            for i in range(DC):
                act.wait_ge(*unit_done.at(UNIT[("og", i)]))
                A(osg[:, i, :], bank.of(("og", i))[:, :], ACT.Tanh, scale=0.5).then_inc(*act_did.up(("og", i)))
            act.wait_ge(*tabload.at("distC"))
            for h in range(C_HEADS):
                A(obias[:, h, :], distC[:, :], ACT.Copy, scale=2.0 ** (-8.0 * (h + 1) / C_HEADS))\
                    .then_inc(*act_did.up(("obias", h)))
            attention("C")
            for i in range(DC):
                square("z", i, xT[:, i, :], dve_did.at(("x4", i)))

        @block.vector
        def _(dve):
            V = nc.vector

            def link(ins):
                ins.then_inc(*dve_did.up(("link", dve_did.n)))
                dve.wait_ge(dve_did.sem, dve_did.n)

            def rstd(name, c0, scale):
                v, y, t = stat[:, c0 + 1, 0:TT], stat[:, c0, 0:TT], stat[:, c0 + 2, 0:TT]
                link(V.tensor_scalar(v, bank.of((name, "sum"))[:, 0:TT], scale, EPS, ALU.mult, ALU.add))
                bank.freed((name, "sum"), dve_did, ("link", dve_did.n - 1))
                link(V.tensor_scalar(t.bitcast(I32), v.bitcast(I32), 1, None, ALU.logical_shift_right))
                link(V.tensor_scalar(y.bitcast(I32), t.bitcast(I32), -1.0, float(0x5f3759df), ALU.mult, ALU.add))
                for step in range(4):
                    link(V.scalar_tensor_tensor(t, y, -0.5, y, ALU.mult, ALU.mult))
                    link(V.tensor_tensor(t, t, v, ALU.mult))
                    last = V.scalar_tensor_tensor(y, t, 1.5, y, ALU.add, ALU.mult)
                    if step < 3:
                        link(last)
                last.then_inc(*dve_did.up((name, "stat")))

            def h_split(name, src, gain, shift=None):
                dve.wait_ge(*pe_did.at((name, "spread")))
                b = bank.of((name, "spread"))
                for c in range(DC + 1):
                    if c < DC:
                        if c >= 2:
                            dve.wait_ge(*dve_did.at((name, "h", c - 2)))
                        V.scalar_tensor_tensor(hs[:, c % 2, :], src(c), gain(c), b[:, :], ALU.mult, ALU.mult)\
                            .then_inc(*dve_did.up((name, "hs", c)))
                        if c == DC - 1:
                            bank.freed((name, "spread"), dve_did, (name, "hs", c))
                    if c >= 1:
                        k = c - 1
                        dve.wait_ge(*act_did.at((name, "hhi", k)))
                        if shift is None:
                            V.tensor_tensor(hlo[:, k, :], hs[:, k % 2, :], hhi[:, k, :].bitcast(F32),
                                            ALU.subtract).then_inc(*dve_did.up((name, "h", k)))
                        else:
                            V.scalar_tensor_tensor(hlo[:, k, :], hs[:, k % 2, :], shift(k),
                                                   hhi[:, k, :].bitcast(F32), ALU.add, ALU.subtract)\
                                .then_inc(*dve_did.up((name, "h", k)))

            def norm(name, gain, src=lambda c: xT[:, c, :], scale=1.0 / D, shift=None):
                dve.wait_ge(*pe_did.at((name, "sum", DC - 1)))
                rstd(name, 0, scale)
                h_split(name, src, gain, shift)

            link(V.memset(z[:, :, 0:TAPS - 1], 0.0))
            dve.wait_ge(*loaded.at("cols"))
            link(V.tensor_scalar(ctap, col("dww", 0, CC * TAPS).rearrange("p (c n) -> p c n", c=CC), 0.5, None,
                                 ALU.mult))
            norm("n1", lambda c: col("n1g", c))
            for c in range(CC):
                dve.wait_ge(*act_did.at(("convgate", c)))
                V.scalar_tensor_tensor(z[:, c, TAPS - 1:ZW], hs[:, c % 2, :], 1.0, bank.of(("conv", 2 * c))[:, :],
                                       ALU.add, ALU.mult).then_inc(*dve_did.up(("z", c)))
                bank.freed(("conv", 2 * c), dve_did, ("z", c))
                if c == CC - 1:
                    dve.wait_ge(*dve_did.at(("z", c)))
            steps = [(k, c) for k in range(TAPS - 1, -1, -1) for c in range(CC)]

            def tap(k, c):
                w = ctap[:, c, k:k + 1]
                if k == TAPS - 1:
                    V.tensor_scalar(cacc[:, c, :], z[:, c, k:k + T], w, col("dwb", c), ALU.mult, ALU.add)\
                        .then_inc(*dve_did.up(("tap", k, c)))
                    return
                dve.wait_ge(*dve_did.at(("tap", k + 1, c)))
                V.scalar_tensor_tensor(cacc[:, c, :], z[:, c, k:k + T], w, cacc[:, c, :], ALU.mult, ALU.add)\
                    .then_inc(*dve_did.up(("conv", c) if k == 0 else ("tap", k, c)))

            for k, c in steps[:96]:
                tap(k, c)
            steps = steps[96:]
            dve.wait_ge(*act_did.at(("tok", 2)))
            link(V.tensor_scalar(gate3, gate3, 0.5, 0.5, ALU.mult, ALU.add))
            for v in range(2):
                dve.wait_ge(*act_did.at(("k", 2 + v)))
                win = kv[:, 2 + v, :].rearrange("p (m b) -> p b m", b=CMP_STRIDE)
                pe_ = col("pek" if v == 0 else "pev", 0, CMP_BLOCK)
                for half in range(2):
                    ins = V.tensor_tensor(
                        blk[:, v, half * CMP_STRIDE:(half + 1) * CMP_STRIDE, :],
                        win[:, :, half:half + NCMP],
                        pe_[:, half * CMP_STRIDE:(half + 1) * CMP_STRIDE].unsqueeze(2)
                        .to_broadcast([P, CMP_STRIDE, NCMP]), ALU.add)
                    if half == 0:
                        ins.then_inc(*dve_did.up(("blk0", v)))
                    else:
                        ins.then_inc(*dve_did.up(("blk", v)))
            W = 4 * NCP
            gx, g3, gt = gel[:, 0, 0:W], gel[:, 0, 128:128 + W], gel[:, 0, 256:256 + W]
            dve.wait_ge(*act_did.at(("convgate", CC - 1)))
            link(V.memset(gel[:, 0, 0:384], 0.0))
            link(V.memset(tmp[:, 0, :], 0.0))
            link(V.memset(kcmp, 0.0))
            link(V.memset(vblk, 0.0))
            dve.wait_ge(*pe_did.at("hid"))
            hx = gx.rearrange("p (g n) -> p g n", g=4)[:, :, 0:NCMP]
            for g in range(2):
                link(V.tensor_copy(hx[:, g:4:2, :],
                                   bank.of(("hid", g))[:, 0:2 * NCP].rearrange("p (v n) -> p v n", v=2)[:, :, 0:NCMP]))
                bank.freed(("hid", g), dve_did, ("link", dve_did.n - 1))
            link(V.tensor_tensor(g3, gx, gx, ALU.mult))
            link(V.tensor_scalar(g3, g3, 0.044715, 1.0, ALU.mult, ALU.add))
            V.tensor_tensor(g3, g3, gx, ALU.mult).then_inc(*dve_did.up("cubic"))
            dve.wait_ge(*act_did.at("gelu"))
            link(V.tensor_scalar(gt, gt, 0.5, 0.5, ALU.mult, ALU.add))
            hg = lambda v, g: (gt[:, (2 * v + g) * NCP:(2 * v + g) * NCP + NCMP],
                               gx[:, (2 * v + g) * NCP:(2 * v + g) * NCP + NCMP])
            for g in range(2):
                link(V.tensor_tensor(hidk[:, g, 0:NCMP], *hg(0, g), ALU.mult))
                for r in range(4):
                    ins = V.tensor_tensor(hidv[:, g, r, 0:NCMP], *hg(1, g), ALU.mult)
                    if g == 1 and r == 3:
                        ins.then_inc(*dve_did.up("hid"))
                    else:
                        link(ins)
            dve.wait_ge(*pe_did.at("cmp2"))
            c2 = bank.of("cmp2")
            link(V.tensor_copy(kcmp[:, 0:NCMP], c2[:, 0:NCMP]))
            for g in range(2):
                for r in range(4):
                    ins = V.tensor_copy(vblk[32 * r:32 * r + 32, g, r * HD:(r + 1) * HD],
                                        c2[32 * r:32 * r + 32, 64 + g * HD:64 + (g + 1) * HD])
                    if g == 1 and r == 3:
                        ins.then_inc(*dve_did.up("cmp2"))
                    else:
                        link(ins)
            bank.freed("cmp2", dve_did, "cmp2")
            n = len(nsa)
            dve.wait_ge(*act_did.at(("biasc", HEADS - 1)))

            def score_tile(i):
                a = nsa[i]
                kind, qt, j = a
                dve.wait_ge(*s_done.at(a))
                if i >= 2:
                    dve.wait_ge(*pt_done.at(nsa[i - 2]))
                    if nsa[i - 2][0] == "cmp":
                        dve.wait_ge(*dve_did.at(("csum", nsa[i - 2][1])))
                S = bank.of(("S", a))
                if kind == "cmp":
                    x = 128 + qt * 8
                    sc3 = ptile[:, i % 2, 0:256].rearrange("p (h n) -> p h n", h=HEADS)
                    for g in range(2):
                        half = slice(g * 128, (g + 1) * 128)
                        link(V.tensor_tensor(ptile[:, i % 2, half], bank.of((("S", "S2")[g], a))[:, 0:128],
                                             biasc[:, qt].rearrange("p h n -> p (h n)")[:, half], ALU.add))
                    bank.freed(("S2", a), sm_ready, a)
                    link(V.tensor_reduce(nmax[:, x:x + 8], sc3, AX_X, ALU.max))
                    V.tensor_tensor(sc3, sc3, nmax[:, x:x + 8].unsqueeze(2).to_broadcast([P, HEADS, NCP]),
                                    ALU.subtract).then_inc(*sm_ready.up(a))
                else:
                    L = (qt + 1) * P
                    x = qt * 16 + j
                    V.tensor_tensor_reduce(ptile[:, i % 2, 0:L], S[:, 0:L],
                                           bias[:, j % HEADS, T - L:T], -1.0, 3.0e38, ALU.add, ALU.min,
                                           nmax[:, x:x + 1]).then_inc(*sm_ready.up(a))
                bank.freed(("S", a), sm_ready, a)

            def o_add(qt, part):
                a = ("cmp", qt, 0) if part == 0 else ("nsa", qt, part * HEADS - 1)
                dve.wait_ge(*pv_done.at(a))
                x = 128 + qt * 8 if part == 0 else qt * 16 + (part - 1) * HEADS
                r = rinv[:, x:x + 8]
                link(V.reciprocal(r, rsum[:, x:x + 8]))
                link(V.tensor_tensor(r, r, gate3[:, qt, part:24:3], ALU.mult))
                if part == 0 and qt == 0:
                    link(V.tensor_scalar(r, r, col("rowvalid"), None, ALU.mult))
                O = bank.of(("O", qt, part))[:, :].rearrange("p (h e) -> p h e", h=HEADS)
                rb = r.unsqueeze(2).to_broadcast([P, HEADS, HD])
                if part == 0 and qt >= 1:
                    dve.wait_ge(*pe_did.at(("nsa", "oT", qt - 1, 0)))
                dst = otile if part == 0 else tmp[:, 1, :]
                ins = V.tensor_tensor(dst.rearrange("p (h e) -> p h e", h=HEADS), O, rb, ALU.mult)
                link(ins)
                bank.freed(("O", qt, part), dve_did, ("link", dve_did.n - 1))
                if part:
                    ins = V.tensor_tensor(otile, otile, tmp[:, 1, :], ALU.add)
                    if part == 1:
                        link(ins)
                    else:
                        ins.then_inc(*dve_did.up(("nsa", "o", qt)))

            def cmp_sum(i):
                a = nsa[i]
                x = 128 + a[1] * 8
                dve.wait_ge(*p_ready.at(a))
                V.tensor_reduce(rsum[:, x:x + 8], ptile[:, i % 2, 0:256].rearrange("p (h n) -> p h n", h=HEADS),
                                AX_X, ALU.add).then_inc(*dve_did.up(("csum", a[1])))

            def o_low(qt):
                dve.wait_ge(*act_did.at(("ohi", qt)))
                V.tensor_tensor(ysplit[:, 4:8, qt * P:(qt + 1) * P],
                                bank.of(("nsa", "oT", qt, 0))[:, :].rearrange("p (c t) -> p c t", c=4),
                                ysplit[:, 0:4, qt * P:(qt + 1) * P].bitcast(F32), ALU.subtract)\
                    .then_inc(*dve_did.up(("olo", qt)))
                bank.freed(("nsa", "oT", qt, 0), dve_did, ("olo", qt))

            def neg_mean():
                dve.wait_ge(*pe_did.at(("mu", "sum", CC - 1)))
                V.tensor_scalar(stat[:, 2, 0:TT], bank.of(("mu", "sum"))[:, 0:TT], -1.0 / CONV_CH, None, ALU.mult)\
                    .then_inc(*dve_did.up(("mu", "stat")))
                bank.freed(("mu", "sum"), dve_did, ("mu", "stat"))

            def center():
                dve.wait_ge(*pe_did.at(("mu", "spread")))
                for c in range(CC):
                    V.tensor_tensor(cacc[:, c, :], cacc[:, c, :], bank.of(("mu", "spread"))[:, :], ALU.add)\
                        .then_inc(*dve_did.up(("zc", c)))
                bank.freed(("mu", "spread"), dve_did, ("zc", CC - 1))

            def var_rstd():
                dve.wait_ge(*pe_did.at(("var", "sum", CC - 1)))
                rstd("var", 4, 1.0 / CONV_CH)

            def scale_z():
                dve.wait_ge(*pe_did.at(("var", "spread")))
                for c in range(CC):
                    V.tensor_tensor(cacc[:, c, :], cacc[:, c, :], bank.of(("var", "spread"))[:, :], ALU.mult)\
                        .then_inc(*dve_did.up(("zn", c)))
                bank.freed(("var", "spread"), dve_did, ("zn", CC - 1))

            def silu_z():
                for c in range(CC):
                    dve.wait_ge(*act_did.at(("zt", c)))
                    V.scalar_tensor_tensor(cacc[:, c, :], hs[:, c % 2, :], 1.0, cacc[:, c, :], ALU.add, ALU.mult)\
                        .then_inc(*dve_did.up(("zs", c)))

            def low_z():
                for c in range(CC):
                    dve.wait_ge(*act_did.at(("zhi", c)))
                    V.scalar_tensor_tensor(ylo(4 + c), cacc[:, c, :], 0.5, yhi(4 + c).bitcast(F32),
                                           ALU.mult, ALU.subtract).then_inc(*dve_did.up(("y", 4 + c)))

            events = {28: neg_mean, 32: center, 37: var_rstd, 42: scale_z, 46: silu_z, 60: low_z}
            for i in range(n + 3):
                if i < n:
                    score_tile(i)
                if i in events:
                    events[i]()
                if 1 <= i and nsa[min(i - 1, n - 1)][0] == "cmp" and i - 1 < n:
                    cmp_sum(i - 1)
                j = i - 3
                if j >= 0:
                    a = nsa[j]
                    if a[0] == "cmp":
                        o_add(a[1], 0)
                    elif a[2] % HEADS == HEADS - 1:
                        o_add(a[1], 1 + a[2] // HEADS)
                for s in steps[:2]:
                    tap(*s)
                steps = steps[2:]
                if i >= 22 and (i - 22) % 17 == 0:
                    o_low((i - 22) // 17)
            dve.wait_ge(*act_did.at(("ohi", TT - 1)))
            o_low(TT - 1)
            for c in range(4):
                found[("dve_did", ("y", c))] = dve_did.n
            for i in range(DC):
                dve.wait_ge(*unit_done.at(UNIT[("y", i)]))
                if i == 0:
                    dve.wait_ge(*act_did.at(("ga", DC - 1)))
                link(V.scalar_tensor_tensor(merged[:, i, :], merged[:, i, :], 1.0, bank.of(("y", i, 0))[:, :],
                                            ALU.add, ALU.mult))
                bank.freed(("y", i, 0), dve_did, ("link", dve_did.n - 1))
                dve.wait_ge(*act_did.at(("gb", i)))
                link(V.scalar_tensor_tensor(tmp[:, 1, :], hs[:, i % 2, :], 1.0, bank.of(("y", i, 1))[:, :],
                                            ALU.add, ALU.mult))
                bank.freed(("y", i, 1), dve_did, ("link", dve_did.n - 1))
                V.tensor_tensor(merged[:, i, :], merged[:, i, :], tmp[:, 1, :], ALU.add)\
                    .then_inc(*dve_did.up(("mg", i)))
            for i in range(DC):
                dve.wait_ge(*act_did.at(("mhi", i)))
                V.scalar_tensor_tensor(hlo[:, i, :], merged[:, i, :], 0.5, hhi[:, i, :].bitcast(F32),
                                       ALU.mult, ALU.subtract).then_inc(*dve_did.up(("m", i)))
            for i in range(DC):
                dve.wait_ge(*unit_done.at(UNIT[("wout", i)]))
                dve.wait_ge(*x2load[i].at(1))
                V.tensor_tensor(xT[:, i, :], xT[:, i, :], bank.of(("wout", i))[:, :], ALU.add)\
                    .then_inc(*dve_did.up(("x1", i)))
                bank.freed(("wout", i), dve_did, ("x1", i))
            norm("n2", lambda c: col("n2g", c))

            dve.wait_ge(*act_did.at("cact"))
            link(V.scalar_tensor_tensor(cact[:, :], cact[:, :], 1.0, col("c", 0, DC), ALU.add, ALU.mult))
            V.tensor_scalar(cact[:, :], cact[:, :], 0.5, None, ALU.mult).then_inc(*dve_did.up("cact"))

            def ffn_taps(i):
                dve.wait_ge(*act_did.at(("uc", i)))
                b, s, w = bank.of(("up", i)), i % 4, order_up(i) * 3
                link(V.scalar_tensor_tensor(ua[:, s, 1:T], b[:, 0:T - 1], col("ffw", w + 1), ua[:, s, 1:T],
                                            ALU.mult, ALU.add))
                V.scalar_tensor_tensor(ua[:, s, 2:T], b[:, 0:T - 2], col("ffw", w), ua[:, s, 2:T],
                                       ALU.mult, ALU.add).then_inc(*dve_did.up(("ut", i)))
                bank.freed(("up", i), dve_did, ("ut", i))

            def ffn_mul(j):
                dve.wait_ge(*act_did.at(("ft", j)))
                sa, sv = (2 * j) % 4, (2 * j + 1) % 4
                link(V.scalar_tensor_tensor(ft[:, j % 2, :], ft[:, j % 2, :], 1.0, ua[:, sa, :], ALU.add, ALU.mult))
                V.tensor_tensor(fa[:, j, :], ft[:, j % 2, :], ua[:, sv, :], ALU.mult)\
                    .then_inc(*dve_did.up(("fs", j)))

            for i in range(2 * FC):
                ffn_taps(i)
                if i % 2 == 1 and i >= 3:
                    ffn_mul(i // 2 - 1)
            ffn_mul(FC - 1)
            dve.wait_ge(*pe_did.at(("ada", 6 * DC - 1)))
            link(V.tensor_tensor(modc[:].rearrange("p l c -> p (l c)"), bank.of("mod")[:, 0:6 * DC],
                                 col("adab", 0, 6 * DC), ALU.add))
            bank.freed("mod", dve_did, ("link", dve_did.n - 1))
            for layer in range(2):
                link(V.scalar_tensor_tensor(gn[:, layer, :], modc[:, layer, DC:2 * DC], 1.0,
                                            col("nw", layer * DC, DC), ALU.add, ALU.mult))
            for i in range(FC):
                dve.wait_ge(*act_did.at(("fhi", i)))
                V.scalar_tensor_tensor(ylo(i % DC), fa[:, i, :], 0.5, yhi(i % DC).bitcast(F32),
                                       ALU.mult, ALU.subtract).then_inc(*dve_did.up(("fa", i)))
            for i in range(DC):
                if i < DC - 1:
                    dve.wait_ge(*pe_did.at(("down", i)))
                else:
                    dve.wait_ge(*unit_done.at(UNIT[("down", FC - 1)]))
                V.tensor_tensor(xT[:, i, :], xT[:, i, :], bank.of(("down", i))[:, :], ALU.add)\
                    .then_inc(*dve_did.up(("x2", i)))
                bank.freed(("down", i), dve_did, ("x2", i))

            def norm_in_place(name, gain, key):
                dve.wait_ge(*pe_did.at((name, "sum", DC - 1)))
                rstd(name, 0, 1.0 / D)
                dve.wait_ge(*pe_did.at((name, "spread")))
                for c in range(DC):
                    V.scalar_tensor_tensor(xT[:, c, :], xT[:, c, :], gain(c), bank.of((name, "spread"))[:, :],
                                           ALU.mult, ALU.mult).then_inc(*dve_did.up((key, c)))
                bank.freed((name, "spread"), dve_did, (key, DC - 1))

            norm_in_place("f", lambda c: col("fg", c), "xn")
            norm("e", lambda c: gn[:, 0, c:c + 1], shift=lambda c: modc[:, 0, c:c + 1])

            def rope(x, t, cos, sin, last):
                link(V.stream_shuffle(t, x, [(j + 16) % 32 for j in range(32)]))
                link(V.tensor_tensor(t, t, sin, ALU.mult))
                link(V.tensor_tensor(x, x, cos, ALU.mult))
                V.tensor_tensor(x, x, t, ALU.add).then_inc(*dve_did.up(last))

            for i in range(2):
                dve.wait_ge(*unit_done.at(UNIT[("ecq", i)]))
                V.tensor_copy(etmp[:, i, :], bank.of(("ecq", i))[:, :]).then_inc(*dve_did.up(("cqraw", i)))
            dve.wait_ge(*unit_done.at(UNIT[("eckv", 0)]))
            V.tensor_copy(etmp[:, 2, :], bank.of(("eckv", 0))[:, :]).then_inc(*dve_did.up("ckvraw"))
            dve.wait_ge(*pe_did.at(("qk", "sum", 4)))
            v, y, t = st40(EV), st40(EY), st40(ET)
            link(V.tensor_scalar(v, bank.of(("qk", "sum"))[:, 0:40], 1.0 / HD, EPS, ALU.mult, ALU.add))
            bank.freed(("qk", "sum"), dve_did, ("link", dve_did.n - 1))
            link(V.tensor_scalar(t.bitcast(I32), v.bitcast(I32), 1, None, ALU.logical_shift_right))
            link(V.tensor_scalar(y.bitcast(I32), t.bitcast(I32), -1.0, float(0x5f3759df), ALU.mult, ALU.add))
            for step in range(4):
                link(V.scalar_tensor_tensor(t, y, -0.5, y, ALU.mult, ALU.mult))
                link(V.tensor_tensor(t, t, v, ALU.mult))
                link(V.scalar_tensor_tensor(y, t, 1.5, y, ALU.add, ALU.mult))
            V.tensor_scalar(v, y, HD ** -0.5, None, ALU.mult).then_inc(*dve_did.up(("qk", "stat")))
            dve.wait_ge(*pe_did.at(("cq", "sum", 1)))
            rstd("cq", 8, 1.0 / 256)
            dve.wait_ge(*dve_did.at(("cq", "stat")))
            link(V.tensor_scalar(stat[:, 9, 0:TT], stat[:, 8, 0:TT], 96.0 ** -0.5, None, ALU.mult))
            dve.wait_ge(*pe_did.at(("ckv", "sum", 0)))
            rstd("ckv", 11, 1.0 / P)
            dve.wait_ge(*tabload.at("all"))
            for c in range(4):
                link(V.tensor_scalar(eq[:, c, :], eq[:, c, :], col("qn"), None, ALU.mult))
                if c == 0:
                    dve.wait_ge(*sq_ready.at(("ckv", 0)))
                    dve.wait_ge(*sq_ready.at(("qk", 3)))
                rope(eq[:, c, :], etmp[:, 0, :], cosA, sinA, ("eq", c))
                dve.wait_ge(*dve_did.at(("eq", c)))
            dve.wait_ge(*pe_did.at(("qk", "spread")))
            dve.wait_ge(*sq_ready.at(("qk", 4)))
            link(V.scalar_tensor_tensor(ek[:, :], ek[:, :], col("kn"), bank.of(("qk", "spread"))[:, :],
                                        ALU.mult, ALU.mult))
            bank.freed(("qk", "spread"), dve_did, ("link", dve_did.n - 1))
            rope(ek[:, :], etmp[:, 0, :], cosA, sinA, "ek")
            dve.wait_ge(*pe_did.at(("ckv", "spread")))
            V.tensor_tensor(eckv[:, :], eckv[:, :], bank.of(("ckv", "spread"))[:, :], ALU.mult)\
                .then_inc(*dve_did.up("ckv"))
            bank.freed(("ckv", "spread"), dve_did, "ckv")
            dve.wait_ge(*dve_did.at("ek"))
            rope(ekr[64:96, :], etmp[64:96, 0, :], cosT[64:96, :], sinT[64:96, :], "ekr")

            def gates(name, i, dst):
                dve.wait_ge(*act_did.at((name, i)))
                V.scalar_tensor_tensor(dst, dst, 1.0, bank.of((name, i))[:, :], ALU.add, ALU.mult)\
                    .then_inc(*dve_did.up(("g", name, i)))
                bank.freed((name, i), dve_did, ("g", name, i))

            for i in range(4):
                gates("ega", i, esg[:, i, :])
            dve.wait_ge(*dve_did.at(("g", "ega", 3)))

            def gated(phase, g):
                dve.wait_ge(*pe_did.at((phase, "oT", g)))
                c0, qt = {"A": (0, g), "B": (4, g), "C": (g % 2 * 4, g // 2)}[phase]
                sg, dst = (osg, otmp[:, 0, :]) if phase == "C" else (esg, etmp[:, g % 2, :])
                if phase == "B" and g >= 2:
                    dve.wait_ge(*dve_did.at(("B", "ylo", g - 2)))
                V.tensor_tensor(dst.rearrange("p (c t) -> p c t", c=4),
                                bank.of((phase, "oT", g))[:, :].rearrange("p (c t) -> p c t", c=4),
                                sg[:, c0:c0 + 4, qt * P:(qt + 1) * P], ALU.mult)\
                    .then_inc(*dve_did.up((phase, "gated", g)))
                bank.freed((phase, "oT", g), dve_did, (phase, "gated", g))

            def y_low(phase, g):
                dve.wait_ge(*act_did.at((phase, "yhi", g)))
                s, qt = {"A": (0, g), "B": (8, g), "C": (g % 2 * 8, g // 2)}[phase]
                src = otmp[:, 0, :] if phase == "C" else etmp[:, g % 2, :]
                V.scalar_tensor_tensor(ysplit[:, s + 4:s + 8, qt * P:(qt + 1) * P],
                                       src.rearrange("p (c t) -> p c t", c=4), 0.5,
                                       ysplit[:, s:s + 4, qt * P:(qt + 1) * P].bitcast(F32),
                                       ALU.mult, ALU.subtract).then_inc(*dve_did.up((phase, "ylo", g)))

            def row_scale(a):
                if a[0] == "A":
                    at = EV + a[1] * 10 + a[2] % 4 * 2 + a[2] // 4
                    return statf[:, at:at + 1]
                return stat[:, 9, a[2]:a[2] + 1]

            def attention(phase, events=None):
                tiles = tiles_of(phase)
                n = len(tiles)
                per = TT if phase == "B" else HEADS
                P_, PT_ = p_of(phase)
                for i in range(n + 6):
                    if i < n:
                        a = tiles[i]
                        k0, nk, x = geometry(a)[2:5]
                        dve.wait_ge(*s_done.at(a))
                        S = bank.of(("S", a))
                        if phase == "C":
                            if i >= 2:
                                dve.wait_ge(*pt_done.at(tiles[i - 2]))
                            h = a[1] % 2 * 8 + a[2]
                            j0 = (k0 - (a[1] // 2 - 1)) * P
                            V.tensor_tensor_reduce(P_[:, i % 2, 0:nk * P], S[:, 0:nk * P],
                                                   obias[:, h, j0:j0 + nk * P], -1.0, nsink[:, h:h + 1],
                                                   ALU.add, ALU.min, nmax[:, x:x + 1])\
                                .then_inc(*sm_ready.up(a))
                            bank.freed(("S", a), sm_ready, a)
                        else:
                            link(V.tensor_reduce(nmax[:, x:x + 1], S[:, :], AX_X, ALU.max, negate=True))
                            V.tensor_tensor(nmax[:, x:x + 1], nmax[:, x:x + 1], row_scale(a), ALU.mult)\
                                .then_inc(*sm_ready.up(a))
                    if phase == "C" and 1 <= i <= n:
                        a = tiles[i - 1]
                        nk = geometry(a)[3]
                        dve.wait_ge(*pt_done.at(a))
                        if i >= 3:
                            dve.wait_ge(*pv_done.at(tiles[i - 3]))
                        V.tensor_copy(PT_[:, (i - 1) % 2, 0:nk * P], bank.of(("T", a))[:, 0:nk * P])\
                            .then_inc(*dve_did.up(("PT", a)))
                        bank.freed(("T", a), dve_did, ("PT", a))
                    if phase == "C" and i >= 8 and i % 8 == 0 and i <= n:
                        g = i // 8 - 1
                        x = 64 + g * 8
                        dve.wait_ge(*sm_ready.at(tiles[8 * g + 7]))
                        V.tensor_tensor(esink[:, g * 8:g * 8 + 8], nmax[:, x:x + 8],
                                        col("sink", g % 2 * 8, 8), ALU.add).then_inc(*dve_did.up(("sink", g)))
                    j = i - 3
                    if 0 <= j < n and j % per == per - 1:
                        g = j // per
                        a = tiles[j]
                        x = geometry(a)[4] - per + 1
                        dve.wait_ge(*pv_done.at(a))
                        if phase == "C":
                            dve.wait_ge(*act_did.at(("esink", g)))
                            link(V.tensor_tensor(rsum[:, x:x + per], rsum[:, x:x + per],
                                                 esink[:, g * 8:g * 8 + 8], ALU.add))
                        link(V.reciprocal(rinv[:, x:x + per], rsum[:, x:x + per]))
                        O = bank.of(("O", phase, g))[:, 0:per * HD].rearrange("p (h e) -> p h e", h=per)
                        rb = rinv[:, x:x + per].unsqueeze(2).to_broadcast([P, per, HD])
                        if phase == "B":
                            V.tensor_tensor(btok[:, :, g * HD:(g + 1) * HD], O, rb, ALU.mult)\
                                .then_inc(*dve_did.up(("B", "head", g)))
                            bank.freed(("O", "B", g), dve_did, ("B", "head", g))
                        else:
                            dst = ootile if phase == "C" else eotile
                            if g:
                                dve.wait_ge(*pe_did.at((phase, "oT", g - 1)))
                            V.tensor_tensor(dst.rearrange("p (h e) -> p h e", h=8), O, rb, ALU.mult)\
                                .then_inc(*dve_did.up((phase, "o", g)))
                            bank.freed(("O", phase, g), dve_did, (phase, "o", g))
                    if phase != "B" and i >= 11 and (i - 11) % 8 == 0:
                        gated(phase, (i - 11) // 8)
                    if phase != "B" and i >= 13 and (i - 13) % 8 == 0:
                        y_low(phase, (i - 13) // 8)
                    if events and i in events:
                        events[i]()

            gb = lambda i: (lambda: gates("egb", i, esg[:, 4 + i, :]))
            attention("A", {11: gb(0), 19: gb(1), 27: gb(2), 35: gb(3)})

            dve.wait_ge(*unit_done.at(UNIT[("egb", 3)]))
            dve.wait_ge(*dve_did.at("ekr"))
            for slot in range(2):
                link(V.tensor_copy(KF[64:96, slot, :], ekr[64:96, :]))

            def head_rope(h):
                dve.wait_ge(*act_did.at(("QF", h)))
                rope(QF[64:96, h % 2, :], etmp[64:96, 2, :], cosT[64:96, :], sinT[64:96, :], ("QF", h))
                dve.wait_ge(*dve_did.at(("QF", h)))

            head_rope(0)
            attention("B", {4 * h - 1: (lambda h=h: head_rope(h)) for h in range(1, HEADS)})
            dve.wait_ge(*dve_did.at(("B", "head", HEADS - 1)))
            for g in range(TT):
                found[("dve_did", ("B", "o", g))] = dve_did.n
            for g in range(TT + 1):
                if g < TT:
                    gated("B", g)
                if g >= 1:
                    y_low("B", g - 1)
            for k in range(DC):
                found[("dve_did", ("ey", k))] = dve_did.n

            def residual(name, i, layer, key):
                dve.wait_ge(*unit_done.at(UNIT[(name, i)]))
                V.scalar_tensor_tensor(xT[:, i, :], bank.of((name, i))[:, :], modc[:, layer, 2 * DC + i:2 * DC + i + 1],
                                       xT[:, i, :], ALU.mult, ALU.add).then_inc(*dve_did.up((key, i)))
                bank.freed((name, i), dve_did, (key, i))

            for i in range(DC):
                residual("eout", i, 0, "x3")
            norm("o", lambda c: gn[:, 1, c:c + 1], shift=lambda c: modc[:, 1, c:c + 1])
            link(V.tensor_scalar(nsink[:, :], col("sink", 0, C_HEADS), -1.0, None, ALU.mult))
            for i in range(DC):
                gates("og", i, osg[:, i, :])
            dve.wait_ge(*act_did.at(("obias", C_HEADS - 1)))
            attention("C")
            for k in range(DC):
                found[("dve_did", ("oy", k))] = dve_did.n
            for i in range(DC):
                residual("oout", i, 1, "x4")
            norm_in_place("z", lambda c: col("fn", c), "res")
    return found


def kernel(**inputs):
    import concourse.bacc as bacc
    from concourse.bass_utils import run_bass_kernel_spmd

    a = {k: np.asarray(v) for k, v in inputs.items()}
    zeros = np.zeros

    def cat(*blocks):
        return np.concatenate(blocks, axis=1)

    w_in = a["w_in"][0]
    at = np.cumsum([0, 512, 128, 128, 128, 128, 128, 128, 24, 1024, 2048])
    col = lambda w, start, n=P: w[:, start:start + n]
    pair = lambda w, start, h0, h1: cat(col(w, start + h0 * HD, HD), col(w, start + h1 * HD, HD))
    up, down = a["ffn_w_up"][0], a["ffn_w_down"][0]
    even, odd = a["even_w_in_2"][0], a["odd_w_in_2"][0]
    eo = np.cumsum([0, 512, 128, 128, 512, 256, 128, 32, 512])
    parts = {
        "conv": lambda i: col(w_in, at[8] + (i % 2) * CONV_CH + i // 2 * P),
        "tok": lambda i: col(w_in, at[4]) if i == 0 else col(w_in, at[6]) if i == 1
        else cat(col(w_in, at[7], 24), zeros((D, P - 24), np.float32)),
        "q": lambda i: pair(w_in, 0, i, i + 4),
        "k": lambda i: col(w_in, (at[3], at[5], at[1], at[2])[i]),
        "ga": lambda i: col(w_in, at[9] + i * P),
        "gb": lambda i: col(w_in, at[9] + D + i * P),
        "y": lambda i: np.concatenate([col(a["w_attn_br"][0], i * P), col(a["w_conv_br"][0], i * P)]),
        "wout": lambda i: col(a["w_out"][0], i * P),
        "up": lambda i: col(up, order_up(i) * P),
        "ecq": lambda i: col(even, eo[4] + i * P),
        "eckv": lambda i: col(even, eo[5]),
        "ekr": lambda i: cat(zeros((D, 64), np.float32), col(even, eo[6], 32), zeros((D, 32), np.float32)),
        "eq": lambda i: pair(even, 0, i, i + 4),
        "ek": lambda i: col(even, eo[1]),
        "ev": lambda i: col(even, eo[2]),
        "ega": lambda i: col(even, eo[3] + i * P),
        "egb": lambda i: col(even, eo[7] + i * P),
        "eout": lambda i: col(a["even_w_out_2"][0], i * P),
        "oq": lambda i: pair(odd, 0, i // 4 * 8 + i % 4, i // 4 * 8 + i % 4 + 4),
        "ok": lambda i: col(odd, 1024 + i * P),
        "ov": lambda i: col(odd, 1280 + i * P),
        "og": lambda i: col(odd, 1536 + i * P),
        "oout": lambda i: col(a["odd_w_out_2"][0], i * P),
    }
    w = np.empty((NU, P, D), np.float32)
    for n, (name, i) in enumerate(UNITS):
        if name == "down":
            w[n] = down[i * P:(i + 1) * P]
        else:
            w[n] = parts[name](i).reshape(DC, P, P).transpose(1, 0, 2).reshape(P, D)

    vec = lambda v: v.reshape(-1, P).T
    twice = lambda v: np.concatenate([v, v], axis=0)
    c = np.zeros((P, NCOLS), np.float32)
    for name, value in {
        "n1g": vec(a["norm1_g"][0]), "n2g": vec(a["norm2_g"][0]), "fg": vec(a["final_g"]),
        "dwb": vec(a["conv_dw_b"][0]), "lng": vec(a["conv_ln_g"][0]), "lnb": vec(a["conv_ln_b"][0]),
        "dww": a["conv_dw_w"][0].T.reshape(CC, P, TAPS).transpose(1, 0, 2).reshape(P, -1),
        "ffw": a["ffn_dw_w"][0].T.reshape(2 * FC, P, 3).transpose(1, 0, 2).reshape(P, -1),
        "ffb": vec(a["ffn_dw_b"][0]),
        "pek": twice(a["cmp_pe_k"][0].T), "pev": twice(a["cmp_pe_v"][0].T),
        "rowvalid": (np.arange(P) >= CMP_BLOCK - 1).astype(np.float32)[:, None],
        "nw": cat(vec(a["norm_w_2"][0]), vec(a["norm_w_2"][1])),
        "adab": cat(vec(a["ada_b_2"][0]), vec(a["ada_b_2"][1])),
        "c": vec(a["c_2"][0]),
        "qn": twice(a["a_q_norm_2"][0][:, None]), "kn": twice(a["a_k_norm_2"][0][:, None]),
        "cqg": vec(a["b_q_lora_norm_2"][0]), "ckvg": vec(a["b_kv_lora_norm_2"][0]),
        "fn": vec(a["final_norm_2"]),
        "sink": np.broadcast_to(a["c_sink_2"][0][None, :], (P, C_HEADS)),
    }.items():
        s, n = COLS[name]
        c[:, s:s + n] = value

    p = np.arange(P)[:, None]
    j = np.arange(T)[None, :] - (T - P)
    dist = np.where(j <= p, j - p, NEG).astype(np.float32)
    t = (np.arange(TT)[None, :, None] * P + p[:, :, None])
    end = np.arange(NCP)[None, None, :] * CMP_STRIDE + CMP_BLOCK - 1
    distc = np.where((t >= end) & (np.arange(NCP) < NCMP)[None, None, :], end - t, NEG)\
        .astype(np.float32).reshape(P, TT * NCP)
    w1 = np.stack([twice(a[k][0].reshape(CMP_BLOCK, HD, P).transpose(1, 0, 2).reshape(HD, -1))
                   for k in ("cmp_k_w1", "cmp_v_w1")])
    w2 = np.stack([a["cmp_k_w2"][0], a["cmp_v_w2"][0]])
    ada = a["ada_w_2"].reshape(2, DC, P, 3 * DC, P).transpose(0, 3, 2, 1, 4).reshape(6 * DC, P, D)
    j = np.arange(3 * P)[None, :] - P
    distC = np.where(np.abs(j - p) <= WIN, -np.abs(j - p), NEG).astype(np.float32)
    half = np.arange(P)[:, None] % 32
    inv = (np.float32(ROPE_THETA) ** (-(2 * (half % 16)).astype(np.float32) / np.float32(32))).astype(np.float32)
    tok = np.arange(T)[None, :]
    axial = np.where(np.arange(P)[:, None] % 64 < 32, tok // 64, tok % 64).astype(np.float32)
    sign = np.where(half < 16, -1, 1).astype(np.float32)
    angA, angT = axial * inv, tok.astype(np.float32) * inv
    cosA, sinA = np.cos(angA), np.sin(angA) * sign
    cosT, sinT = np.cos(angT), np.sin(angT) * sign
    arrays = {
        "xT": np.ascontiguousarray(a["x"][0].T).reshape(DC, P, T), "w": w, "cols": c, "dist": dist,
        "distc": distc, "w1": w1, "w2": w2, "ada": ada, "distC": distC,
        "cosA": cosA, "sinA": sinA, "cosT": cosT, "sinT": sinT,
        "uq": a["b_w_uq_2"][0].reshape(2, P, HEADS * 96).transpose(1, 0, 2).reshape(P, -1),
        "uk": a["b_w_uk_2"][0].reshape(P, -1), "uv": a["b_w_uv_2"][0].reshape(P, -1),
    }
    arrays = {k: np.ascontiguousarray(v) for k, v in arrays.items()}

    def build(known):
        nc = bacc.Bacc("TRN2", target_bir_lowering=False, num_devices=1)
        d = {k: nc.dram_tensor(f"in_{k}", v.shape, F32, kind="ExternalInput").ap() for k, v in arrays.items()}
        out = nc.dram_tensor("out_t", (DC, P, T), F32, kind="ExternalOutput").ap()
        return nc, program(nc, d, out, known)

    _, known = build({})
    nc, again = build(known)
    assert again == known
    r = run_bass_kernel_spmd(nc, [{f"in_{k}": v for k, v in arrays.items()}], core_ids=[0])
    return np.ascontiguousarray(r.results[0]["out_t"].reshape(D, T).T)[None]
```

```python
from contextlib import ExitStack

import numpy as np

import concourse.bass as bass
from concourse import mybir

F32 = mybir.dt.float32
F32R = mybir.dt.float32r
I32 = mybir.dt.int32
ACT = mybir.ActivationFunctionType
ALU = mybir.AluOpType
AX_X = mybir.AxisListType.X

P = 128
T = 512
TT = T // P
D = 1024
DC = D // P
EPS = 1e-6
NEG = -1.0e30
HEADS = 8
HD = 64
CMP_BLOCK, CMP_STRIDE = 32, 16
NCMP = (T - CMP_BLOCK) // CMP_STRIDE + 1
NCP = 32
TAPS = 31
CONV_CH = 512
CC = CONV_CH // P
FFN = 2816
FC = FFN // P
WIN = 128
C_HEADS = 16
ROPE_THETA = 10000.0

UNITS = (
    [("conv", i) for i in range(2 * CC)]
    + [("tok", i) for i in range(3)]
    + [("q", i) for i in range(4)]
    + [("k", i) for i in range(4)]
    + [("ga", i) for i in range(DC)]
    + [u for i in range(DC) for u in (("gb", i), ("y", i))]
    + [("wout", i) for i in range(DC)]
    + [("up", i) for i in range(2 * FC)]
    + [("down", i) for i in range(FC)]
    + [("ecq", 0), ("ecq", 1), ("eckv", 0), ("ekr", 0)]
    + [("eq", i) for i in range(4)] + [("ek", 0), ("ev", 0)]
    + [("ega", i) for i in range(4)] + [("egb", i) for i in range(4)]
    + [("eout", i) for i in range(DC)]
    + [("oq", i) for i in range(DC)] + [("ok", i) for i in range(2)] + [("ov", i) for i in range(2)]
    + [("og", i) for i in range(DC)]
    + [("oout", i) for i in range(DC)]
)
UNIT = {u: n for n, u in enumerate(UNITS)}
NU = len(UNITS)
WS = 5

COLS = {}
_n = 0
for _name, _w in (
    ("n1g", DC), ("n2g", DC), ("fg", DC), ("dwb", CC), ("lng", CC), ("lnb", CC),
    ("dww", CC * TAPS), ("ffw", 2 * FC * 3), ("ffb", 2 * FC), ("pek", CMP_BLOCK), ("pev", CMP_BLOCK),
    ("rowvalid", 1), ("nw", 2 * DC), ("adab", 2 * 3 * DC), ("qn", 1), ("kn", 1),
    ("cqg", 2), ("ckvg", 1), ("fn", DC), ("sink", C_HEADS),
):
    COLS[_name] = (_n, _w)
    _n += _w
NCOLS = _n


VB_AT = 29
GA_STEPS = 11


def order_up(i):
    return i // 2 + (i % 2) * FC


class Signal:

    def __init__(self, sem, name, known, found):
        self.sem, self.name, self.known, self.found, self.n = sem, name, known, found, 0

    def up(self, key, by=1):
        self.n += by
        self.found[(self.name, key)] = self.n
        return self.sem, by

    def at(self, key):
        return self.sem, self.known.get((self.name, key), 1)


class Banks:

    def __init__(self, tiles, signals, known, found):
        self.tiles, self.signals, self.known, self.found = tiles, signals, known, found
        self.last, self.turn = {}, {}

    def take(self, pe, pool, key):
        n = self.turn.get(pool, 0)
        self.turn[pool] = n + 1
        b = pool[n % len(pool)]
        if b in self.last:
            name, step = self.known.get(("freed", self.last[b]), ("sq_ready", "x"))
            pe.wait_ge(*self.signals[name].at(step))
        self.last[b] = key
        self.found[("bank", key)] = b
        return self.tiles[b]

    def of(self, key):
        return self.tiles[self.known.get(("bank", key), 0)]

    def freed(self, key, signal, step):
        self.found[("freed", key)] = (signal.name, step)


LIN, SC, TR, OB = (0, 1), (2, 3), (4, 5), (6, 7)
WIDE = LIN + SC


def program(nc, d, out, known):
    found = {}
    ctx = ExitStack()
    with ctx:
        def sb(name, cols, dt=F32):
            return ctx.enter_context(nc.sbuf_tensor(name, [P] + list(cols), dt))

        signals = {}

        def signal(name):
            signals[name] = Signal(ctx.enter_context(nc.semaphore(name)), name, known, found)
            return signals[name]

        bank = Banks([ctx.enter_context(nc.psum_tensor(f"bank{b}", [P, 512], F32)) for b in range(8)],
                     signals, known, found)

        with nc.sbuf_tensor("h_first", [P, 16 * T], F32) as h_use:
            pass
        hhi, hlo = sb("hhi", [DC, T], F32R), sb("hlo", [DC, T], F32R)
        ZW = TAPS - 1 + T
        with nc.sbuf_tensor("first", [P, 16 * T], F32) as first_use:
            pass
        ysplit = sb("ysplit", [16, T], F32R)
        z = first_use[:, 8 * T:8 * T + CC * ZW].rearrange("p (c t) -> p c t", c=CC)
        ctap = first_use[:, 8 * T + CC * ZW:8 * T + CC * ZW + CC * TAPS].rearrange("p (c n) -> p c n", c=CC)

        def yhi(k):
            return ysplit[:, k // 4 * 8 + k % 4, :]

        def ylo(k):
            return ysplit[:, k // 4 * 8 + 4 + k % 4, :]

        whi = sb("whi", [WS, D], F32R)
        with nc.sbuf_tensor("raw", [P, WS, D], F32) as raw:
            pass
        wlo = sb("wlo", [WS, D], F32R)
        ident, ones = sb("ident", [P]), sb("ones", [2])
        cols = sb("cols", [NCOLS])
        stat = sb("stat", [24, 16])
        nmax, rsum, rinv = sb("nmax", [192]), sb("rsum", [192]), sb("rinv", [192])
        XB, AB = DC * T, 17920
        xbuf = sb("xbuf", [XB])
        arena = sb("arena", [AB])
        xT = xbuf[:].rearrange("p (c t) -> p c t", c=DC)

        place = [0]

        def area(n, at=None):
            if at is not None:
                place[0] = at
            a = place[0]
            place[0] += n
            assert place[0] <= AB, place[0]
            return arena[:, a:a + n]

        def col(name, i=0, n=1):
            return cols[:, COLS[name][0] + i:COLS[name][0] + i + n]

        def chunks(ap, c):
            return ap.rearrange("p (c t) -> p c t", c=c)

        qT = chunks(area(4 * T, 0), 4)
        kv = chunks(area(4 * T), 4)
        vtok = area(TT * 256).rearrange("p (t n) -> p t n", t=TT)
        gate3 = area(TT * 24).rearrange("p (t n) -> p t n", t=TT)
        cacc = chunks(area(CC * T), CC)
        dist = area(T)
        distc = area(TT * NCP)
        biasc = area(TT * HEADS * NCP).rearrange("p (t h n) -> p t h n", t=TT, h=HEADS)
        kcmp = area(2 * NCP)[:, 0:NCP]
        vblk = area(2 * 256).rearrange("p (g n) -> p g n", g=2)
        w2k, w2v = area(HD), area(HD)
        w1_at = place[0]
        bias = chunks(area(HEADS * T), HEADS)
        ptile = chunks(area(2 * T), 2)
        pslots = [ptile[:, 0, :], ptile[:, 1, :], kv[:, 2, :]]
        pttile = chunks(area(2 * T), 2)
        otile = area(T)
        tmp = chunks(area(2 * T), 2)
        hs = sb("hs", [2, T])
        w1v = xbuf[:].rearrange("p (j m) -> p j m", j=CMP_BLOCK)
        w1k = arena[:, w1_at:w1_at + CMP_BLOCK * P].rearrange("p (j m) -> p j m", j=CMP_BLOCK)
        blk_at = w1_at + CMP_BLOCK * P
        blk = arena[:, blk_at:blk_at + 2 * CMP_BLOCK * 2 * NCMP].rearrange(
            "p (v j g n) -> p v j g n", v=2, j=CMP_BLOCK, g=2)
        assert blk_at + 2 * CMP_BLOCK * 2 * NCMP <= AB
        gel = hs[:, 0:1, :]
        hidk = tmp[:, 0, 0:64].rearrange("p (g n) -> p g n", g=2)
        hidv = tmp[:, 0, 128:384].rearrange("p (g r n) -> p g r n", g=2, r=4)

        def tokbuf(i):
            return tmp[:, i, :] if i < 2 else otile
        merged = xT
        fa = chunks(area(FC * T, 0), FC)
        ua = chunks(area(4 * T), 4)
        ft = chunks(area(2 * T), 2)
        ada = area(2 * D).rearrange("p (s n) -> p s n", s=2)
        cact = area(D)
        sqt = sb("sqt", [2, T])
        modc = sb("modc", [2, 3 * DC])

        statf = stat[:].rearrange("p a b -> p (a b)")
        EY, EV, ET = 256, 296, 336
        def st40(at):
            return statf[:, at:at + 40]
        eq = chunks(area(4 * T, 0), 4)
        btok = eq
        ek = area(T)
        ev = area(TT * P).rearrange("p (t n) -> p t n", t=TT)
        ecq = chunks(area(2 * T), 2)
        eckv, ekr = area(T), area(T)
        esg = chunks(area(8 * T), 8)
        cosT, sinT = area(T), area(T)
        eotile = area(T)
        etmp = chunks(area(3 * T), 3)
        p2 = chunks(area(3 * T), 3)
        pt2 = chunks(area(2 * T), 2)
        late = first_use[:, 8 * T:16 * T]
        cosA, sinA = late[:, 0:T], late[:, T:2 * T]
        uq = late[:, 2 * T:2 * T + 1536].rearrange("p (k h m) -> p k h m", k=2, h=8)
        uk, uv = late[:, 2 * T + 1536:3 * T + 1536], late[:, 3 * T + 1536:4 * T + 1536]
        vB = chunks(h_use[:, 0:4 * T], 4)
        QF = chunks(h_use[:, 4 * T:6 * T], 2)
        KF = chunks(h_use[:, 6 * T:8 * T], 2)
        oq = chunks(area(8 * T, 0), 8)
        ok = chunks(area(2 * T), 2)
        ov = area(TT * 256).rearrange("p (t n) -> p t n", t=TT)
        osg = chunks(area(8 * T), 8)
        ootile = area(T)
        otmp = chunks(area(2 * T), 2)
        p3 = chunks(area(3 * T), 3)
        pt3 = chunks(area(2 * T), 2)
        distC = area(3 * P)
        nsink = area(C_HEADS)
        esink = area(C_HEADS * TT)
        obias0, obias1 = chunks(area(8 * 3 * P), 8), chunks(h_use[:, 0:8 * 3 * P], 8)
        obias = [obias0[:, h, :] for h in range(8)] + [obias1[:, h, :] for h in range(8)]
        sel2 = sb("sel2", [2])
        gn, fgn = sb("gn", [2, DC]), sb("fgn", [DC])

        loaded = signal("loaded")
        landed = [signal(f"landed{r}") for r in range(WS)]
        w_hi = signal("w_hi")
        w_split = signal("w_split")
        unit_done = signal("unit_done")
        pe_did = signal("pe_did")
        s_done = signal("s_done")
        pt_done = signal("pt_done")
        pv_done = signal("pv_done")
        sq_ready = signal("sq_ready")
        act_did = signal("act_did")
        p_ready = signal("p_ready")
        ptc = signal("ptc")
        dve_did = signal("dve_did")
        sm_ready = signal("sm_ready")
        pool_did = signal("pool_did")
        stored = signal("stored")
        xload = [signal(f"xload{c}") for c in range(DC)]
        tables_load = signal("tables_load")
        w1load = signal("w1load")
        w1v_load = signal("w1v_load")
        block = ctx.enter_context(nc.Block())

        c_load = signal("cload")
        adaload = [signal(f"adaload{i}") for i in range(2)]
        tabload = signal("tabload")

        def tiles_of(phase):
            groups, per = {"A": (TT, HEADS), "B": (HEADS, TT), "C": (2 * TT, HEADS)}[phase]
            return [(phase, g, u) for g in range(groups) for u in range(per)]

        def geometry(tile):
            phase, g, u = tile
            if phase == "A":
                half = 64 * (u // 4)
                return eq[half:half + 64, u % 4, g * P:(g + 1) * P], ek[half:half + 64, :], 0, TT, g * 8 + u
            if phase == "B":
                return QF[0:96, g % 2, u * P:(u + 1) * P], KF[0:96, g % 2, :], 0, TT, 32 + g * 4 + u
            qt, h = g // 2, g % 2 * 8 + u
            half = 64 * (h // 4 % 2)
            k0, k1 = max(qt - 1, 0), min(qt + 1, TT - 1)
            return (oq[half:half + 64, h // 8 * 4 + h % 4, qt * P:(qt + 1) * P],
                    ok[half:half + 64, h // 8, k0 * P:(k1 + 1) * P], k0, k1 - k0 + 1, 64 + g * 8 + u)

        def values(tile, k):
            phase, g, u = tile
            if phase == "A":
                return ev[:, k, u // 4 * HD:(u // 4 + 1) * HD]
            if phase == "B":
                return vB[:, k, g * HD:(g + 1) * HD]
            h = g % 2 * 8 + u
            return ov[:, k, h // 4 * HD:(h // 4 + 1) * HD]

        def p_of(phase):
            return (p3, pt3) if phase == "C" else (p2, pt2)

        nsa = []
        for qt in range(TT):
            nsa.append(("cmp", qt, 0))
            for br in range(2):
                nsa += [("nsa", qt, br * HEADS + h) for h in range(HEADS)]

        @block.tensor
        def _(pe):
            mm = nc.tensor.matmul

            def h_parts(k):
                return hhi[:, k, :], hlo[:, k, :]

            def y_parts(k):
                return yhi(k), ylo(k)

            def unit(name, i, src=h_parts, first=None, inline=True, pool=WIDE):
                u = UNIT[(name, i)]
                s = u % WS
                state = {}

                def piece(k):
                    if k == 0:
                        pe.wait_ge(w_split.sem, u + 1)
                        state["b"] = bank.take(pe, pool, (name, i))
                    if first:
                        pe.wait_ge(*first(k))
                    b = state["b"]
                    hi, lo = src(k)
                    for part, (w, x) in enumerate(((whi, hi), (whi, lo), (wlo, hi))):
                        m = mm(b[:, :], w[:, s, k * P:(k + 1) * P], x,
                               start=(k == 0 and part == 0), stop=(k == DC - 1 and part == 2))
                    if k == DC - 1:
                        m.then_inc(*unit_done.up(u))
                if inline:
                    for k in range(DC):
                        piece(k)
                return piece

            def turn_unit(name, i, src):
                pe.wait_ge(*act_did.at((name, i, "copy")))
                b = bank.take(pe, TR, (name, i, "T"))
                for tt in range(TT):
                    m = nc.tensor.transpose(b[:, tt * P:(tt + 1) * P], src[:, tt * P:(tt + 1) * P], ident[:, :])
                m.then_inc(*pe_did.up((name, i, "T")))

            def sums(name, c, n, src=None, ready=None, pool=TR):
                pe.wait_ge(*(ready(c) if ready else sq_ready.at((name, c))))
                if c == 0:
                    bank.take(pe, pool, (name, "sum"))
                b = bank.tiles[found[("bank", (name, "sum"))]]
                x = src[:, c, :] if src is not None else sqt[:, known.get(("sqslot", (name, c)), 0), :]
                for tt in range(TT):
                    m = mm(b[:, tt:tt + 1], x[:, tt * P:(tt + 1) * P], ones[:, 0:1],
                           start=(c == 0 and tt == 0), stop=(c == n - 1), skip_group_check=True)
                m.then_inc(*pe_did.up((name, "sum", c)))

            def stats(name, n, src=None, ready=None, pool=TR):
                for c in range(n):
                    sums(name, c, n, src, ready, pool)

            def layer_out(norm_name, i):
                if i:
                    sums(norm_name, i - 1, DC)
                if i == DC - 1:
                    sums(norm_name, i, DC)

            def spread(name, c0, pool=TR, at=0):
                pe.wait_ge(*dve_did.at((name, "stat")))
                b = bank.take(pe, pool, (name, "spread"))
                for tt in range(TT):
                    m = mm(b[:, tt * P:(tt + 1) * P], stat[:, c0, at + tt:at + tt + 1].to_broadcast([P, P]),
                           ident[:, :], start=True, stop=True)
                m.then_inc(*pe_did.up((name, "spread")))

            def norm(name, c0=0):
                stats(name, DC)
                spread(name, c0)

            def att_scores(a):
                kind, qt, j = a
                b = bank.take(pe, SC, ("S", a))
                if kind == "cmp":
                    for h in range(HEADS):
                        g = h // 4
                        if h == 4:
                            b = bank.take(pe, SC, ("S2", a))
                        m = mm(b[:, h % 4 * NCP:(h % 4 + 1) * NCP], qT[64 * g:64 * g + 64, h % 4, qt * P:(qt + 1) * P],
                               kcmp[64 * g:64 * g + 64, :], start=True, stop=True)
                else:
                    br, h = j // HEADS, j % HEADS
                    g = h // 4
                    L = (qt + 1) * P
                    m = mm(b[:, 0:L], qT[64 * g:64 * g + 64, h % 4, qt * P:(qt + 1) * P],
                           kv[64 * g:64 * g + 64, br, 0:L], start=True, stop=True)
                m.then_inc(*s_done.up(a))

            def att_turn(a, n):
                kind, qt, j = a
                pe.wait_ge(*p_ready.at(a))
                b = bank.take(pe, TR, ("T", a))
                for k in range(n):
                    m = nc.tensor.transpose(b[:, k * P:(k + 1) * P],
                                            pslots[nsa.index(a) % 3][:, k * P:(k + 1) * P], ident[:, :])
                m.then_inc(*pt_done.up(a))

            def att_pv(a, n, key, h, first, rhs, width=HD):
                pe.wait_ge(*ptc.at(a))
                if first:
                    bank.take(pe, OB, key)
                b = bank.tiles[found[("bank", key)]]
                s = nsa.index(a) % 2
                for k in range(n):
                    m = mm(b[:, h * width:(h + 1) * width], pttile[:, s, k * P:(k + 1) * P], rhs(k),
                           start=(first and k == 0), stop=(k == n - 1), skip_group_check=True)
                m.then_inc(*pv_done.up(a))

            def nsa_turn(a):
                att_turn(a, 2 if a[0] == "cmp" else a[1] + 1)

            def nsa_pv(a):
                kind, qt, j = a
                if kind == "cmp":
                    pe.wait_ge(*ptc.at(a))
                    b = bank.take(pe, OB, ("O", qt, 0))
                    s = nsa.index(a) % 2
                    for g in range(2):
                        m = mm(b[:, g * 256:(g + 1) * 256], pttile[:, s, g * P:(g + 1) * P], vblk[:, g, :],
                               start=True, stop=True)
                    m.then_inc(*pv_done.up(a))
                else:
                    br, h = j // HEADS, j % HEADS
                    att_pv(a, qt + 1, ("O", qt, 1 + br), h, h == 0,
                           lambda k: vtok[:, k, br * P + (h // 4) * HD:br * P + (h // 4) * HD + HD])

            def turn_o(phase, qt, n=4):
                for half in range(n // 4):
                    pe.wait_ge(*dve_did.at((phase, "o", qt)))
                    b = bank.take(pe, TR, (phase, "oT", qt, half))
                    for c in range(4):
                        m = nc.tensor.transpose(b[:, c * P:(c + 1) * P],
                                                otile[:, (half * 4 + c) * P:(half * 4 + c + 1) * P],
                                                ident[:, :])
                    m.then_inc(*pe_did.up((phase, "oT", qt, half)))

            pe.wait_ge(*pool_did.at("const"))
            norm("n1")
            for i in range(2 * CC):
                unit("conv", i, first=(lambda k: dve_did.at(("n1", "h", k))) if i == 0 else None)
            for i in range(3):
                unit("tok", i)
                if i:
                    turn_unit("tok", i - 1, tokbuf(i - 1))
            for i in range(4):
                unit("q", i)
                if i == 0:
                    turn_unit("tok", 2, tokbuf(2))
            for i in range(4):
                unit("k", i)
            hb = bank.take(pe, TR, "hid")
            for v in range(2):
                pe.wait_ge(*(w1load, w1v_load)[v].at(("w1", v)))
                pe.wait_ge(*dve_did.at(("blk", v)))
                w1 = w1k if v == 0 else w1v
                for j in range(CMP_BLOCK):
                    m = mm(hb[:, v * 64:v * 64 + 2 * NCMP], w1[:, j, :],
                           blk[:, v, j, :, :].rearrange("p g n -> p (g n)"),
                           start=(j == 0), stop=(j == CMP_BLOCK - 1))
            m.then_inc(*pe_did.up("hid"))
            unit("ga", 0)
            pe.wait_ge(*dve_did.at("hid"))
            pe.wait_ge(*tables_load.at("dist"))
            b = bank.take(pe, TR, "cmp2")
            for g in range(2):
                mm(b[64 * g:64 * g + 64, 0:NCMP], w2k[:, :], hidk[:, g, 0:NCMP], start=True, stop=True)
            for g in range(2):
                m = mm(b[:, 64 + g * HD:64 + (g + 1) * HD],
                       tmp[:, 0, 128 + g * P:128 + (g + 1) * P], w2v[:, :], start=True, stop=True)
            m.then_inc(*pe_did.up("cmp2"))
            unit("ga", 1)
            pe.wait_ge(*dve_did.at("cmp2"))
            pieces = {}
            for i in range(2, DC):
                part = unit("ga", i, inline=False, pool=(0,))
                for k in range(DC):
                    pieces[GA_STEPS * (i - 2) + k] = (part, k)
            n = len(nsa)
            for i in range(n + 3):
                if i < n:
                    att_scores(nsa[i])
                if 0 <= i - 2 < n:
                    nsa_turn(nsa[i - 2])
                if i >= 3:
                    nsa_pv(nsa[i - 3])
                if i in pieces:
                    f, k = pieces[i]
                    f(k)
                if i >= 21 and (i - 21) % 17 == 0 and i < n:
                    turn_o("nsa", (i - 21) // 17)
                if i == 26:
                    stats("mu", CC, src=cacc, ready=lambda c: dve_did.at(("conv", c)), pool=(1,))
                if i == 29:
                    spread("mu", 2, pool=(1,))
                if 35 <= i < 35 + CC:
                    sums("var", i - 35, CC, pool=(1,))
                if i == 42:
                    spread("var", 4, pool=(1,))
            turn_o("nsa", TT - 1)
            for i in range(DC):
                unit("gb", i)
                u = UNIT[("y", i)]
                pe.wait_ge(w_split.sem, u + 1)
                for half, pool in ((0, SC), (1, OB)):
                    if i == 0:
                        for c in range(4):
                            pe.wait_ge(*dve_did.at(("y", 4 * half + c)))
                    b = bank.take(pe, pool, ("y", i, half))
                    for k in range(4):
                        kk = 4 * half + k
                        for part, (w, x) in enumerate(((whi, yhi(kk)), (whi, ylo(kk)), (wlo, yhi(kk)))):
                            m = mm(b[:, :], w[:, u % WS, kk * P:(kk + 1) * P], x,
                                   start=(k == 0 and part == 0), stop=(k == 3 and part == 2))
                m.then_inc(*unit_done.up(u))
            for i in range(DC):
                unit("wout", i, first=(lambda k: dve_did.at(("m", k))) if i == 0 else None)
                layer_out("n2", i)
            spread("n2", 0)
            for i in range(2 * FC):
                unit("up", i, first=(lambda k: dve_did.at(("n2", "h", k))) if i == 0 else None)
            def down_block(i, n):
                b = bank.tiles[n]
                u = UNIT[("down", i)]
                hi, lo = y_parts(i % DC)
                for part, (w, x) in enumerate(((whi, hi), (whi, lo), (wlo, hi))):
                    m = mm(b[:, :], w[:, u % WS, n * P:(n + 1) * P], x,
                           start=(i == 0 and part == 0), stop=(i == FC - 1 and part == 2))
                return m

            LATE = FC - 4
            for i in range(FC):
                u = UNIT[("down", i)]
                pe.wait_ge(w_split.sem, u + 1)
                pe.wait_ge(*dve_did.at(("fa", i)))
                for n in range(DC if i < LATE else 0):
                    if i == 0:
                        bank.take(pe, (n,), ("down", n))
                    m = down_block(i, n)
                if i < LATE:
                    m.then_inc(*unit_done.up(u))

            def double_sums(c):
                if c == 0:
                    bank.take(pe, (0,), ("fe", "sum"))
                b = bank.tiles[0]
                for half, name in enumerate(("f", "e")):
                    pe.wait_ge(*sq_ready.at((name, c)))
                    for tt in range(TT):
                        m = mm(b[:, half * TT + tt:half * TT + tt + 1],
                               sqt[:, known.get(("sqslot", (name, c)), 0), tt * P:(tt + 1) * P], ones[:, 0:1],
                               start=(c == 0 and half == 0 and tt == 0), stop=(c == DC - 1),
                               skip_group_check=True)
                    m.then_inc(*pe_did.up((name, "sum", c)))

            for n in range(DC):
                for i in range(LATE, FC):
                    m = down_block(i, n)
                    if n == DC - 1:
                        m.then_inc(*unit_done.up(UNIT[("down", i)]))
                    elif i == FC - 1:
                        m.then_inc(*pe_did.up(("down", n)))
                if n >= 2:
                    double_sums(n - 2)
            for c in range(DC - 2, DC):
                double_sums(c)

            spread("e", 0, at=TT)
            spread("f", 0)

            def attention(phase, filler=None, events=None):
                tiles = tiles_of(phase)
                n = len(tiles)
                P_, PT_ = p_of(phase)
                for i in range(n + 4):
                    if i < n:
                        q, k, k0, nk, x = geometry(tiles[i])
                        if phase == "B" and tiles[i][2] == 0:
                            pe.wait_ge(*dve_did.at(("QF", tiles[i][1])))
                        b = bank.take(pe, SC, ("S", tiles[i]))
                        mm(b[:, 0:nk * P], q, k, start=True, stop=True).then_inc(*s_done.up(tiles[i]))
                    if 2 <= i <= n + 1:
                        a = tiles[i - 2]
                        nk = geometry(a)[3]
                        pe.wait_ge(*p_ready.at(a))
                        b = bank.take(pe, TR, ("T", a))
                        for k in range(nk):
                            m = nc.tensor.transpose(b[:, k * P:(k + 1) * P], P_[:, (i - 2) % 3, k * P:(k + 1) * P],
                                                    ident[:, :])
                        m.then_inc(*pt_done.up(a))
                    if 3 <= i <= n + 2:
                        a = tiles[i - 3]
                        k0, nk = geometry(a)[2:4]
                        pe.wait_ge(*ptc.at(("PT", a)))
                        if a[2] == 0:
                            ob = bank.take(pe, OB, ("O", phase, a[1]))
                        for k in range(nk):
                            m = mm(ob[:, a[2] * HD:(a[2] + 1) * HD], PT_[:, (i - 3) % 2, k * P:(k + 1) * P],
                                   values(a, k0 + k), start=(a[2] == 0 and k == 0), stop=(k == nk - 1),
                                   skip_group_check=True)
                        m.then_inc(*pv_done.up(a))
                    for x in (2 * i, 2 * i + 1) if i < 4 else (i + 4,):
                        if filler and x in filler:
                            f, k = filler[x]
                            f(k)
                    if phase != "B" and i >= 11 and (i - 11) % 8 == 0:
                        turn2(phase, (i - 11) // 8, (ootile if phase == "C" else eotile)[:, :])
                    if events and i in events:
                        events[i]()

            def turn2(phase, g, src):
                pe.wait_ge(*dve_did.at((phase, "o", g)))
                b = bank.take(pe, TR, (phase, "oT", g))
                for c in range(4):
                    m = nc.tensor.transpose(b[:, c * P:(c + 1) * P], src[:, c * P:(c + 1) * P], ident[:, :])
                m.then_inc(*pe_did.up((phase, "oT", g)))

            def head_sums(c):
                pe.wait_ge(*sq_ready.at(("qk", c)))
                if c == 0:
                    bank.take(pe, TR, ("qk", "sum"))
                b = bank.tiles[found[("bank", ("qk", "sum"))]]
                for tt in range(TT):
                    m = mm(b[:, tt * 10 + 2 * c:tt * 10 + 2 * c + 2],
                           sqt[:, known.get(("sqslot", ("qk", c)), 0), tt * P:(tt + 1) * P], sel2[:, :],
                           start=(c == 0 and tt == 0), stop=(c == 4), skip_group_check=True)
                m.then_inc(*pe_did.up(("qk", "sum", c)))

            unit("ecq", 0, first=lambda k: dve_did.at(("e", "h", k)))
            unit("ecq", 1)
            sums("cq", 0, 2)
            unit("eckv", 0)
            sums("cq", 1, 2)
            unit("ekr", 0)
            sums("ckv", 0, 1)
            for c in range(5):
                unit(*(("eq", c) if c < 4 else ("ek", 0)))
                if c:
                    head_sums(c - 1)
            unit("ev", 0)
            head_sums(4)
            spread("ckv", 11)
            unit("ega", 0)
            pe.wait_ge(*dve_did.at(("qk", "stat")))
            b = bank.take(pe, TR, ("qk", "spread"))
            for tt in range(TT):
                for g in range(2):
                    at = EY + tt * 10 + 8 + g
                    m = mm(b[g * HD:(g + 1) * HD, tt * P:(tt + 1) * P], statf[:, at:at + 1].to_broadcast([P, HD]),
                           ident[:, :], start=True, stop=True)
            m.then_inc(*pe_did.up(("qk", "spread")))
            turn_unit("ev", 0, eotile)
            for i in range(1, 4):
                unit("ega", i)
            pe.wait_ge(*dve_did.at("ek"))
            pieces = {}
            for i in range(4):
                part = unit("egb", i, inline=False, pool=LIN)
                for k in range(DC):
                    pieces[i * DC + k] = (part, k)

            def values_b(tt):
                pe.wait_ge(*dve_did.at("ckv"))
                b = bank.take(pe, LIN, ("vB", tt))
                mm(b[:, :], eckv[:, tt * P:(tt + 1) * P], uv, start=True, stop=True)\
                    .then_inc(*pe_did.up(("vB", tt)))

            def head_prep(h):
                b = bank.take(pe, LIN, ("KF", h))
                mm(b[0:64, :], uk[:, h * HD:(h + 1) * HD], eckv[:, :], start=True, stop=True)\
                    .then_inc(*pe_did.up(("KF", h)))
                b = bank.take(pe, LIN, ("QF", h))
                for k in range(2):
                    m = mm(b[0:96, :], uq[:, k, h, :], ecq[:, k, :], start=(k == 0), stop=(k == 1))
                m.then_inc(*pe_did.up(("QF", h)))

            events = {VB_AT + tt: (lambda tt=tt: values_b(tt)) for tt in range(TT)}
            events[VB_AT + TT] = lambda: head_prep(0)
            events[VB_AT + TT + 1] = lambda: head_prep(1)
            attention("A", pieces, events)
            attention("B", events={4 * h - 5: (lambda h=h: head_prep(h)) for h in range(2, HEADS)})
            for qt in range(TT):
                turn2("B", qt, btok[:, qt, :])
            for i in range(DC):
                unit("eout", i, src=y_parts, first=(lambda k: dve_did.at(("ey", k))) if i == 0 else None)
                layer_out("o", i)
            spread("o", 0)
            for i in range(DC):
                unit("oq", i, first=(lambda k: dve_did.at(("o", "h", k))) if i == 0 else None)
            for i in range(2):
                unit("ok", i)
            for i in range(2):
                unit("ov", i)
            for i in range(DC - 1):
                unit("og", i)
                if i < 2:
                    turn_unit("ov", i, otmp[:, i, :])
            part = unit("og", DC - 1, inline=False, pool=LIN)
            pe.wait_ge(*act_did.at(("ok", 1)))
            pe.wait_ge(*act_did.at(("ov", 1)))
            attention("C", {k: (part, k) for k in range(DC)})
            for i in range(DC):
                unit("oout", i, src=y_parts, first=(lambda k: dve_did.at(("oy", k))) if i == 0 else None)
                layer_out("z", i)
            spread("z", 0)

        @block.gpsimd
        def _(pool):
            g = nc.gpsimd
            g.memset(ident[:, :], 0.0).then_inc(*pool_did.up("ident0"))
            g.memset(ones[:, :], 1.0).then_inc(*pool_did.up("ones"))
            g.memset(sel2[:, :], 0.0).then_inc(*pool_did.up("sel0"))
            pool.wait_ge(*pool_did.at("sel0"))
            g.memset(sel2[0:64, 0:1], 1.0).then_inc(*pool_did.up("sel1"))
            g.memset(sel2[64:128, 1:2], 1.0).then_inc(*pool_did.up("sel2"))
            pool.wait_ge(*pool_did.at("sel2"))
            g.affine_select(out=ident[:, :], in_=ident[:, :], compare_op=ALU.not_equal, fill=1.0, base=0,
                            pattern=[[-1, P]], channel_multiplier=1).then_inc(*pool_did.up("const"))

            def split(turn, s):
                pool.wait_ge(landed[s].sem, turn * 16 + 16)
                g.tensor_tensor(whi[:, s, 0:2], raw[:, s, 0:2], ones[:, :], ALU.mult)
                g.tensor_scalar(whi[:, s, 2:D], raw[:, s, 2:D], 1.0, 1.0, ALU.mult, ALU.mult)\
                    .then_inc(w_hi.sem, 1)
                pool.wait_ge(w_hi.sem, turn * WS + (s + 1))
                g.tensor_tensor(wlo[:, s, :], raw[:, s, :], whi[:, s, :].bitcast(F32), ALU.subtract)\
                    .then_inc(w_split.sem, 1)

            for s in range(WS):
                split(0, s)
            with pool.Fori(1, NU // WS, 1) as turn:
                for s in range(WS):
                    split(turn, s)
            for s in range(NU % WS):
                split(NU // WS, s)

        @block.sync
        def _(sp):
            for c in range(DC):
                sp.dma_start(xT[:, c, :], d["xT"][c]).then_inc(*xload[c].up(0, 16))
            sp.dma_start(cols[:, :], d["cols"]).then_inc(*loaded.up("cols", 16))

            def load(turn, s, wait):
                if wait:
                    sp.wait_ge(unit_done.sem, turn * WS + (s + 1 - WS))
                u = turn * WS + s
                src = d["w"][bass.ds(u, 1)] if wait else d["w"][u:u + 1]
                sp.dma_start(raw[:, s, :], src.rearrange("a p n -> (a p) n")).then_inc(landed[s].sem, 16)

            for s in range(WS):
                load(0, s, False)
            with sp.Fori(1, NU // WS, 1) as turn:
                for s in range(WS):
                    load(turn, s, True)
            for s in range(NU % WS):
                load(NU // WS, s, True)
            for i in range(DC):
                sp.wait_ge(*dve_did.at(("res", i)))
                sp.dma_start(out[i], xT[:, i, :]).then_inc(*stored.up(i, 16))
            sp.wait_ge(*stored.at(DC - 1))

        @block.scalar
        def _(act):
            A = nc.scalar.activation
            sqn = [0]

            def row_scale(a):
                if a[0] == "A":
                    at = EV + a[1] * 10 + a[2] % 4 * 2 + a[2] // 4
                    return statf[:, at:at + 1]
                return stat[:, 9, a[2]:a[2] + 1]

            def square(name, c, src, ready, scale=1.0):
                s = sqn[0] % 2
                if sqn[0] >= 2:
                    act.wait_ge(*pe_did.at(sqkeys[sqn[0] - 2]))
                found[("sqslot", (name, c))] = s
                sqkeys.append((name, "sum", c))
                sqn[0] += 1
                if ready is not None:
                    act.wait_ge(*ready)
                A(sqt[:, s, :], src, ACT.Square, scale=scale).then_inc(*sq_ready.up((name, c)))

            sqkeys = []

            def h_high(name, n=DC, shift=None):
                for c in range(n):
                    act.wait_ge(*dve_did.at((name, "hs", c)))
                    if shift is None:
                        A(hhi[:, c, :], hs[:, c % 2, :], ACT.Copy).then_inc(*act_did.up((name, "hhi", c)))
                    else:
                        A(hhi[:, c, :], hs[:, c % 2, :], ACT.Identity, bias=shift(c))\
                            .then_inc(*act_did.up((name, "hhi", c)))

            for c in range(DC):
                square("n1", c, xT[:, c, :], xload[c].at(0))
            act.wait_ge(*xload[DC - 1].at(0))
            act.dma_start(w1k, d["w1"][0].rearrange("p (j m) -> p j m", m=P)).then_inc(*w1load.up(("w1", 0), 16))
            act.dma_start(w2k, d["w2"][0]).then_inc(*tables_load.up("w2k", 16))
            act.dma_start(w2v, d["w2"][1]).then_inc(*tables_load.up("w2v", 16))
            act.dma_start(dist, d["dist"]).then_inc(*tables_load.up("d", 16))
            act.dma_start(distc, d["distc"]).then_inc(*tables_load.up("dist", 16))
            h_high("n1")
            act.wait_ge(*dve_did.at(("n1", "hs", DC - 1)))
            act.dma_start(w1v, d["w1"][1].rearrange("p (j m) -> p j m", m=P)).then_inc(*w1v_load.up(("w1", 1), 16))
            for c in range(CC):
                act.wait_ge(*unit_done.at(UNIT[("conv", 2 * c + 1)]))
                if c >= 2:
                    act.wait_ge(*dve_did.at(("z", c - 2)))
                A(hs[:, c % 2, :], bank.of(("conv", 2 * c + 1))[:, :], ACT.Tanh, scale=0.5)\
                    .then_inc(*act_did.up(("convgate", c)))
                bank.freed(("conv", 2 * c + 1), act_did, ("convgate", c))
            def q_evac(i):
                act.wait_ge(*unit_done.at(UNIT[("q", i)]))
                A(qT[:, i, :], bank.of(("q", i))[:, :], ACT.Copy, scale=HD ** -0.5)\
                    .then_inc(*act_did.up(("q", i)))
                bank.freed(("q", i), act_did, ("q", i))

            for i in range(4):
                if i == 3:
                    q_evac(0)
                if i < 3:
                    act.wait_ge(*unit_done.at(UNIT[("tok", i)]))
                    A(tokbuf(i), bank.of(("tok", i))[:, :], ACT.Copy).then_inc(*act_did.up(("tok", i, "copy")))
                    bank.freed(("tok", i), act_did, ("tok", i, "copy"))
                if i == 0:
                    continue
                j = i - 1
                act.wait_ge(*pe_did.at(("tok", j, "T")))
                turned = bank.of(("tok", j, "T"))[:, :].rearrange("p (t n) -> p t n", t=TT)
                if j < 2:
                    A(vtok[:, :, j * P:(j + 1) * P], turned, ACT.Copy).then_inc(*act_did.up(("tok", j)))
                else:
                    A(gate3, turned[:, :, 0:24], ACT.Tanh, scale=0.5).then_inc(*act_did.up(("tok", j)))
                bank.freed(("tok", j, "T"), act_did, ("tok", j))
            for i in range(1, 4):
                q_evac(i)
            for i in range(4):
                act.wait_ge(*unit_done.at(UNIT[("k", i)]))
                A(kv[:, i, :], bank.of(("k", i))[:, :], ACT.Copy).then_inc(*act_did.up(("k", i)))
                bank.freed(("k", i), act_did, ("k", i))
            act.wait_ge(*tables_load.at("dist"))
            for h in range(HEADS):
                A(biasc[:, :, h, :], distc.rearrange("p (t n) -> p t n", t=TT), ACT.Copy,
                  scale=2.0 ** -(h + 1)).then_inc(*act_did.up(("biasc", h)))
            act.wait_ge(*dve_did.at("cubic"))
            A(gel[:, 0, 256:256 + 4 * NCP], gel[:, 0, 128:128 + 4 * NCP], ACT.Tanh, scale=0.7978845608028654)\
                .then_inc(*act_did.up("gelu"))
            for h in range(HEADS):
                A(bias[:, h, :], dist[:, :], ACT.Copy, scale=2.0 ** -(h + 1)).then_inc(*act_did.up(("bias", h)))

            n = len(nsa)

            def exp_tile(i):
                a = nsa[i]
                kind, qt, j = a
                act.wait_ge(*sm_ready.at(a))
                if kind == "cmp":
                    A(pslots[i % 3][:, 0:256], pslots[i % 3][:, 0:256], ACT.Exp).then_inc(*p_ready.up(a))
                else:
                    L = (qt + 1) * P
                    x = qt * 16 + j
                    A(pslots[i % 3][:, 0:L], pslots[i % 3][:, 0:L], ACT.Exp, bias=nmax[:, x:x + 1], scale=-1.0,
                      accum_out=rsum[:, x:x + 1]).then_inc(*p_ready.up(a))

            def copy_tile(i):
                a = nsa[i]
                w = 256 if a[0] == "cmp" else (a[1] + 1) * P
                act.wait_ge(*pt_done.at(a))
                if i >= 2:
                    act.wait_ge(*pv_done.at(nsa[i - 2]))
                A(pttile[:, i % 2, 0:w], bank.of(("T", a))[:, 0:w], ACT.Copy).then_inc(*ptc.up(a))
                bank.freed(("T", a), ptc, a)

            def ga_evac(i):
                act.wait_ge(*unit_done.at(UNIT[("ga", i)]))
                A(merged[:, i, :], bank.of(("ga", i))[:, :], ACT.Tanh, scale=0.5)\
                    .then_inc(*act_did.up(("ga", i)))
                bank.freed(("ga", i), act_did, ("ga", i))

            def o_high(qt):
                act.wait_ge(*pe_did.at(("nsa", "oT", qt, 0)))
                A(ysplit[:, 0:4, qt * P:(qt + 1) * P],
                  bank.of(("nsa", "oT", qt, 0))[:, :].rearrange("p (c t) -> p c t", c=4), ACT.Copy)\
                    .then_inc(*act_did.up(("ohi", qt)))

            ga_evac(0)
            ga_evac(1)
            ga_at = {GA_STEPS * (j - 2) + DC: j for j in range(2, DC)}
            assert max(ga_at) < n + 2
            for i in range(n + 2):
                if i < n:
                    exp_tile(i)
                if i >= 2:
                    copy_tile(i - 2)
                if i in ga_at:
                    ga_evac(ga_at[i])
                if i >= 22 and (i - 22) % 17 == 0:
                    o_high((i - 22) // 17)
                if 33 <= i < 33 + CC:
                    square("var", i - 33, cacc[:, i - 33, :], dve_did.at(("zc", i - 33)))
                if 46 <= i < 46 + CC:
                    c = i - 46
                    act.wait_ge(*dve_did.at(("zn", c)))
                    A(cacc[:, c, :], cacc[:, c, :], ACT.Identity, scale=col("lng", c), bias=col("lnb", c))\
                        .then_inc(*act_did.up(("zu", c)))
                    if c >= 2:
                        act.wait_ge(*dve_did.at(("zs", c - 2)))
                    act.wait_ge(*act_did.at(("zu", c)))
                    A(hs[:, c % 2, :], cacc[:, c, :], ACT.Tanh, scale=0.5).then_inc(*act_did.up(("zt", c)))
                if 52 <= i < 52 + CC:
                    c = i - 52
                    act.wait_ge(*dve_did.at(("zs", c)))
                    A(yhi(4 + c), cacc[:, c, :], ACT.Copy, scale=0.5).then_inc(*act_did.up(("zhi", c)))
            o_high(TT - 1)
            for i in range(DC):
                act.wait_ge(*unit_done.at(UNIT[("gb", i)]))
                if i >= 2:
                    act.wait_ge(*dve_did.at(("mg", i - 2)))
                A(hs[:, i % 2, :], bank.of(("gb", i))[:, :], ACT.Tanh, scale=0.5)\
                    .then_inc(*act_did.up(("gb", i)))
                bank.freed(("gb", i), act_did, ("gb", i))
            for i in range(DC):
                if i == 0:
                    act.wait_ge(*unit_done.at(UNIT[("gb", DC - 1)]))
                act.wait_ge(*dve_did.at(("mg", i)))
                A(hhi[:, i, :], merged[:, i, :], ACT.Copy, scale=0.5).then_inc(*act_did.up(("mhi", i)))
            for i in range(DC):
                act.wait_ge(*dve_did.at(("m", i)))
                act.dma_start(xT[:, i, :], d["xT"][i]).then_inc(*xload[i].up(1, 16))
            act.dma_start(cact, d["c"]).then_inc(*c_load.up("c", 16))
            for i in range(DC):
                square("n2", i, xT[:, i, :], dve_did.at(("x1", i)))
            h_high("n2")
            act.wait_ge(*c_load.at("c"))
            A(ada[:, 0, :], cact, ACT.Tanh, scale=0.5).then_inc(*act_did.up("cact"))
            def ffn_conv(i):
                u = UNIT[("up", i)]
                act.wait_ge(*unit_done.at(u))
                if i >= 4:
                    act.wait_ge(*dve_did.at(("fs", (i - 4) // 2)))
                A(ua[:, i % 4, :], bank.of(("up", i))[:, :], ACT.Identity,
                  scale=col("ffw", order_up(i) * 3 + 2), bias=col("ffb", order_up(i)))\
                    .then_inc(*act_did.up(("uc", i)))

            def ffn_tanh(j):
                act.wait_ge(*dve_did.at(("ut", 2 * j)))
                if j >= 2:
                    act.wait_ge(*dve_did.at(("fs", j - 2)))
                A(ft[:, j % 2, :], ua[:, (2 * j) % 4, :], ACT.Tanh, scale=0.5).then_inc(*act_did.up(("ft", j)))

            def fa_high(i):
                if i >= DC:
                    act.wait_ge(*unit_done.at(UNIT[("down", i - DC)]))
                act.wait_ge(*dve_did.at(("fs", i)))
                A(yhi(i % DC), fa[:, i, :], ACT.Copy, scale=0.5).then_inc(*act_did.up(("fhi", i)))

            def ada_load(j):
                if j >= 2:
                    act.wait_ge(*dve_did.at(("ada", j - 2)))
                elif j == 0:
                    act.wait_ge(*dve_did.at("cact"))
                act.dma_start(ada[:, j % 2, :], d["ada"][j]).then_inc(*adaload[j % 2].up(j, 16))

            ada_load(0)
            ada_load(1)
            for i in range(2 * FC):
                ffn_conv(i)
                if 1 <= i:
                    ada_load(i + 1)
                if i >= 2 and i % 2 == 0:
                    ffn_tanh(i // 2 - 1)
                if i >= 2 * FC - DC:
                    fa_high(i - (2 * FC - DC))
            ffn_tanh(FC - 1)
            ada_load(2 * FC + 1)
            for i in range(DC, FC):
                if i == DC + 2:
                    for j in range(2 * FC + 2, 6 * DC):
                        ada_load(j)
                fa_high(i)
            for i in range(DC):
                square("f", i, xT[:, i, :], dve_did.at(("x2", i)))
                square("e", i, xT[:, i, :], None, scale=col("fg", i))
            act.wait_ge(*unit_done.at(UNIT[("down", FC - 1)]))
            for dst, name in ((cosA, "cosA"), (sinA, "sinA"), (cosT, "cosT"), (sinT, "sinT"), (uk, "uk"), (uv, "uv")):
                act.dma_start(dst, d[name]).then_inc(*tabload.up(name, 16))
            act.dma_start(late[:, 2 * T:2 * T + 1536], d["uq"]).then_inc(*tabload.up("all", 16))
            h_high("e", shift=lambda c: modc[:, 0, c:c + 1])

            def evac(name, i, dst, func=ACT.Copy, scale=1.0, key=None):
                act.wait_ge(*unit_done.at(UNIT[(name, i)]))
                A(dst, bank.of((name, i))[:, :], func, scale=scale).then_inc(*act_did.up(key or (name, i)))

            def square_unit(name, i, key, c):
                act.wait_ge(*unit_done.at(UNIT[(name, i)]))
                square(key, c, bank.of((name, i))[:, :], None)

            def tok_evac(name, i, dst):
                act.wait_ge(*pe_did.at((name, i, "T")))
                A(dst, bank.of((name, i, "T"))[:, :].rearrange("p (t n) -> p t n", t=TT), ACT.Copy)\
                    .then_inc(*act_did.up((name, i)))
                bank.freed((name, i, "T"), act_did, (name, i))

            def squared(name, i, key, c, dst, scale):
                act.wait_ge(*unit_done.at(UNIT[(name, i)]))
                square(key, c, bank.of((name, i))[:, :], None)
                evac(name, i, dst, ACT.Copy, scale)
                bank.freed((name, i), act_did, (name, i))

            for i in range(2):
                squared("ecq", i, "cq", i, ecq[:, i, :], col("cqg", i))
            squared("eckv", 0, "ckv", 0, eckv[:, :], col("ckvg"))
            evac("ekr", 0, ekr[:, :])
            bank.freed(("ekr", 0), act_did, ("ekr", 0))
            for i in range(4):
                squared("eq", i, "qk", i, eq[:, i, :], col("qn"))
            squared("ek", 0, "qk", 4, ek[:, :], col("kn"))
            evac("ev", 0, eotile, key=("ev", 0, "copy"))
            bank.freed(("ev", 0), act_did, ("ev", 0, "copy"))
            tok_evac("ev", 0, ev)
            for i in range(4):
                act.wait_ge(*unit_done.at(UNIT[("ega", i)]))
                A(esg[:, i, :], bank.of(("ega", i))[:, :], ACT.Tanh, scale=0.5).then_inc(*act_did.up(("ega", i)))

            def attention(phase, events=None):
                tiles = tiles_of(phase)
                n = len(tiles)
                P_, PT_ = p_of(phase)
                for i in range(n + 6):
                    if i < n:
                        a = tiles[i]
                        nk, x = geometry(a)[3:5]
                        act.wait_ge(*sm_ready.at(a))
                        if phase == "C":
                            A(P_[:, i % 3, 0:nk * P], P_[:, i % 3, 0:nk * P], ACT.Exp, bias=nmax[:, x:x + 1],
                              scale=-1.0, accum_out=rsum[:, x:x + 1]).then_inc(*p_ready.up(a))
                        else:
                            if i >= 3:
                                act.wait_ge(*pt_done.at(tiles[i - 3]))
                            A(P_[:, i % 3, :], bank.of(("S", a))[:, :], ACT.Exp, bias=nmax[:, x:x + 1],
                              scale=row_scale(a), accum_out=rsum[:, x:x + 1]).then_inc(*p_ready.up(a))
                            bank.freed(("S", a), p_ready, a)
                    if 2 <= i <= n + 1:
                        a = tiles[i - 2]
                        w = geometry(a)[3] * P
                        act.wait_ge(*pt_done.at(a))
                        if i >= 4:
                            act.wait_ge(*pv_done.at(tiles[i - 4]))
                        A(PT_[:, i % 2, 0:w], bank.of(("T", a))[:, 0:w], ACT.Copy)\
                            .then_inc(*ptc.up(("PT", a)))
                        bank.freed(("T", a), ptc, ("PT", a))
                    if phase != "B" and i >= 13 and (i - 13) % 8 == 0:
                        y_high(phase, (i - 13) // 8)
                    if phase == "C" and i >= 9 and (i - 9) % 8 == 0:
                        g = (i - 9) // 8
                        act.wait_ge(*dve_did.at(("sink", g)))
                        A(esink[:, g * 8:g * 8 + 8], esink[:, g * 8:g * 8 + 8], ACT.Exp)\
                            .then_inc(*act_did.up(("esink", g)))
                    if events and i in events:
                        events[i]()

            def y_high(phase, g):
                act.wait_ge(*dve_did.at((phase, "gated", g)))
                if phase == "C":
                    s, qt, tmp_ = g % 2 * 8, g // 2, otmp[:, 0, :]
                else:
                    s, qt, tmp_ = {"A": 0, "B": 8}[phase], g, etmp[:, g % 2, :]
                A(ysplit[:, s:s + 4, qt * P:(qt + 1) * P], tmp_.rearrange("p (c t) -> p c t", c=4), ACT.Copy,
                  scale=0.5).then_inc(*act_did.up((phase, "yhi", g)))

            def gb_evac(i):
                act.wait_ge(*unit_done.at(UNIT[("egb", i)]))
                A(esg[:, 4 + i, :], bank.of(("egb", i))[:, :], ACT.Tanh, scale=0.5).then_inc(*act_did.up(("egb", i)))

            def vb_copy(tt):
                act.wait_ge(*pe_did.at(("vB", tt)))
                A(vB[:, tt, :], bank.of(("vB", tt))[:, :], ACT.Copy).then_inc(*act_did.up(("vB", tt)))
                bank.freed(("vB", tt), act_did, ("vB", tt))

            def head_copy(h):
                act.wait_ge(*pe_did.at(("KF", h)))
                A(KF[0:64, h % 2, :], bank.of(("KF", h))[0:64, :], ACT.Copy).then_inc(*act_did.up(("KF", h)))
                bank.freed(("KF", h), act_did, ("KF", h))
                act.wait_ge(*pe_did.at(("QF", h)))
                A(QF[0:96, h % 2, :], bank.of(("QF", h))[0:96, :], ACT.Copy).then_inc(*act_did.up(("QF", h)))
                bank.freed(("QF", h), act_did, ("QF", h))

            events = {5 + 8 * i: (lambda i=i: gb_evac(i)) for i in range(4)}
            for tt in range(TT):
                events[VB_AT + 1 + tt] = lambda tt=tt: vb_copy(tt)
            events[VB_AT + TT + 1] = lambda: head_copy(0)
            attention("A", events)
            attention("B", {max(4 * h - 4, 0): (lambda h=h: head_copy(h)) for h in range(1, HEADS)})
            for g in range(TT):
                y_high("B", g)
            for i in range(DC):
                square("o", i, xT[:, i, :], dve_did.at(("x3", i)))
            h_high("o", shift=lambda c: modc[:, 1, c:c + 1])
            act.dma_start(distC, d["distC"]).then_inc(*tabload.up("distC", 16))
            for i in range(DC):
                evac("oq", i, oq[:, i, :], scale=HD ** -0.5)
                bank.freed(("oq", i), act_did, ("oq", i))
            for i in range(2):
                evac("ok", i, ok[:, i, :])
                bank.freed(("ok", i), act_did, ("ok", i))
            for i in range(2):
                evac("ov", i, otmp[:, i, :], key=("ov", i, "copy"))
                bank.freed(("ov", i), act_did, ("ov", i, "copy"))
            def head_bias(h):
                if h == 0:
                    act.wait_ge(*tabload.at("distC"))
                if h == 8:
                    act.wait_ge(*unit_done.at(UNIT[("og", DC - 1)]))
                A(obias[h], distC[:, :], ACT.Copy, scale=2.0 ** (-8.0 * (h + 1) / C_HEADS))\
                    .then_inc(*act_did.up(("obias", h)))

            for h in range(8):
                head_bias(h)
            def og_evac(i):
                act.wait_ge(*unit_done.at(UNIT[("og", i)]))
                A(osg[:, i, :], bank.of(("og", i))[:, :], ACT.Tanh, scale=0.5).then_inc(*act_did.up(("og", i)))

            for i in range(DC - 1):
                if 1 <= i <= 2:
                    tok_evac("ov", i - 1, ov[:, :, (i - 1) * P:i * P])
                og_evac(i)
            events = {h - 3: (lambda h=h: head_bias(h)) for h in range(8, C_HEADS)}
            events[4] = lambda: og_evac(DC - 1)
            attention("C", events)
            for i in range(DC):
                square("z", i, xT[:, i, :], dve_did.at(("x4", i)))

        @block.vector
        def _(dve):
            V = nc.vector

            def link(ins):
                ins.then_inc(*dve_did.up(("link", dve_did.n)))
                dve.wait_ge(dve_did.sem, dve_did.n)

            def inverse_root(y, v, t):
                link(V.tensor_scalar(t.bitcast(I32), v.bitcast(I32), 1, None, ALU.logical_shift_right))
                link(V.tensor_scalar(y.bitcast(I32), t.bitcast(I32), -1.0, float(0x5f3759df), ALU.mult, ALU.add))
                for step in range(3):
                    link(V.scalar_tensor_tensor(t, y, -0.5, y, ALU.mult, ALU.mult))
                    link(V.tensor_tensor(t, t, v, ALU.mult))
                    link(V.scalar_tensor_tensor(y, t, 1.5, y, ALU.add, ALU.mult))

            def rstd(name, c0, scale):
                v, y, t = stat[:, c0 + 1, 0:TT], stat[:, c0, 0:TT], stat[:, c0 + 2, 0:TT]
                link(V.tensor_scalar(v, bank.of((name, "sum"))[:, 0:TT], scale, EPS, ALU.mult, ALU.add))
                bank.freed((name, "sum"), dve_did, ("link", dve_did.n - 1))
                inverse_root(y, v, t)
                found[("dve_did", (name, "stat"))] = dve_did.n

            def h_split(name, src, gain, shift=None):
                dve.wait_ge(*pe_did.at((name, "spread")))
                b = bank.of((name, "spread"))
                for c in range(DC + 1):
                    if c < DC:
                        if c >= 2:
                            dve.wait_ge(*dve_did.at((name, "h", c - 2)))
                        V.scalar_tensor_tensor(hs[:, c % 2, :], src(c), gain(c), b[:, :], ALU.mult, ALU.mult)\
                            .then_inc(*dve_did.up((name, "hs", c)))
                        if c == DC - 1:
                            bank.freed((name, "spread"), dve_did, (name, "hs", c))
                    if c >= 1:
                        k = c - 1
                        dve.wait_ge(*act_did.at((name, "hhi", k)))
                        if shift is None:
                            V.tensor_tensor(hlo[:, k, :], hs[:, k % 2, :], hhi[:, k, :].bitcast(F32),
                                            ALU.subtract).then_inc(*dve_did.up((name, "h", k)))
                        else:
                            V.scalar_tensor_tensor(hlo[:, k, :], hs[:, k % 2, :], shift(k),
                                                   hhi[:, k, :].bitcast(F32), ALU.add, ALU.subtract)\
                                .then_inc(*dve_did.up((name, "h", k)))

            def norm(name, gain, src=lambda c: xT[:, c, :], scale=1.0 / D, shift=None):
                dve.wait_ge(*pe_did.at((name, "sum", DC - 1)))
                rstd(name, 0, scale)
                h_split(name, src, gain, shift)

            link(V.memset(z[:, :, 0:TAPS - 1], 0.0))
            dve.wait_ge(*loaded.at("cols"))
            link(V.tensor_scalar(ctap, col("dww", 0, CC * TAPS).rearrange("p (c n) -> p c n", c=CC), 0.5, None,
                                 ALU.mult))
            norm("n1", lambda c: col("n1g", c))
            for c in range(CC):
                dve.wait_ge(*act_did.at(("convgate", c)))
                V.scalar_tensor_tensor(z[:, c, TAPS - 1:ZW], hs[:, c % 2, :], 1.0, bank.of(("conv", 2 * c))[:, :],
                                       ALU.add, ALU.mult).then_inc(*dve_did.up(("z", c)))
                bank.freed(("conv", 2 * c), dve_did, ("z", c))
                if c == CC - 1:
                    dve.wait_ge(*dve_did.at(("z", c)))
            steps = [(k, c) for k in range(TAPS - 1, -1, -1) for c in range(CC)]

            def tap(k, c):
                w = ctap[:, c, k:k + 1]
                if k == TAPS - 1:
                    V.tensor_scalar(cacc[:, c, :], z[:, c, k:k + T], w, col("dwb", c), ALU.mult, ALU.add)\
                        .then_inc(*dve_did.up(("tap", k, c)))
                    return
                dve.wait_ge(*dve_did.at(("tap", k + 1, c)))
                V.scalar_tensor_tensor(cacc[:, c, :], z[:, c, k:k + T], w, cacc[:, c, :], ALU.mult, ALU.add)\
                    .then_inc(*dve_did.up(("conv", c) if k == 0 else ("tap", k, c)))

            for k, c in steps[:84]:
                tap(k, c)
            steps = steps[84:]
            dve.wait_ge(*act_did.at(("tok", 2)))
            link(V.tensor_scalar(gate3, gate3, 0.5, 0.5, ALU.mult, ALU.add))
            dve.wait_ge(*pe_did.at(("tok", 2, "T")))
            for g in range(2):
                link(V.memset(blk[64 * g:64 * g + 64, :, :, 1 - g, :], 0.0))
            for v in range(2):
                dve.wait_ge(*act_did.at(("k", 2 + v)))
                win = kv[:, 2 + v, :].rearrange("p (m b) -> p b m", b=CMP_STRIDE)
                pe_ = col("pek" if v == 0 else "pev", 0, CMP_BLOCK)
                for half in range(2):
                    for g in range(2):
                        row = slice(64 * g, 64 * g + 64)
                        V.tensor_tensor(
                            blk[row, v, half * CMP_STRIDE:(half + 1) * CMP_STRIDE, g, :],
                            win[row, :, half:half + NCMP],
                            pe_[row, half * CMP_STRIDE:(half + 1) * CMP_STRIDE].unsqueeze(2)
                            .to_broadcast([64, CMP_STRIDE, NCMP]), ALU.add)\
                            .then_inc(*dve_did.up(("blk", v) if half and g else ("blk0", v, half, g)))
            W = 4 * NCP
            gx, g3, gt = gel[:, 0, 0:W], gel[:, 0, 128:128 + W], gel[:, 0, 256:256 + W]
            dve.wait_ge(*act_did.at(("convgate", CC - 1)))
            link(V.memset(gel[:, 0, 0:384], 0.0))
            link(V.memset(kcmp, 0.0))
            link(V.memset(vblk, 0.0))
            dve.wait_ge(*pe_did.at("hid"))
            link(V.memset(tmp[:, 0, :], 0.0))
            link(V.tensor_copy(gx.rearrange("p (v g n) -> p v g n", v=2, g=2)[:, :, :, 0:NCMP],
                               bank.of("hid")[:, 0:128].rearrange("p (v m) -> p v m", v=2)[:, :, 0:2 * NCMP]
                               .rearrange("p v (g n) -> p v g n", g=2)))
            bank.freed("hid", dve_did, ("link", dve_did.n - 1))
            link(V.tensor_tensor(g3, gx, gx, ALU.mult))
            link(V.tensor_scalar(g3, g3, 0.044715, 1.0, ALU.mult, ALU.add))
            V.tensor_tensor(g3, g3, gx, ALU.mult).then_inc(*dve_did.up("cubic"))
            dve.wait_ge(*act_did.at("gelu"))
            link(V.tensor_scalar(gt, gt, 0.5, 0.5, ALU.mult, ALU.add))
            hg = lambda v, g: (gt[:, (2 * v + g) * NCP:(2 * v + g) * NCP + NCMP],
                               gx[:, (2 * v + g) * NCP:(2 * v + g) * NCP + NCMP])
            for g in range(2):
                link(V.tensor_tensor(hidk[:, g, 0:NCMP], *hg(0, g), ALU.mult))
                for r in range(4):
                    ins = V.tensor_tensor(hidv[:, g, r, 0:NCMP], *hg(1, g), ALU.mult)
                    if g == 1 and r == 3:
                        ins.then_inc(*dve_did.up("hid"))
                    else:
                        link(ins)
            dve.wait_ge(*pe_did.at("cmp2"))
            c2 = bank.of("cmp2")
            link(V.tensor_copy(kcmp[:, 0:NCMP], c2[:, 0:NCMP]))
            for g in range(2):
                for r in range(4):
                    ins = V.tensor_copy(vblk[32 * r:32 * r + 32, g, r * HD:(r + 1) * HD],
                                        c2[32 * r:32 * r + 32, 64 + g * HD:64 + (g + 1) * HD])
                    if g == 1 and r == 3:
                        ins.then_inc(*dve_did.up("cmp2"))
                    else:
                        link(ins)
            bank.freed("cmp2", dve_did, "cmp2")
            n = len(nsa)
            def score_tile(i):
                a = nsa[i]
                kind, qt, j = a
                dve.wait_ge(*s_done.at(a))
                if i >= 3:
                    dve.wait_ge(*pt_done.at(nsa[i - 3]))
                    if nsa[i - 3][0] == "cmp":
                        dve.wait_ge(*dve_did.at(("csum", nsa[i - 3][1])))
                S = bank.of(("S", a))
                if qt == 0 and (kind == "cmp" or j < HEADS):
                    dve.wait_ge(*act_did.at(("biasc", HEADS - 1) if kind == "cmp" else ("bias", j)))
                if kind == "cmp":
                    x = 128 + qt * 8
                    sc3 = pslots[i % 3][:, 0:256].rearrange("p (h n) -> p h n", h=HEADS)
                    for g in range(2):
                        half = slice(g * 128, (g + 1) * 128)
                        link(V.tensor_tensor(pslots[i % 3][:, half], bank.of((("S", "S2")[g], a))[:, 0:128],
                                             biasc[:, qt].rearrange("p h n -> p (h n)")[:, half], ALU.add))
                    bank.freed(("S2", a), sm_ready, a)
                    link(V.tensor_reduce(nmax[:, x:x + 8], sc3, AX_X, ALU.max))
                    V.tensor_tensor(sc3, sc3, nmax[:, x:x + 8].unsqueeze(2).to_broadcast([P, HEADS, NCP]),
                                    ALU.subtract).then_inc(*sm_ready.up(a))
                else:
                    L = (qt + 1) * P
                    x = qt * 16 + j
                    V.tensor_tensor_reduce(pslots[i % 3][:, 0:L], S[:, 0:L],
                                           bias[:, j % HEADS, T - L:T], -1.0, 3.0e38, ALU.add, ALU.min,
                                           nmax[:, x:x + 1]).then_inc(*sm_ready.up(a))
                bank.freed(("S", a), sm_ready, a)

            def o_add(qt, part):
                a = ("cmp", qt, 0) if part == 0 else ("nsa", qt, part * HEADS - 1)
                dve.wait_ge(*pv_done.at(a))
                x = 128 + qt * 8 if part == 0 else qt * 16 + (part - 1) * HEADS
                r = rinv[:, x:x + 8]
                link(V.reciprocal(r, rsum[:, x:x + 8]))
                link(V.tensor_tensor(r, r, gate3[:, qt, part:24:3], ALU.mult))
                if part == 0 and qt == 0:
                    link(V.tensor_scalar(r, r, col("rowvalid"), None, ALU.mult))
                O = bank.of(("O", qt, part))[:, :].rearrange("p (h e) -> p h e", h=HEADS)
                rb = r.unsqueeze(2).to_broadcast([P, HEADS, HD])
                if part == 0 and qt >= 1:
                    dve.wait_ge(*pe_did.at(("nsa", "oT", qt - 1, 0)))
                dst = otile if part == 0 else tmp[:, 1, :]
                ins = V.tensor_tensor(dst.rearrange("p (h e) -> p h e", h=HEADS), O, rb, ALU.mult)
                link(ins)
                bank.freed(("O", qt, part), dve_did, ("link", dve_did.n - 1))
                if part:
                    ins = V.tensor_tensor(otile, otile, tmp[:, 1, :], ALU.add)
                    if part == 1:
                        link(ins)
                    else:
                        ins.then_inc(*dve_did.up(("nsa", "o", qt)))

            def cmp_sum(i):
                a = nsa[i]
                x = 128 + a[1] * 8
                dve.wait_ge(*p_ready.at(a))
                V.tensor_reduce(rsum[:, x:x + 8], pslots[i % 3][:, 0:256].rearrange("p (h n) -> p h n", h=HEADS),
                                AX_X, ALU.add).then_inc(*dve_did.up(("csum", a[1])))

            def o_low(qt):
                dve.wait_ge(*act_did.at(("ohi", qt)))
                V.tensor_tensor(ysplit[:, 4:8, qt * P:(qt + 1) * P],
                                bank.of(("nsa", "oT", qt, 0))[:, :].rearrange("p (c t) -> p c t", c=4),
                                ysplit[:, 0:4, qt * P:(qt + 1) * P].bitcast(F32), ALU.subtract)\
                    .then_inc(*dve_did.up(("olo", qt)))
                bank.freed(("nsa", "oT", qt, 0), dve_did, ("olo", qt))

            def neg_mean():
                dve.wait_ge(*pe_did.at(("mu", "sum", CC - 1)))
                V.tensor_scalar(stat[:, 2, 0:TT], bank.of(("mu", "sum"))[:, 0:TT], -1.0 / CONV_CH, None, ALU.mult)\
                    .then_inc(*dve_did.up(("mu", "stat")))
                bank.freed(("mu", "sum"), dve_did, ("mu", "stat"))

            def center(c):
                dve.wait_ge(*pe_did.at(("mu", "spread")))
                V.tensor_tensor(cacc[:, c, :], cacc[:, c, :], bank.of(("mu", "spread"))[:, :], ALU.add)\
                    .then_inc(*dve_did.up(("zc", c)))
                if c == CC - 1:
                    bank.freed(("mu", "spread"), dve_did, ("zc", c))

            def var_rstd():
                dve.wait_ge(*pe_did.at(("var", "sum", CC - 1)))
                rstd("var", 4, 1.0 / CONV_CH)

            def scale_z(c):
                dve.wait_ge(*pe_did.at(("var", "spread")))
                V.tensor_tensor(cacc[:, c, :], cacc[:, c, :], bank.of(("var", "spread"))[:, :], ALU.mult)\
                    .then_inc(*dve_did.up(("zn", c)))
                if c == CC - 1:
                    bank.freed(("var", "spread"), dve_did, ("zn", c))

            def silu_z(c):
                dve.wait_ge(*act_did.at(("zt", c)))
                V.scalar_tensor_tensor(cacc[:, c, :], hs[:, c % 2, :], 1.0, cacc[:, c, :], ALU.add, ALU.mult)\
                    .then_inc(*dve_did.up(("zs", c)))

            def low_z(c):
                dve.wait_ge(*act_did.at(("zhi", c)))
                V.scalar_tensor_tensor(ylo(4 + c), cacc[:, c, :], 0.5, yhi(4 + c).bitcast(F32),
                                       ALU.mult, ALU.subtract).then_inc(*dve_did.up(("y", 4 + c)))

            events = {27: neg_mean, 40: var_rstd}
            for first, step in ((31, center), (44, scale_z), (48, silu_z), (54, low_z)):
                for c in range(CC):
                    events[first + c] = (lambda step=step, c=c: step(c))
            for i in range(n + 4):
                if i < n:
                    score_tile(i)
                if i in events:
                    events[i]()
                if 2 <= i < n + 2 and nsa[i - 2][0] == "cmp":
                    cmp_sum(i - 2)
                j = i - 4
                if j >= 0:
                    a = nsa[j]
                    if a[0] == "cmp":
                        o_add(a[1], 0)
                    elif a[2] % HEADS == HEADS - 1:
                        o_add(a[1], 1 + a[2] // HEADS)
                for s in steps[:2]:
                    tap(*s)
                steps = steps[2:]
                if i >= 23 and (i - 23) % 17 == 0:
                    o_low((i - 23) // 17)
            dve.wait_ge(*act_did.at(("ohi", TT - 1)))
            o_low(TT - 1)
            for c in range(4):
                found[("dve_did", ("y", c))] = dve_did.n
            for i in range(DC):
                dve.wait_ge(*unit_done.at(UNIT[("y", i)]))
                if i == 0:
                    dve.wait_ge(*act_did.at(("ga", DC - 1)))
                link(V.scalar_tensor_tensor(merged[:, i, :], merged[:, i, :], 1.0, bank.of(("y", i, 0))[:, :],
                                            ALU.add, ALU.mult))
                bank.freed(("y", i, 0), dve_did, ("link", dve_did.n - 1))
                dve.wait_ge(*act_did.at(("gb", i)))
                link(V.scalar_tensor_tensor(tmp[:, 1, :], hs[:, i % 2, :], 1.0, bank.of(("y", i, 1))[:, :],
                                            ALU.add, ALU.mult))
                bank.freed(("y", i, 1), dve_did, ("link", dve_did.n - 1))
                V.tensor_tensor(merged[:, i, :], merged[:, i, :], tmp[:, 1, :], ALU.add)\
                    .then_inc(*dve_did.up(("mg", i)))
            for i in range(DC):
                dve.wait_ge(*act_did.at(("mhi", i)))
                V.scalar_tensor_tensor(hlo[:, i, :], merged[:, i, :], 0.5, hhi[:, i, :].bitcast(F32),
                                       ALU.mult, ALU.subtract).then_inc(*dve_did.up(("m", i)))
            for i in range(DC):
                dve.wait_ge(*unit_done.at(UNIT[("wout", i)]))
                dve.wait_ge(*xload[i].at(1))
                V.tensor_tensor(xT[:, i, :], xT[:, i, :], bank.of(("wout", i))[:, :], ALU.add)\
                    .then_inc(*dve_did.up(("x1", i)))
                bank.freed(("wout", i), dve_did, ("x1", i))
            norm("n2", lambda c: col("n2g", c))

            dve.wait_ge(*act_did.at("cact"))
            link(V.scalar_tensor_tensor(cact, ada[:, 0, :], 1.0, cact, ALU.add, ALU.mult))
            V.tensor_scalar(cact, cact, 0.5, None, ALU.mult).then_inc(*dve_did.up("cact"))
            dve.wait_ge(*dve_did.at("cact"))

            def ada_unit(j):
                dve.wait_ge(*adaload[j % 2].at(j))
                V.tensor_tensor_reduce(ada[:, j % 2, :], ada[:, j % 2, :], cact, 1.0, 0.0, ALU.mult, ALU.add,
                                       modc[:, j // (3 * DC), j % (3 * DC):j % (3 * DC) + 1])\
                    .then_inc(*dve_did.up(("ada", j)))

            def fa_low(i):
                dve.wait_ge(*act_did.at(("fhi", i)))
                V.scalar_tensor_tensor(ylo(i % DC), fa[:, i, :], 0.5, yhi(i % DC).bitcast(F32),
                                       ALU.mult, ALU.subtract).then_inc(*dve_did.up(("fa", i)))

            def ffn_taps(i):
                dve.wait_ge(*act_did.at(("uc", i)))
                b, s, w = bank.of(("up", i)), i % 4, order_up(i) * 3
                link(V.scalar_tensor_tensor(ua[:, s, 1:T], b[:, 0:T - 1], col("ffw", w + 1), ua[:, s, 1:T],
                                            ALU.mult, ALU.add))
                V.scalar_tensor_tensor(ua[:, s, 2:T], b[:, 0:T - 2], col("ffw", w), ua[:, s, 2:T],
                                       ALU.mult, ALU.add).then_inc(*dve_did.up(("ut", i)))
                bank.freed(("up", i), dve_did, ("ut", i))

            def ffn_mul(j):
                dve.wait_ge(*act_did.at(("ft", j)))
                sa, sv = (2 * j) % 4, (2 * j + 1) % 4
                link(V.scalar_tensor_tensor(ft[:, j % 2, :], ft[:, j % 2, :], 1.0, ua[:, sa, :], ALU.add, ALU.mult))
                V.tensor_tensor(fa[:, j, :], ft[:, j % 2, :], ua[:, sv, :], ALU.mult)\
                    .then_inc(*dve_did.up(("fs", j)))

            for i in range(2 * FC):
                ffn_taps(i)
                if i % 2 == 1 and i >= 3:
                    ffn_mul(i // 2 - 1)
                ada_unit(i)
                if i >= 2 * FC - DC:
                    fa_low(i - (2 * FC - DC))
            ffn_mul(FC - 1)
            def modulation():
                for j in range(2 * FC, 6 * DC):
                    ada_unit(j)
                dve.wait_ge(*dve_did.at(("ada", 6 * DC - 1)))
                mod = modc[:].rearrange("p l c -> p (l c)")
                link(V.tensor_tensor(mod, mod, col("adab", 0, 6 * DC), ALU.add))
                for layer in range(2):
                    link(V.scalar_tensor_tensor(gn[:, layer, :], modc[:, layer, DC:2 * DC], 1.0,
                                                col("nw", layer * DC, DC), ALU.add, ALU.mult))
                link(V.tensor_tensor(fgn[:, :], gn[:, 0, :], col("fg", 0, DC), ALU.mult))

            for i in range(DC, FC):
                if i == DC + 2:
                    modulation()
                fa_low(i)
            for i in range(DC):
                if i < DC - 1:
                    dve.wait_ge(*pe_did.at(("down", i)))
                else:
                    dve.wait_ge(*unit_done.at(UNIT[("down", FC - 1)]))
                V.tensor_tensor(xT[:, i, :], xT[:, i, :], bank.of(("down", i))[:, :], ALU.add)\
                    .then_inc(*dve_did.up(("x2", i)))
                bank.freed(("down", i), dve_did, ("x2", i))

            def norm_in_place(name, gain, key):
                dve.wait_ge(*pe_did.at((name, "sum", DC - 1)))
                rstd(name, 0, 1.0 / D)
                dve.wait_ge(*pe_did.at((name, "spread")))
                for c in range(DC):
                    V.scalar_tensor_tensor(xT[:, c, :], xT[:, c, :], gain(c), bank.of((name, "spread"))[:, :],
                                           ALU.mult, ALU.mult).then_inc(*dve_did.up((key, c)))
                bank.freed((name, "spread"), dve_did, (key, DC - 1))

            dve.wait_ge(*pe_did.at(("e", "sum", DC - 1)))
            y, v, t = (stat[:, c, 0:2 * TT] for c in (0, 1, 2))
            link(V.tensor_scalar(v[:, 0:TT], bank.of(("fe", "sum"))[:, 0:TT], 1.0 / D, EPS, ALU.mult, ALU.add))
            link(V.tensor_scalar(v[:, TT:2 * TT], v[:, 0:TT], EPS * D, None, ALU.mult))
            link(V.tensor_tensor(v[:, TT:2 * TT], v[:, TT:2 * TT], bank.of(("fe", "sum"))[:, TT:2 * TT], ALU.add))
            bank.freed(("fe", "sum"), dve_did, ("link", dve_did.n - 1))
            link(V.tensor_scalar(v[:, TT:2 * TT], v[:, TT:2 * TT], 1.0 / D, None, ALU.mult))
            inverse_root(y, v, t)
            for name in ("e", "f"):
                found[("dve_did", (name, "stat"))] = dve_did.n
            h_split("e", lambda c: xT[:, c, :], lambda c: fgn[:, c:c + 1], shift=lambda c: modc[:, 0, c:c + 1])
            dve.wait_ge(*pe_did.at(("f", "spread")))
            for c in range(DC):
                V.scalar_tensor_tensor(xT[:, c, :], xT[:, c, :], col("fg", c), bank.of(("f", "spread"))[:, :],
                                       ALU.mult, ALU.mult).then_inc(*dve_did.up(("xn", c)))
            bank.freed(("f", "spread"), dve_did, ("xn", DC - 1))

            def rope(x, t, cos, sin, last):
                link(V.stream_shuffle(t, x, [(j + 16) % 32 for j in range(32)]))
                link(V.tensor_tensor(t, t, sin, ALU.mult))
                link(V.tensor_tensor(x, x, cos, ALU.mult))
                V.tensor_tensor(x, x, t, ALU.add).then_inc(*dve_did.up(last))

            dve.wait_ge(*pe_did.at(("cq", "sum", 1)))
            rstd("cq", 8, 1.0 / 256)
            link(V.tensor_scalar(stat[:, 9, 0:TT], stat[:, 8, 0:TT], 96.0 ** -0.5, None, ALU.mult))
            dve.wait_ge(*pe_did.at(("ckv", "sum", 0)))
            rstd("ckv", 11, 1.0 / P)
            dve.wait_ge(*tabload.at("all"))
            for c in range(4):
                dve.wait_ge(*act_did.at(("eq", c)))
                rope(eq[:, c, :], etmp[:, 0, :], cosA, sinA, ("eq", c))
                dve.wait_ge(*dve_did.at(("eq", c)))
            dve.wait_ge(*pe_did.at(("qk", "sum", 4)))
            v, y, t = st40(EV), st40(EY), st40(ET)
            link(V.tensor_scalar(v, bank.of(("qk", "sum"))[:, 0:40], 1.0 / HD, EPS, ALU.mult, ALU.add))
            bank.freed(("qk", "sum"), dve_did, ("link", dve_did.n - 1))
            inverse_root(y, v, t)
            V.tensor_scalar(v, y, HD ** -0.5, None, ALU.mult).then_inc(*dve_did.up(("qk", "stat")))
            dve.wait_ge(*act_did.at(("ek", 0)))
            dve.wait_ge(*pe_did.at(("qk", "spread")))
            link(V.tensor_tensor(ek[:, :], ek[:, :], bank.of(("qk", "spread"))[:, :], ALU.mult))
            bank.freed(("qk", "spread"), dve_did, ("link", dve_did.n - 1))
            rope(ek[:, :], etmp[:, 0, :], cosA, sinA, "ek")
            dve.wait_ge(*pe_did.at(("ckv", "spread")))
            V.tensor_tensor(eckv[:, :], eckv[:, :], bank.of(("ckv", "spread"))[:, :], ALU.mult)\
                .then_inc(*dve_did.up("ckv"))
            bank.freed(("ckv", "spread"), dve_did, "ckv")
            dve.wait_ge(*dve_did.at("ek"))
            rope(ekr[64:96, :], etmp[64:96, 0, :], cosT[64:96, :], sinT[64:96, :], "ekr")

            def gates(name, i, dst):
                dve.wait_ge(*act_did.at((name, i)))
                V.scalar_tensor_tensor(dst, dst, 1.0, bank.of((name, i))[:, :], ALU.add, ALU.mult)\
                    .then_inc(*dve_did.up(("g", name, i)))
                bank.freed((name, i), dve_did, ("g", name, i))

            for i in range(4):
                gates("ega", i, esg[:, i, :])
            dve.wait_ge(*dve_did.at(("g", "ega", 3)))

            def gated(phase, g):
                dve.wait_ge(*pe_did.at((phase, "oT", g)))
                c0, qt = {"A": (0, g), "B": (4, g), "C": (g % 2 * 4, g // 2)}[phase]
                sg, dst = (osg, otmp[:, 0, :]) if phase == "C" else (esg, etmp[:, g % 2, :])
                if phase == "B" and g >= 2:
                    dve.wait_ge(*dve_did.at(("B", "ylo", g - 2)))
                V.tensor_tensor(dst.rearrange("p (c t) -> p c t", c=4),
                                bank.of((phase, "oT", g))[:, :].rearrange("p (c t) -> p c t", c=4),
                                sg[:, c0:c0 + 4, qt * P:(qt + 1) * P], ALU.mult)\
                    .then_inc(*dve_did.up((phase, "gated", g)))
                bank.freed((phase, "oT", g), dve_did, (phase, "gated", g))

            def y_low(phase, g):
                dve.wait_ge(*act_did.at((phase, "yhi", g)))
                s, qt = {"A": (0, g), "B": (8, g), "C": (g % 2 * 8, g // 2)}[phase]
                src = otmp[:, 0, :] if phase == "C" else etmp[:, g % 2, :]
                V.scalar_tensor_tensor(ysplit[:, s + 4:s + 8, qt * P:(qt + 1) * P],
                                       src.rearrange("p (c t) -> p c t", c=4), 0.5,
                                       ysplit[:, s:s + 4, qt * P:(qt + 1) * P].bitcast(F32),
                                       ALU.mult, ALU.subtract).then_inc(*dve_did.up((phase, "ylo", g)))

            def row_scale(a):
                if a[0] == "A":
                    at = EV + a[1] * 10 + a[2] % 4 * 2 + a[2] // 4
                    return statf[:, at:at + 1]
                return stat[:, 9, a[2]:a[2] + 1]

            def attention(phase, events=None):
                tiles = tiles_of(phase)
                n = len(tiles)
                per = TT if phase == "B" else HEADS
                P_, PT_ = p_of(phase)
                for i in range(n + 7):
                    if i < n:
                        a = tiles[i]
                        k0, nk, x = geometry(a)[2:5]
                        dve.wait_ge(*s_done.at(a))
                        S = bank.of(("S", a))
                        if phase == "C":
                            if i >= 3:
                                dve.wait_ge(*pt_done.at(tiles[i - 3]))
                            h = a[1] % 2 * 8 + a[2]
                            j0 = (k0 - (a[1] // 2 - 1)) * P
                            if a[1] < 2:
                                dve.wait_ge(*act_did.at(("obias", h)))
                            V.tensor_tensor_reduce(P_[:, i % 3, 0:nk * P], S[:, 0:nk * P],
                                                   obias[h][:, j0:j0 + nk * P], -1.0, nsink[:, h:h + 1],
                                                   ALU.add, ALU.min, nmax[:, x:x + 1])\
                                .then_inc(*sm_ready.up(a))
                            bank.freed(("S", a), sm_ready, a)
                        else:
                            link(V.tensor_reduce(nmax[:, x:x + 1], S[:, :], AX_X, ALU.max, negate=True))
                            V.tensor_tensor(nmax[:, x:x + 1], nmax[:, x:x + 1], row_scale(a), ALU.mult)\
                                .then_inc(*sm_ready.up(a))
                    if phase == "C" and i >= 8 and i % 8 == 0 and i <= n:
                        g = i // 8 - 1
                        x = 64 + g * 8
                        dve.wait_ge(*sm_ready.at(tiles[8 * g + 7]))
                        V.tensor_tensor(esink[:, g * 8:g * 8 + 8], nmax[:, x:x + 8],
                                        col("sink", g % 2 * 8, 8), ALU.add).then_inc(*dve_did.up(("sink", g)))
                    j = i - 4
                    if 0 <= j < n and j % per == per - 1:
                        g = j // per
                        a = tiles[j]
                        x = geometry(a)[4] - per + 1
                        dve.wait_ge(*pv_done.at(a))
                        if phase == "C":
                            dve.wait_ge(*act_did.at(("esink", g)))
                            link(V.tensor_tensor(rsum[:, x:x + per], rsum[:, x:x + per],
                                                 esink[:, g * 8:g * 8 + 8], ALU.add))
                        link(V.reciprocal(rinv[:, x:x + per], rsum[:, x:x + per]))
                        O = bank.of(("O", phase, g))[:, 0:per * HD].rearrange("p (h e) -> p h e", h=per)
                        rb = rinv[:, x:x + per].unsqueeze(2).to_broadcast([P, per, HD])
                        if phase == "B":
                            V.tensor_tensor(btok[:, :, g * HD:(g + 1) * HD], O, rb, ALU.mult)\
                                .then_inc(*dve_did.up(("B", "head", g)))
                            bank.freed(("O", "B", g), dve_did, ("B", "head", g))
                        else:
                            dst = ootile if phase == "C" else eotile
                            if g:
                                dve.wait_ge(*pe_did.at((phase, "oT", g - 1)))
                            V.tensor_tensor(dst.rearrange("p (h e) -> p h e", h=8), O, rb, ALU.mult)\
                                .then_inc(*dve_did.up((phase, "o", g)))
                            bank.freed(("O", phase, g), dve_did, (phase, "o", g))
                    if phase != "B" and i >= 12 and (i - 12) % 8 == 0:
                        gated(phase, (i - 12) // 8)
                    if phase != "B" and i >= 14 and (i - 14) % 8 == 0:
                        y_low(phase, (i - 14) // 8)
                    if events and i in events:
                        events[i]()

            gb = lambda i: (lambda: gates("egb", i, esg[:, 4 + i, :]))
            def key_rope():
                dve.wait_ge(*unit_done.at(UNIT[("egb", 3)]))
                dve.wait_ge(*dve_did.at("ekr"))
                for slot in range(2):
                    link(V.tensor_copy(KF[64:96, slot, :], ekr[64:96, :]))

            def head_rope(h, half):
                x, t = QF[64:96, h % 2, :], etmp[64:96, 2, :]
                if half == 0:
                    dve.wait_ge(*act_did.at(("QF", h)))
                    link(V.stream_shuffle(t, x, [(j + 16) % 32 for j in range(32)]))
                    link(V.tensor_tensor(t, t, sinT[64:96, :], ALU.mult))
                else:
                    link(V.tensor_tensor(x, x, cosT[64:96, :], ALU.mult))
                    V.tensor_tensor(x, x, t, ALU.add).then_inc(*dve_did.up(("QF", h)))
                    dve.wait_ge(*dve_did.at(("QF", h)))

            attention("A", {6: gb(0), 14: gb(1), 22: gb(2), 30: gb(3), VB_AT + TT: key_rope,
                            VB_AT + TT + 2: lambda: (head_rope(0, 0), head_rope(0, 1))})
            attention("B", {4 * h - 3 + half: (lambda h=h, half=half: head_rope(h, half))
                            for h in range(1, HEADS) for half in range(2)})
            dve.wait_ge(*dve_did.at(("B", "head", HEADS - 1)))
            for g in range(TT):
                found[("dve_did", ("B", "o", g))] = dve_did.n
            for g in range(TT + 1):
                if g < TT:
                    gated("B", g)
                if g >= 1:
                    y_low("B", g - 1)
            for k in range(DC):
                found[("dve_did", ("ey", k))] = dve_did.n

            def residual(name, i, layer, key):
                dve.wait_ge(*unit_done.at(UNIT[(name, i)]))
                V.scalar_tensor_tensor(xT[:, i, :], bank.of((name, i))[:, :], modc[:, layer, 2 * DC + i:2 * DC + i + 1],
                                       xT[:, i, :], ALU.mult, ALU.add).then_inc(*dve_did.up((key, i)))
                bank.freed((name, i), dve_did, (key, i))

            for i in range(DC):
                residual("eout", i, 0, "x3")
            norm("o", lambda c: gn[:, 1, c:c + 1], shift=lambda c: modc[:, 1, c:c + 1])
            link(V.tensor_scalar(nsink[:, :], col("sink", 0, C_HEADS), -1.0, None, ALU.mult))
            for i in range(DC - 1):
                gates("og", i, osg[:, i, :])
            attention("C", {5: lambda: gates("og", DC - 1, osg[:, DC - 1, :])})
            for k in range(DC):
                found[("dve_did", ("oy", k))] = dve_did.n
            for i in range(DC):
                residual("oout", i, 1, "x4")
            norm_in_place("z", lambda c: col("fn", c), "res")
    return found


def kernel(**inputs):
    import concourse.bacc as bacc
    from concourse.bass_utils import run_bass_kernel_spmd

    a = {k: np.asarray(v) for k, v in inputs.items()}
    zeros = np.zeros

    def cat(*blocks):
        return np.concatenate(blocks, axis=1)

    w_in = a["w_in"][0]
    at = np.cumsum([0, 512, 128, 128, 128, 128, 128, 128, 24, 1024, 2048])
    col = lambda w, start, n=P: w[:, start:start + n]
    pair = lambda w, start, h0, h1: cat(col(w, start + h0 * HD, HD), col(w, start + h1 * HD, HD))
    up, down = a["ffn_w_up"][0], a["ffn_w_down"][0]
    even, odd = a["even_w_in_2"][0], a["odd_w_in_2"][0]
    eo = np.cumsum([0, 512, 128, 128, 512, 256, 128, 32, 512])
    parts = {
        "conv": lambda i: col(w_in, at[8] + (i % 2) * CONV_CH + i // 2 * P),
        "tok": lambda i: col(w_in, at[4]) if i == 0 else col(w_in, at[6]) if i == 1
        else cat(col(w_in, at[7], 24), zeros((D, P - 24), np.float32)),
        "q": lambda i: pair(w_in, 0, i, i + 4),
        "k": lambda i: col(w_in, (at[3], at[5], at[1], at[2])[i]),
        "ga": lambda i: col(w_in, at[9] + i * P),
        "gb": lambda i: col(w_in, at[9] + D + i * P),
        "y": lambda i: np.concatenate([col(a["w_attn_br"][0], i * P), col(a["w_conv_br"][0], i * P)]),
        "wout": lambda i: col(a["w_out"][0], i * P),
        "up": lambda i: col(up, order_up(i) * P),
        "ecq": lambda i: col(even, eo[4] + i * P),
        "eckv": lambda i: col(even, eo[5]),
        "ekr": lambda i: cat(zeros((D, 64), np.float32), col(even, eo[6], 32), zeros((D, 32), np.float32)),
        "eq": lambda i: pair(even, 0, i, i + 4),
        "ek": lambda i: col(even, eo[1]),
        "ev": lambda i: col(even, eo[2]),
        "ega": lambda i: col(even, eo[3] + i * P),
        "egb": lambda i: col(even, eo[7] + i * P),
        "eout": lambda i: col(a["even_w_out_2"][0], i * P),
        "oq": lambda i: pair(odd, 0, i // 4 * 8 + i % 4, i // 4 * 8 + i % 4 + 4),
        "ok": lambda i: col(odd, 1024 + i * P),
        "ov": lambda i: col(odd, 1280 + i * P),
        "og": lambda i: col(odd, 1536 + i * P),
        "oout": lambda i: col(a["odd_w_out_2"][0], i * P),
    }
    w = np.empty((NU, P, D), np.float32)
    for n, (name, i) in enumerate(UNITS):
        if name == "down":
            w[n] = down[i * P:(i + 1) * P]
        else:
            w[n] = parts[name](i).reshape(DC, P, P).transpose(1, 0, 2).reshape(P, D)

    vec = lambda v: v.reshape(-1, P).T
    twice = lambda v: np.concatenate([v, v], axis=0)
    c = np.zeros((P, NCOLS), np.float32)
    for name, value in {
        "n1g": vec(a["norm1_g"][0]), "n2g": vec(a["norm2_g"][0]), "fg": vec(a["final_g"]),
        "dwb": vec(a["conv_dw_b"][0]), "lng": vec(a["conv_ln_g"][0]), "lnb": vec(a["conv_ln_b"][0]),
        "dww": a["conv_dw_w"][0].T.reshape(CC, P, TAPS).transpose(1, 0, 2).reshape(P, -1),
        "ffw": a["ffn_dw_w"][0].T.reshape(2 * FC, P, 3).transpose(1, 0, 2).reshape(P, -1),
        "ffb": vec(a["ffn_dw_b"][0]),
        "pek": twice(a["cmp_pe_k"][0].T), "pev": twice(a["cmp_pe_v"][0].T),
        "rowvalid": (np.arange(P) >= CMP_BLOCK - 1).astype(np.float32)[:, None],
        "nw": cat(vec(a["norm_w_2"][0]), vec(a["norm_w_2"][1])),
        "adab": cat(vec(a["ada_b_2"][0]), vec(a["ada_b_2"][1])),
        "qn": twice(a["a_q_norm_2"][0][:, None]), "kn": twice(a["a_k_norm_2"][0][:, None]),
        "cqg": vec(a["b_q_lora_norm_2"][0]), "ckvg": vec(a["b_kv_lora_norm_2"][0]),
        "fn": vec(a["final_norm_2"]),
        "sink": np.broadcast_to(a["c_sink_2"][0][None, :], (P, C_HEADS)),
    }.items():
        s, n = COLS[name]
        c[:, s:s + n] = value

    p = np.arange(P)[:, None]
    j = np.arange(T)[None, :] - (T - P)
    dist = np.where(j <= p, j - p, NEG).astype(np.float32)
    t = (np.arange(TT)[None, :, None] * P + p[:, :, None])
    end = np.arange(NCP)[None, None, :] * CMP_STRIDE + CMP_BLOCK - 1
    distc = np.where((t >= end) & (np.arange(NCP) < NCMP)[None, None, :], end - t, NEG)\
        .astype(np.float32).reshape(P, TT * NCP)
    w1 = np.stack([twice(a[k][0].reshape(CMP_BLOCK, HD, P).transpose(1, 0, 2).reshape(HD, -1))
                   for k in ("cmp_k_w1", "cmp_v_w1")])
    w2 = np.stack([a["cmp_k_w2"][0], a["cmp_v_w2"][0]])
    ada = a["ada_w_2"].reshape(2, DC, P, 3 * DC, P).transpose(0, 3, 4, 1, 2).reshape(6 * DC, P, D)
    j = np.arange(3 * P)[None, :] - P
    distC = np.where(np.abs(j - p) <= WIN, -np.abs(j - p), NEG).astype(np.float32)
    half = np.arange(P)[:, None] % 32
    inv = (np.float32(ROPE_THETA) ** (-(2 * (half % 16)).astype(np.float32) / np.float32(32))).astype(np.float32)
    tok = np.arange(T)[None, :]
    axial = np.where(np.arange(P)[:, None] % 64 < 32, tok // 64, tok % 64).astype(np.float32)
    sign = np.where(half < 16, -1, 1).astype(np.float32)
    angA, angT = axial * inv, tok.astype(np.float32) * inv
    cosA, sinA = np.cos(angA), np.sin(angA) * sign
    cosT, sinT = np.cos(angT), np.sin(angT) * sign
    arrays = {
        "xT": np.ascontiguousarray(a["x"][0].T).reshape(DC, P, T), "w": w, "cols": c, "dist": dist,
        "distc": distc, "w1": w1, "w2": w2, "ada": ada, "distC": distC,
        "c": np.broadcast_to(a["c_2"][0][None, :], (P, D)), "cosA": cosA, "sinA": sinA, "cosT": cosT, "sinT": sinT,
        "uq": a["b_w_uq_2"][0].reshape(2, P, HEADS * 96).transpose(1, 0, 2).reshape(P, -1),
        "uk": a["b_w_uk_2"][0].reshape(P, -1), "uv": a["b_w_uv_2"][0].reshape(P, -1),
    }
    arrays = {k: np.ascontiguousarray(v) for k, v in arrays.items()}

    def build(known):
        nc = bacc.Bacc("TRN2", target_bir_lowering=False, num_devices=1)
        d = {k: nc.dram_tensor(f"in_{k}", v.shape, F32, kind="ExternalInput").ap() for k, v in arrays.items()}
        out = nc.dram_tensor("out_t", (DC, P, T), F32, kind="ExternalOutput").ap()
        return nc, program(nc, d, out, known)

    _, known = build({})
    nc, again = build(known)
    assert again == known
    r = run_bass_kernel_spmd(nc, [{f"in_{k}": v for k, v in arrays.items()}], core_ids=[0])
    return np.ascontiguousarray(r.results[0]["out_t"].reshape(D, T).T)[None]
```
